# Optimizing a Trainium2 kernel written in Bass

```python
import jax, jax.numpy as jnp
from jax import lax
import numpy as np
import math

D_MODEL = 1024
BATCH = 1
SEQ = 512
DEPTH = 2

MIX_WIDTH = D_MODEL
POOL_WIDTH = MIX_WIDTH // 4
POOL_WINDOWS = (2, 4, 8, 16)
POOL_GROUPS = len(POOL_WINDOWS)
POOL_GROUP_DIM = POOL_WIDTH // POOL_GROUPS
HEAD_DIM = 64
ATTN_WIDTH = MIX_WIDTH - POOL_WIDTH
N_HEADS = ATTN_WIDTH // HEAD_DIM
DILATED_PATTERNS = ((128, 1), (512, 4), (2048, 16))
ROPE_THETA = 500000.0
ROPE_DIM = HEAD_DIM // 4
D_FF = 2816
IN_PROJ_WIDTH = POOL_WIDTH + 3 * ATTN_WIDTH
NORM_EPS = 1e-6
MASK_VALUE = -1e30


def rmsnorm(x, g):
    xf = x.astype(jnp.float32)
    y = xf * lax.rsqrt(jnp.mean(xf * xf, axis=-1, keepdims=True) + NORM_EPS)
    return (y * g.astype(jnp.float32)).astype(x.dtype)

def swiglu(h, w_gate, w_up, w_down):
    return (jax.nn.silu(h @ w_gate) * (h @ w_up)) @ w_down

def rope_tables(positions):
    inv_freq = ROPE_THETA ** (-jnp.arange(0, ROPE_DIM, 2, dtype=jnp.float32) / ROPE_DIM)
    ang = positions.astype(jnp.float32)[..., None] * inv_freq
    return jnp.cos(ang)[:, :, None, :], jnp.sin(ang)[:, :, None, :]

def apply_partial_rope(t, cos, sin):
    tf = t.astype(jnp.float32)
    half = ROPE_DIM // 2
    t1, t2, rest = tf[..., :half], tf[..., half:ROPE_DIM], tf[..., ROPE_DIM:]
    rot = jnp.concatenate([t1 * cos - t2 * sin, t2 * cos + t1 * sin, rest], axis=-1)
    return rot.astype(t.dtype)

def multiscale_pool(v, pool_w, pool_scale):
    B, S, _ = v.shape
    vf = v.astype(jnp.float32).reshape(B, S, POOL_GROUPS, POOL_GROUP_DIM)
    cs = jnp.pad(lax.cumsum(vf, axis=1), ((0, 0), (1, 0), (0, 0), (0, 0)))
    pos = jnp.arange(S)
    means = []
    for g, w in enumerate(POOL_WINDOWS):
        lo = jnp.maximum(pos - w // 2, 0)
        hi = jnp.minimum(pos + w - 1 - w // 2, S - 1)
        cnt = (hi - lo + 1).astype(jnp.float32)
        means.append((cs[:, hi + 1, g] - cs[:, lo, g]) / cnt[None, :, None])
    pooled = jnp.stack(means, axis=2)
    diff = (pooled - vf).astype(v.dtype)
    y = jnp.einsum('bsgc,gcd->bsgd', diff, pool_w).reshape(B, S, POOL_WIDTH)
    return y * pool_scale

def dilated_branch(q, k, v, window, dilation):
    B, S, H, Dh = q.shape
    half = window // (2 * dilation)
    blk = half
    L = S // dilation
    nb = -(-L // blk)
    Lp = nb * blk

    def to_compressed(t):
        t = t.astype(jnp.float32).reshape(B, L, dilation, H, Dh)
        return jnp.pad(t, ((0, 0), (0, Lp - L), (0, 0), (0, 0), (0, 0)))

    def band(t):
        tp = jnp.pad(t, ((0, 0), (blk, blk), (0, 0), (0, 0), (0, 0)))
        tp = tp.reshape(B, nb + 2, blk, dilation, H, Dh)
        return jnp.concatenate([tp[:, :-2], tp[:, 1:-1], tp[:, 2:]], axis=2)

    qb = to_compressed(q).reshape(B, nb, blk, dilation, H, Dh)
    kb = band(to_compressed(k))
    vb = band(to_compressed(v))

    t_idx = jnp.arange(nb)[:, None] * blk + jnp.arange(blk)[None, :]
    j_idx = jnp.arange(nb)[:, None] * blk - blk + jnp.arange(3 * blk)[None, :]
    jj = j_idx[:, None, :]
    valid = (jnp.abs(jj - t_idx[:, :, None]) <= half) & (jj >= 0) & (jj < L)

    scale = 1.0 / np.sqrt(Dh)
    s = jnp.einsum('bnqrhd,bnkrhd->bnrhqk', qb, kb) * scale
    s = jnp.where(valid[None, :, None, None], s, MASK_VALUE)
    m = jnp.max(s, axis=-1, keepdims=True)
    p = jnp.exp(s - m)
    denom = jnp.sum(p, axis=-1)
    num = jnp.einsum('bnrhqk,bnkrhd->bnqrhd', p, vb)

    num = num.reshape(B, Lp, dilation, H, Dh)[:, :L].reshape(B, S, H, Dh)

    def stat_back(t):
        t = jnp.transpose(t, (0, 1, 4, 2, 3)).reshape(B, Lp, dilation, H)
        return t[:, :L].reshape(B, S, H)

    return num, stat_back(m[..., 0]), stat_back(denom)

def dilated_mixture_attention(q, k, v):
    branches = [dilated_branch(q, k, v, w, d) for (w, d) in DILATED_PATTERNS]
    m_all = jnp.stack([b[1] for b in branches], axis=0)
    wts = jnp.exp(m_all - jnp.max(m_all, axis=0, keepdims=True))
    num = sum(wts[i][..., None] * branches[i][0] for i in range(len(branches)))
    den = sum(wts[i] * branches[i][2] for i in range(len(branches)))
    return (num / den[..., None]).astype(q.dtype)

def first_inputs(seed: int = 0) -> dict:
    key = jax.random.key(seed)
    ks = jax.random.split(key, 20)
    f32 = jnp.float32

    def normal(k, shape, fan_in):
        return jax.random.normal(k, shape, f32) * (fan_in ** -0.5)

    def gain(k, shape):
        return jnp.ones(shape, f32) + 0.02 * jax.random.normal(k, shape, f32)

    x = jax.random.normal(ks[0], (BATCH, SEQ, D_MODEL), f32)
    start = jax.random.randint(ks[1], (BATCH, 1), 0, 4096, dtype=jnp.int32)
    positions = start + jnp.arange(SEQ, dtype=jnp.int32)[None, :]
    return {
        "x": x,
        "positions": positions,
        "ffn1_norm": gain(ks[2], (DEPTH, D_MODEL)),
        "ffn1_w_gate": normal(ks[3], (DEPTH, D_MODEL, D_FF), D_MODEL),
        "ffn1_w_up": normal(ks[4], (DEPTH, D_MODEL, D_FF), D_MODEL),
        "ffn1_w_down": normal(ks[5], (DEPTH, D_FF, D_MODEL), D_FF),
        "mix_norm": gain(ks[6], (DEPTH, D_MODEL)),
        "w_in": normal(ks[7], (DEPTH, D_MODEL, IN_PROJ_WIDTH), D_MODEL),
        "pool_w": normal(ks[8], (DEPTH, POOL_GROUPS, POOL_GROUP_DIM, POOL_GROUP_DIM), POOL_GROUP_DIM),
        "pool_scale": gain(ks[9], (DEPTH, POOL_WIDTH)),
        "w_out": normal(ks[10], (DEPTH, MIX_WIDTH, D_MODEL), MIX_WIDTH),
        "ffn2_norm": gain(ks[11], (DEPTH, D_MODEL)),
        "ffn2_w_gate": normal(ks[12], (DEPTH, D_MODEL, D_FF), D_MODEL),
        "ffn2_w_up": normal(ks[13], (DEPTH, D_MODEL, D_FF), D_MODEL),
        "ffn2_w_down": normal(ks[14], (DEPTH, D_FF, D_MODEL), D_FF),
        "final_norm": gain(ks[15], (D_MODEL,)),
    }

def first_block(x, positions, ffn1_norm, ffn1_w_gate, ffn1_w_up, ffn1_w_down, mix_norm, w_in,
              pool_w, pool_scale, w_out, ffn2_norm, ffn2_w_gate, ffn2_w_up, ffn2_w_down, final_norm):
    B, S, _ = x.shape
    cos, sin = rope_tables(positions)
    for l in range(DEPTH):
        x = x + 0.5 * swiglu(rmsnorm(x, ffn1_norm[l]), ffn1_w_gate[l], ffn1_w_up[l], ffn1_w_down[l])

        h = rmsnorm(x, mix_norm[l])
        proj = h @ w_in[l]
        v_pool = proj[..., :POOL_WIDTH]
        q = proj[..., POOL_WIDTH:POOL_WIDTH + ATTN_WIDTH].reshape(B, S, N_HEADS, HEAD_DIM)
        k = proj[..., POOL_WIDTH + ATTN_WIDTH:POOL_WIDTH + 2 * ATTN_WIDTH].reshape(B, S, N_HEADS, HEAD_DIM)
        v = proj[..., POOL_WIDTH + 2 * ATTN_WIDTH:].reshape(B, S, N_HEADS, HEAD_DIM)

        y_pool = multiscale_pool(v_pool, pool_w[l], pool_scale[l])
        q = apply_partial_rope(q, cos, sin)
        k = apply_partial_rope(k, cos, sin)
        y_attn = dilated_mixture_attention(q, k, v).reshape(B, S, ATTN_WIDTH)

        mixed = jnp.concatenate([y_pool.astype(x.dtype), y_attn.astype(x.dtype)], axis=-1)
        x = x + mixed @ w_out[l]

        x = x + 0.5 * swiglu(rmsnorm(x, ffn2_norm[l]), ffn2_w_gate[l], ffn2_w_up[l], ffn2_w_down[l])
    return rmsnorm(x, final_norm)


DEPTH_2 = 1

D_MIX = D_MODEL
D_A = D_MIX // 2
D_B = D_MIX - D_A
H_A = D_A // HEAD_DIM
H_B = D_B // HEAD_DIM
N_KV = 2
GQA = H_B // N_KV
D_KV = N_KV * HEAD_DIM
CHUNK = 128
CMP_BLOCK = 32
CMP_STRIDE = 16
CMP_HIDDEN = 256
SEL_BLOCK = 64
N_SELECT = 16
WINDOW = 512
Q_BLOCK = 128
N_GATES = 3
D_IN = 2 * D_A + D_B + 6 * D_KV + N_GATES * H_B
D_FF_2 = int(math.ceil(8 * D_MODEL / 3 / 256)) * 256
EPS = 1e-6
NEG = -1e30
FORCE = 1e4


def rmsnorm_2(x, w):
    xf = x.astype(jnp.float32)
    y = xf * lax.rsqrt(jnp.mean(xf * xf, axis=-1, keepdims=True) + EPS)
    return (y * w.astype(jnp.float32)).astype(x.dtype)

def masked_softmax(s, mask):
    p = jax.nn.softmax(jnp.where(mask, s.astype(jnp.float32), NEG), axis=-1)
    return jnp.where(mask, p, 0.0)

def split_offsets():
    sizes = [D_A, D_A, D_B, D_KV, D_KV, D_KV, D_KV, D_KV, D_KV, N_GATES * H_B]
    return [int(o) for o in np.cumsum(sizes)[:-1]]

def gmlp_group(u, v, norm_w, ws, bs):
    B, S, _ = u.shape
    nc = S // CHUNK
    u = jax.nn.gelu(u).reshape(B, nc, CHUNK, H_A, HEAD_DIM)
    v = rmsnorm_2(jax.nn.gelu(v), norm_w).reshape(B, nc, CHUNK, H_A, HEAD_DIM)
    causal = jnp.tril(jnp.ones((CHUNK, CHUNK), dtype=bool))
    w = jnp.where(causal[None], ws, 0).astype(v.dtype)
    sv = jnp.einsum('hts,bcshd->bcthd', w, v) + bs.T.astype(v.dtype)[None, None, :, :, None]
    return (u * sv).reshape(B, S, D_A)

def compress(kv, pos, w1, w2):
    B, S = kv.shape[0], kv.shape[1]
    n_cmp = (S - CMP_BLOCK) // CMP_STRIDE + 1
    idx = jnp.arange(n_cmp)[:, None] * CMP_STRIDE + jnp.arange(CMP_BLOCK)[None, :]
    blk = kv[:, idx] + pos[None, None, :, None, :]
    blk = blk.transpose(0, 1, 3, 2, 4).reshape(B, n_cmp, N_KV, CMP_BLOCK * HEAD_DIM)
    return jax.nn.gelu(blk @ w1) @ w2

def nsa_group(q, k_c, v_c, k_s, v_s, k_w, v_w, g_raw,
              cmp_pos_k, cmp_pos_v, cmp_k_w1, cmp_k_w2, cmp_v_w1, cmp_v_w2, gate_b):
    B, S = q.shape[0], q.shape[1]
    q = (q * (HEAD_DIM ** -0.5)).reshape(B, S, N_KV, GQA, HEAD_DIM)
    kv_shape = (B, S, N_KV, HEAD_DIM)
    k_c, v_c, k_s, v_s, k_w, v_w = [a.reshape(kv_shape) for a in (k_c, v_c, k_s, v_s, k_w, v_w)]
    t = jnp.arange(S)
    n_qb = S // Q_BLOCK

    kc = compress(k_c, cmp_pos_k, cmp_k_w1, cmp_k_w2)
    vc = compress(v_c, cmp_pos_v, cmp_v_w1, cmp_v_w2)
    n_cmp = kc.shape[1]
    cmp_start = jnp.arange(n_cmp) * CMP_STRIDE
    cmp_mask = (cmp_start + CMP_BLOCK - 1)[None, :] <= t[:, None]
    s_cmp = jnp.einsum('bskgd,bnkd->bkgsn', q, kc)
    p_cmp = masked_softmax(s_cmp, cmp_mask)
    o_cmp = jnp.einsum('bkgsn,bnkd->bskgd', p_cmp.astype(vc.dtype), vc)

    n_blk = S // SEL_BLOCK
    n_sel = min(N_SELECT, n_blk)
    blk_start = jnp.arange(n_blk) * SEL_BLOCK
    overlap = ((cmp_start[:, None] < blk_start[None, :] + SEL_BLOCK)
               & (cmp_start[:, None] + CMP_BLOCK > blk_start[None, :])).astype(jnp.float32)
    imp = jnp.einsum('bkgsn,nj->bksj', p_cmp, overlap)
    cur = t // SEL_BLOCK
    j = jnp.arange(n_blk)
    valid = j[None, :] <= cur[:, None]
    forced = (j[None, :] == 0) | (j[None, :] == cur[:, None]) | (j[None, :] == cur[:, None] - 1)
    score = jnp.where(forced, FORCE, jnp.where(valid, imp, -FORCE))
    _, sel = lax.top_k(score, n_sel)
    sel = sel.transpose(0, 2, 1, 3)

    kb = k_s.reshape(B, n_blk, SEL_BLOCK, N_KV, HEAD_DIM).transpose(0, 3, 1, 2, 4)
    vb = v_s.reshape(B, n_blk, SEL_BLOCK, N_KV, HEAD_DIM).transpose(0, 3, 1, 2, 4)
    b_ix = jnp.arange(B)[:, None, None, None]
    h_ix = jnp.arange(N_KV)[None, None, :, None]

    def sel_block(args):
        qc, ic, tc = args
        kg = kb[b_ix, h_ix, ic]
        vg = vb[b_ix, h_ix, ic]
        pos = ic[..., None] * SEL_BLOCK + jnp.arange(SEL_BLOCK)
        mask = (pos <= tc[None, :, None, None, None]).reshape(B, Q_BLOCK, N_KV, 1, n_sel * SEL_BLOCK)
        s = jnp.einsum('bqkgd,bqknrd->bqkgnr', qc, kg).reshape(B, Q_BLOCK, N_KV, GQA, n_sel * SEL_BLOCK)
        p = masked_softmax(s, mask)
        vg = vg.reshape(B, Q_BLOCK, N_KV, n_sel * SEL_BLOCK, HEAD_DIM)
        return jnp.einsum('bqkgm,bqkmd->bqkgd', p.astype(vg.dtype), vg)

    qs = q.reshape(B, n_qb, Q_BLOCK, N_KV, GQA, HEAD_DIM).transpose(1, 0, 2, 3, 4, 5)
    sels = sel.reshape(B, n_qb, Q_BLOCK, N_KV, n_sel).transpose(1, 0, 2, 3, 4)
    ts = t.reshape(n_qb, Q_BLOCK)
    o_slc = lax.map(sel_block, (qs, sels, ts))
    o_slc = o_slc.transpose(1, 0, 2, 3, 4, 5).reshape(B, S, N_KV, GQA, HEAD_DIM)

    span = WINDOW + Q_BLOCK
    pad = ((0, 0), (WINDOW, 0), (0, 0), (0, 0))
    band = jnp.arange(n_qb)[:, None] * Q_BLOCK + jnp.arange(span)[None, :]
    kw = jnp.pad(k_w, pad)[:, band]
    vw = jnp.pad(v_w, pad)[:, band]
    kpos = band - WINDOW
    diff = ts[:, :, None] - kpos[:, None, :]
    win_mask = (diff >= 0) & (diff < WINDOW) & (kpos[:, None, :] >= 0)
    qw = q.reshape(B, n_qb, Q_BLOCK, N_KV, GQA, HEAD_DIM)
    s_win = jnp.einsum('bcqkgd,bcmkd->bckgqm', qw, kw)
    p_win = masked_softmax(s_win, win_mask[None, :, None, None])
    o_win = jnp.einsum('bckgqm,bcmkd->bcqkgd', p_win.astype(vw.dtype), vw).reshape(B, S, N_KV, GQA, HEAD_DIM)

    g = jax.nn.sigmoid(g_raw + gate_b).reshape(B, S, N_GATES, N_KV, GQA, 1)
    o = g[:, :, 0] * o_cmp + g[:, :, 1] * o_slc + g[:, :, 2] * o_win
    return o.reshape(B, S, D_B)

def second_inputs(seed: int = 0) -> dict:
    key = jax.random.key(seed)
    ks = iter(jax.random.split(key, 32))

    def nrm(shape, scale):
        return jax.random.normal(next(ks), shape, jnp.float32) * scale

    def gain(shape):
        return 1.0 + nrm(shape, 0.01)

    L = DEPTH_2
    return {
        "x": nrm((BATCH, SEQ, D_MODEL), 1.0),
        "norm_mix_w": gain((L, D_MODEL)),
        "w_in": nrm((L, D_MODEL, D_IN), D_MODEL ** -0.5),
        "gmlp_norm_w": gain((L, D_A)),
        "gmlp_ws": nrm((L, H_A, CHUNK, CHUNK), 0.5 * CHUNK ** -0.5),
        "gmlp_bs": 1.0 + nrm((L, H_A, CHUNK), 0.01),
        "cmp_pos_k": nrm((L, CMP_BLOCK, HEAD_DIM), 0.1),
        "cmp_pos_v": nrm((L, CMP_BLOCK, HEAD_DIM), 0.1),
        "cmp_k_w1": nrm((L, CMP_BLOCK * HEAD_DIM, CMP_HIDDEN), (CMP_BLOCK * HEAD_DIM) ** -0.5),
        "cmp_k_w2": nrm((L, CMP_HIDDEN, HEAD_DIM), CMP_HIDDEN ** -0.5),
        "cmp_v_w1": nrm((L, CMP_BLOCK * HEAD_DIM, CMP_HIDDEN), (CMP_BLOCK * HEAD_DIM) ** -0.5),
        "cmp_v_w2": nrm((L, CMP_HIDDEN, HEAD_DIM), CMP_HIDDEN ** -0.5),
        "gate_b": nrm((L, N_GATES * H_B), 0.01),
        "out_norm_a_w": gain((L, D_A)),
        "out_norm_b_w": gain((L, D_B)),
        "w_o": nrm((L, D_MIX, D_MODEL), D_MIX ** -0.5),
        "norm_ffn_w": gain((L, D_MODEL)),
        "w_gate": nrm((L, D_MODEL, D_FF_2), D_MODEL ** -0.5),
        "w_up": nrm((L, D_MODEL, D_FF_2), D_MODEL ** -0.5),
        "w_down": nrm((L, D_FF_2, D_MODEL), D_FF_2 ** -0.5),
        "final_norm_w": gain((D_MODEL,)),
    }

def second_block(x, norm_mix_w, w_in, gmlp_norm_w, gmlp_ws, gmlp_bs,
              cmp_pos_k, cmp_pos_v, cmp_k_w1, cmp_k_w2, cmp_v_w1, cmp_v_w2,
              gate_b, out_norm_a_w, out_norm_b_w, w_o, norm_ffn_w,
              w_gate, w_up, w_down, final_norm_w):
    offsets = split_offsets()
    for l in range(DEPTH_2):
        h = rmsnorm_2(x, norm_mix_w[l])
        z = h @ w_in[l]
        u, v, q, k_c, v_c, k_s, v_s, k_w, v_w, g_raw = jnp.split(z, offsets, axis=-1)
        a = gmlp_group(u, v, gmlp_norm_w[l], gmlp_ws[l], gmlp_bs[l])
        b = nsa_group(q, k_c, v_c, k_s, v_s, k_w, v_w, g_raw,
                      cmp_pos_k[l], cmp_pos_v[l], cmp_k_w1[l], cmp_k_w2[l],
                      cmp_v_w1[l], cmp_v_w2[l], gate_b[l])
        mix = jnp.concatenate([rmsnorm_2(a, out_norm_a_w[l]), rmsnorm_2(b, out_norm_b_w[l])], axis=-1)
        x = x + mix @ w_o[l]
        h = rmsnorm_2(x, norm_ffn_w[l])
        x = x + (jax.nn.silu(h @ w_gate[l]) * (h @ w_up[l])) @ w_down[l]
    return rmsnorm_2(x, final_norm_w)


_first_inputs = second_inputs


def second_inputs(seed=0):
    import zlib

    import numpy as np

    out = dict(_first_inputs(seed))
    spreads = {}
    factors = {'norm_mix_w': 6.381,
     'gmlp_norm_w': 64.0,
     'gmlp_bs': 48.476,
     'cmp_pos_k': 5.802,
     'gate_b': 49.652,
     'out_norm_a_w': 46.307,
     'out_norm_b_w': 48.521,
     'norm_ffn_w': 33.148,
     'final_norm_w': 34.207,
     'cmp_pos_v': 7.836}
    for name, (base, spread) in spreads.items():
        noise = np.random.default_rng([zlib.crc32(name.encode()), seed]).standard_normal(out[name].shape)
        drawn = base * np.exp(spread * noise) if base else spread * noise
        out[name] = __import__('jax').numpy.asarray(drawn.astype(out[name].dtype))
    for name, factor in factors.items():
        out[name] = (out[name] * factor).astype(out[name].dtype)
    return out


_narrow_inputs = second_inputs


def second_inputs(seed=0):

    out = dict(_narrow_inputs(seed))
    wider = {'gmlp_norm_w': 12.0,
     'gmlp_bs': 7.16,
     'out_norm_a_w': 6.61,
     'out_norm_b_w': 6.62,
     'norm_ffn_w': 4.61,
     'final_norm_w': 6.64}
    for name, times in wider.items():
        mean = out[name].mean()
        out[name] = (mean + times * (out[name] - mean)).astype(out[name].dtype)
    return out


def setup_inputs(seed=0):
    out = dict(first_inputs(seed))
    for name, value in second_inputs(seed + 1).items():
        if name != "x":
            out[name + "_2"] = value
    return out


def reference(
    x, positions, ffn1_norm, ffn1_w_gate, ffn1_w_up, ffn1_w_down, mix_norm, w_in, pool_w,
    pool_scale, w_out, ffn2_norm, ffn2_w_gate, ffn2_w_up, ffn2_w_down, final_norm, norm_mix_w_2,
    w_in_2, gmlp_norm_w_2, gmlp_ws_2, gmlp_bs_2, cmp_pos_k_2, cmp_pos_v_2, cmp_k_w1_2,
    cmp_k_w2_2, cmp_v_w1_2, cmp_v_w2_2, gate_b_2, out_norm_a_w_2, out_norm_b_w_2, w_o_2,
    norm_ffn_w_2, w_gate_2, w_up_2, w_down_2, final_norm_w_2,
):
    x = first_block(
        x, positions, ffn1_norm, ffn1_w_gate, ffn1_w_up, ffn1_w_down, mix_norm, w_in, pool_w,
        pool_scale, w_out, ffn2_norm, ffn2_w_gate, ffn2_w_up, ffn2_w_down, final_norm,
    )
    return second_block(
        x, norm_mix_w_2, w_in_2, gmlp_norm_w_2, gmlp_ws_2, gmlp_bs_2, cmp_pos_k_2, cmp_pos_v_2,
        cmp_k_w1_2, cmp_k_w2_2, cmp_v_w1_2, cmp_v_w2_2, gate_b_2, out_norm_a_w_2,
        out_norm_b_w_2, w_o_2, norm_ffn_w_2, w_gate_2, w_up_2, w_down_2, final_norm_w_2,
    )


_drawn_inputs = setup_inputs


def setup_inputs(seed=0):
    import zlib

    import numpy as np

    out = dict(_drawn_inputs(seed))
    spreads = {}
    factors = {}
    for name, (base, spread) in spreads.items():
        noise = np.random.default_rng([zlib.crc32(name.encode()), seed]).standard_normal(out[name].shape)
        drawn = base * np.exp(spread * noise) if base else spread * noise
        out[name] = __import__('jax').numpy.asarray(drawn.astype(out[name].dtype))
    for name, factor in factors.items():
        out[name] = (out[name] * factor).astype(out[name].dtype)
    return out
```

```python
from contextlib import ExitStack

import numpy as np

import concourse.bass as bass
from concourse import mybir

F32 = mybir.dt.float32
F32R = mybir.dt.float32r
I32 = mybir.dt.int32
ALU = mybir.AluOpType
ACT = mybir.ActivationFunctionType

P = 128
T = 512
D = 1024
KT = D // P
DEPTH = 2
DFF = 2816
FT = DFF // P
NQ = T // P
HD = 64
EPS = 1e-6
SCALE = HD ** -0.5
NEG = -1e30

POOL_W = 256
PAIRS = 6
WINDOWS = (2, 4, 8, 16)
PAD = 8
NKV = 2
NCMP = (T - 32) // 16 + 1
CH = 256
NGATE = 24
SLABS = 16

U_FFN = 3 * FT
U_PROJ = 2 + 3 * PAIRS
U_OUT = KT
U_LAYER = 2 * U_FFN + U_PROJ + U_OUT
U_PROJ2 = 18
U_BLOCK2 = DEPTH * U_LAYER
U_ALL = U_BLOCK2 + U_PROJ2 + U_OUT + U_FFN
ORDER2 = [4, 5, 6, 7, 12, 13, 14, 16, 15, 17, 8, 9, 10, 11, 0, 1, 2, 3]


def shape_constants():
    p = np.arange(P)[:, None]
    c = np.arange(T + 384)[None, :]
    d = c - 384 - p
    count = (np.abs(d) <= 64) * 1 + ((d % 4 == 0) & (np.abs(d) <= 256)) + (d % 16 == 0)
    band = np.where(count > 0, np.log(np.maximum(count, 1)) / SCALE, NEG)
    tri = np.where(c[:, :T] - 384 <= p, 0.0, NEG)
    tq = (np.arange(NQ)[None, :, None] * P + np.arange(P)[:, None, None])
    seen = (16 * np.arange(NCMP)[None, None, :] + 31) <= tq
    rot = np.zeros((P, P))
    for h in (0, HD):
        for i in range(8):
            rot[h + i + 8, h + i] = -1.0
            rot[h + i, h + i + 8] = 1.0
    pos = np.arange(T)
    inv = np.zeros((P, 2, T))
    for g, w in enumerate(WINDOWS):
        lo = np.maximum(pos - w // 2, 0)
        hi = np.minimum(pos + w - 1 - w // 2, T - 1)
        inv[64 * (g % 2):64 * (g % 2) + 64, g // 2, :] = 1.0 / (hi - lo + 1)
    dim = np.arange(P) % HD
    freq = np.where(dim < 16, np.float32(500000.0) ** (-(2 * (dim % 8)).astype(np.float32) / np.float32(16)), 0.0)
    cols = np.stack([freq, dim < 16, dim >= 16], 1)
    out = {
        "c_band": band, "c_tri": tri, "c_cmpbias": np.where(seen, 0.0, NEG), "c_cmpseen": seen,
        "c_ident": np.eye(P), "c_ones": np.ones((P, P)), "c_rot": rot, "c_invcount": inv,
        "c_causal": p <= np.arange(P)[None, :], "c_rope": cols,
    }
    return {k: np.ascontiguousarray(v.astype(np.float32)) for k, v in out.items()}


def build(nc, d):
    ctx = ExitStack()
    with ctx:
        def sem(name):
            return ctx.enter_context(nc.semaphore(name))

        def sb(name, shape, dt=F32, at=ctx):
            return at.enter_context(nc.sbuf_tensor(name, shape, dt))

        x = sb("x", [P, KT, T])
        xh = sb("xh", [P, KT, T], F32R)
        xl = sb("xl", [P, KT, T], F32R)
        raw = sb("raw", [P, 2, 2, 8 * P])
        wh = sb("wh", [P, 2, 8, P], F32R)
        wl = sb("wl", [P, 2, 8, P], F32R)
        sq = sb("sq", [P, 2, T])
        rstd = sb("rstd", [P, T])
        ident = sb("ident", [P, P])
        ones = sb("ones", [P, P])
        gains = sb("gains", [P, DEPTH, 3, KT])
        gains2 = sb("gains2", [P, 4, KT])
        gain = sb("gain", [P, 3, KT])

        block1 = ExitStack()
        cos = sb("cos", [P, T], at=block1)
        sin = sb("sin", [P, T], at=block1)
        rot = sb("rot", [P, P], at=block1)
        band = sb("band", [P, T + 384], at=block1)
        invcount = sb("invcount", [P, 2, T], at=block1)
        ropecol = sb("ropecol", [P, 3], at=block1)
        poolw = sb("poolw", [P, DEPTH, 2, HD], at=block1)
        poolscale = sb("poolscale", [P, DEPTH, 2], at=block1)
        poolw_now = sb("poolw_now", [P, 2, HD], at=block1)
        poolscale_now = sb("poolscale_now", [P, 2], at=block1)

        mix1 = ExitStack()
        posi = sb("posi", [P, T], I32, at=mix1)
        cosr = sb("cosr", [P, T], at=mix1)
        sinr = sb("sinr", [P, T], at=mix1)
        mh1 = sb("mh1", [P, KT, T], F32R, at=mix1)
        ml1 = sb("ml1", [P, KT, T], F32R, at=mix1)
        qkraw = sb("qkraw", [P, 2, T], at=mix1)
        vraw = sb("vraw", [P, T], at=mix1)
        qk = sb("qk", [P, 2, 2, T], at=mix1)
        vtok = sb("vtok", [P, 2, NQ, P], at=mix1)
        sc = sb("sc", [P, 2, T], at=mix1)
        pt = sb("pt", [P, 2, T], at=mix1)
        ropet = sb("ropet", [P, 2, T], at=mix1)
        padded = sb("padded", [P, 2, PAD + T + PAD], at=mix1)
        win = sb("win", [P, 2, PAD + T + PAD], at=mix1)
        win16 = sb("win16", [P, PAD + T + PAD], at=mix1)
        smax = sb("smax", [P, 8], at=mix1)
        sneg = sb("sneg", [P, 8], at=mix1)
        sden = sb("sden", [P, 8], at=mix1)
        srec = sb("srec", [P, 8], at=mix1)
        mix1.close()

        ffn = ExitStack()
        acth = sb("acth", [P, FT, T], F32R, at=ffn)
        actl = sb("actl", [P, FT, T], F32R, at=ffn)
        gn = sb("gn", [P, 2, T], at=ffn)
        un = sb("un", [P, 2, T], at=ffn)
        ffn.close()
        block1.close()

        mix2 = ExitStack()
        gu = sb("gu", [P, 4, T], at=mix2)
        bsb = sb("bsb", [P, 4, P], at=mix2)
        causal = sb("causal", [P, P], at=mix2)
        tri = sb("tri", [P, T], at=mix2)
        cmpbias = sb("cmpbias", [P, NQ, NCMP], at=mix2)
        cmpseen = sb("cmpseen", [P, NQ, NCMP], at=mix2)
        wg = sb("wg", [P, KT, NGATE], at=mix2)
        wgh = sb("wgh", [P, KT, NGATE], F32R, at=mix2)
        wgl = sb("wgl", [P, KT, NGATE], F32R, at=mix2)
        gateb = sb("gateb", [P, NGATE], at=mix2)
        gates = sb("gates", [P, NQ, NGATE], at=mix2)
        rcol = sb("rcol", [P, NQ], at=mix2)
        vec2 = sb("vec2", [P, 3, 4], at=mix2)
        poscol = sb("poscol", [P, 2, SLABS], at=mix2)
        w2k = sb("w2k", [P, 2, P], at=mix2)
        w2v = sb("w2v", [P, 2, HD], at=mix2)
        kdup = sb("kdup", [P, 2, NKV, T], at=mix2)
        vall = sb("vall", [P, 2, NQ, P], at=mix2)
        qall = sb("qall", [P, 4, T], at=mix2)
        oall = sb("oall", [P, 4, T], at=mix2)
        kcall = sb("kcall", [P, NKV, NCMP], at=mix2)
        vcall = sb("vcall", [P, NKV, HD], at=mix2)
        rstd2 = sb("rstd2", [P, T], at=mix2)

        comp = ExitStack()
        gv = sb("gv", [P, 4, T], at=comp)
        gvtok = sb("gvtok", [P, 4, NQ, P], at=comp)
        wst = sb("wst", [P, 8, P], at=comp)
        vs2 = sb("vs2", [P, 2, T], at=comp)

        def svt(t):
            return vs2[:, t % 2, :].rearrange("p (c n) -> p c n", c=NQ)
        w1 = sb("w1", [P, SLABS, CH], at=comp)
        shifted = sb("shifted", [P, NKV, T], at=comp)
        blk = sb("blk", [P, 2, SLABS, NKV * NCMP], at=comp)
        hid = sb("hid", [P, 2, 2, NKV * NCMP], at=comp)
        comp.close()
        attn2 = ExitStack()
        mh2 = sb("mh2", [P, KT, T], F32R, at=attn2)
        ml2 = sb("ml2", [P, KT, T], F32R, at=attn2)
        kst = sb("kst", [P, 2, T], at=attn2)
        vst = sb("vst", [P, 2, NQ, HD], at=attn2)
        qst = sb("qst", [P, 2, T], at=attn2)
        kcst = sb("kcst", [P, NCMP], at=attn2)
        vcst = sb("vcst", [P, HD], at=attn2)
        gst = sb("gst", [P, NQ, 3, 4], at=attn2)
        sc2 = sb("sc2", [P, 2, 2, T], at=attn2)
        scc = sb("scc", [P, NQ, NCMP], at=attn2)
        pt2 = sb("pt2", [P, 2, 2, T], at=attn2)
        ptc = sb("ptc", [P, 2, T], at=attn2)
        smax2 = sb("smax2", [P, 2, 2], at=attn2)
        sneg2 = sb("sneg2", [P, 2, 2], at=attn2)
        sden2 = sb("sden2", [P, 2, 2], at=attn2)
        srec2 = sb("srec2", [P, 2, 2], at=attn2)
        coef2 = sb("coef2", [P, 2, 2], at=attn2)
        cmax = sb("cmax", [P, NQ], at=attn2)
        cden = sb("cden", [P, NQ], at=attn2)
        attn2.close()
        mix2.close()

        B = [ctx.enter_context(nc.psum_tensor(f"bank{i}", [P, T], F32)) for i in range(8)]

        raw_in = [sem("raw_in0"), sem("raw_in1")]
        x_in = sem("x_in")
        const_in = sem("const_in")
        const2_in = sem("const2_in")
        pos_in = sem("pos_in")
        w1k_in = sem("w1k_in")
        w1v_in = sem("w1v_in")
        out_done = sem("out_done")
        split_begun = sem("split_begun")
        hi_split = sem("hi_split")
        split_done = sem("split_done")
        unit_used = sem("unit_used")
        x_done = sem("x_done")
        sq_done = sem("sq_done")
        ss_done = sem("ss_done")
        xh_done = sem("xh_done")
        xl_done = sem("xl_done")
        mean_done = sem("mean_done")
        root_done = sem("root_done")
        rstd_done = sem("rstd_done")
        layer_set = sem("layer_set")
        gu_evac = sem("gu_evac")
        silu_done = sem("silu_done")
        act_part = sem("act_part")
        act_done = sem("act_done")
        acc_done = sem("acc_done")
        trig = sem("trig")
        trig_act = sem("trig_act")
        tables_done = sem("tables_done")
        pool_step = sem("pool_step")
        pool_evac = sem("pool_evac")
        qk_raw = sem("qk_raw")
        v_evac = sem("v_evac")
        rot_done = sem("rot_done")
        rope_a = sem("rope_a")
        rope_b = sem("rope_b")
        rope_done = sem("rope_done")
        vt_done = sem("vt_done")
        vtok_done = sem("vtok_done")
        s_done = sem("s_done")
        dve_turn = sem("dve_turn")
        t_done = sem("t_done")
        neg_done = sem("neg_done")
        exp_done = sem("exp_done")
        rec_done = sem("rec_done")
        p_done = sem("p_done")
        tr_done = sem("tr_done")
        pte_done = sem("pte_done")
        pv_done = sem("pv_done")
        poolmm_done = sem("poolmm_done")
        out_turn = sem("out_turn")
        mh_done = sem("mh_done")
        ml_done = sem("ml_done")
        evac2 = sem("evac2")
        half2 = sem("half2")
        gelu_in = sem("gelu_in")
        gelu_done = sem("gelu_done")
        sq2_done = sem("sq2_done")
        ss2_done = sem("ss2_done")
        mean2 = sem("mean2")
        root2 = sem("root2")
        rstd2_done = sem("rstd2_done")
        wg_part = sem("wg_part")
        wg_done = sem("wg_done")
        gate_mm = sem("gate_mm")
        gate_a = sem("gate_a")
        gate_b = sem("gate_b")
        gates_done = sem("gates_done")
        rc_mm = sem("rc_mm")
        rcol_done = sem("rcol_done")
        shift_done = sem("shift_done")
        blk_done = sem("blk_done")
        hid_mm = sem("hid_mm")
        hid_done = sem("hid_done")
        cmp_mm = sem("cmp_mm")
        cmp_done = sem("cmp_done")
        v2_mm = sem("v2_mm")
        v2_done = sem("v2_done")
        vn_done = sem("vn_done")
        gt_mm = sem("gt_mm")
        gt_done = sem("gt_done")
        ws_done = sem("ws_done")
        sv_mm = sem("sv_mm")
        sv_add = sem("sv_add")
        a_done = sem("a_done")
        norm_mul = sem("norm_mul")
        mh2_done = sem("mh2_done")
        ml2_done = sem("ml2_done")
        stage_open = sem("stage_open")
        staged = sem("staged")
        s2_done = sem("s2_done")
        turn2 = sem("turn2")
        t2_done = sem("t2_done")
        neg2_done = sem("neg2_done")
        exp2_done = sem("exp2_done")
        rec2_done = sem("rec2_done")
        coef2_done = sem("coef2_done")
        p2_done = sem("p2_done")
        cs_done = sem("cs_done")
        ct_step = sem("ct_step")
        ct_done = sem("ct_done")
        ce_done = sem("ce_done")
        cn_step = sem("cn_step")
        cp_done = sem("cp_done")
        ctr_done = sem("ctr_done")
        cpt_done = sem("cpt_done")
        tr2_done = sem("tr2_done")
        pte2_done = sem("pte2_done")
        pv2_done = sem("pv2_done")
        o2_done = sem("o2_done")
        fin_done = sem("fin_done")

        N_CONST = 10
        N_CONST2 = 14
        STAGED = 9
        LAYER_COPIES = 3

        block = ctx.enter_context(nc.Block())

        @block.sync
        def _(sp):
            sp.dma_start(x[:, :, :], d["x"]).then_inc(x_in, 16)
            for dst, name in ((ident, "c_ident"), (ones, "c_ones"), (rot, "c_rot"), (band, "c_band"),
                              (invcount, "c_invcount"), (ropecol, "c_rope"), (poolw, "poolw"),
                              (poolscale, "poolscale"), (gains, "gains"), (gains2, "gains2")):
                sp.dma_start(dst[tuple([slice(None)] * len(dst.shape))], d[name]).then_inc(const_in, 16)

            def load_pair(pair, e, first):
                if not first:
                    sp.wait_ge(split_done, pair * 2 - 2)
                sp.dma_start(raw[:, e, :, :], d["stream"][pair]).then_inc(raw_in[e], 16)

            for e in range(2):
                load_pair(e, e, True)
            sp.dma_start(posi[:, :], d["positions"].to_broadcast([P, T])).then_inc(pos_in, 16)
            with sp.Fori(1, U_BLOCK2 // 4 + 1) as i:
                for e in range(2):
                    load_pair(i * 2 + e, e, False)

            sp.wait_ge(x_done, 8 * 8)
            for dst, name in ((wst, "ws_2"), (causal, "c_causal"), (tri, "c_tri"), (cmpbias, "c_cmpbias"),
                              (cmpseen, "c_cmpseen"), (wg, "wg_2"), (gateb, "gate_b_2"), (vec2, "vec_2"),
                              (poscol, "pos_2"), (w2v, "w2v_2")):
                sp.dma_start(dst[tuple([slice(None)] * len(dst.shape))], d[name]).then_inc(const2_in, 16)
            for half in range(2):
                sp.dma_start(w2k[:, :, HD * half:HD * half + HD], d["w2k_2"]).then_inc(const2_in, 16)
                sp.dma_start(bsb[HD * half:HD * half + HD, :, :],
                             d["bs_2"][half:half + 1].to_broadcast([HD, 4, P])).then_inc(const2_in, 16)
            sp.dma_start(w1[:, :, :], d["w1k_2"]).then_inc(w1k_in, 16)

            with sp.Fori(U_BLOCK2 // 4 + 1, U_BLOCK2 // 4 + 5) as i:
                for e in range(2):
                    load_pair(i * 2 + e, e, False)
            sp.wait_ge(hid_mm, 1)
            sp.dma_start(w1[:, :, :], d["w1v_2"]).then_inc(w1v_in, 16)
            with sp.Fori(U_BLOCK2 // 4 + 5, U_ALL // 4) as i:
                for e in range(2):
                    load_pair(i * 2 + e, e, False)
            sp.wait_ge(fin_done, KT)
            sp.dma_start(d["out"], x[:, :, :]).then_inc(out_done, 16)
            sp.wait_ge(out_done, 16)

        @block.gpsimd
        def _(pool):
            with pool.Fori(0, U_ALL // 4) as i:
                for e in range(2):
                    for h in range(2):
                        u = i * 4 + (2 * e + h)
                        if h == 0:
                            pool.wait_ge(raw_in[e], i * 16 + 16)
                        pool.wait_ge(unit_used, u + 1)
                        nc.gpsimd.nop().then_inc(split_begun, 1)
                        src = raw[:, e, h, :].rearrange("p (k n) -> p k n", k=8)
                        nc.gpsimd.tensor_scalar(wh[:, h, :, :], src, 1.0, 1.0, ALU.mult, ALU.mult)\
                            .then_inc(hi_split, 1)
                        pool.wait_ge(hi_split, u + 1)
                        nc.gpsimd.tensor_tensor(wl[:, h, :, :], src, wh[:, h, :, :].bitcast(F32),
                                                ALU.subtract).then_inc(split_done, 1)

        @block.tensor
        def _(pe):
            pe.nop().then_inc(unit_used, 2)
            pe.nop().then_inc(ss_done, 2)
            pe.nop().then_inc(tr_done, 2)
            pe.nop().then_inc(pv_done, 2)
            pe.nop().then_inc(tr2_done, 2)
            pe.nop().then_inc(pv2_done, 2)
            pe.nop().then_inc(ctr_done, 1)
            pe.wait_ge(const_in, 16 * N_CONST)

            def split_product(bank, slot, k, rh, rl, start, stop):
                mm = nc.tensor.matmul(bank, wh[:, slot, k, :], rh, start=start, stop=False)
                mm = nc.tensor.matmul(bank, wh[:, slot, k, :], rl, start=False, stop=False)
                return nc.tensor.matmul(bank, wl[:, slot, k, :], rh, start=False, stop=stop)

            def square_sum(prep, m, bank):
                pe.wait_ge(sq_done, prep * 8 + (m + 1))
                nc.tensor.matmul(bank[:, :], ones[:, :], sq[:, m % 2, :], start=(m == 0), stop=(m == KT - 1))\
                    .then_inc(ss_done, 1)

            def first_unit(prep, ready, u, slot):
                for m in range(5):
                    square_sum(prep, m, B[0])
                pe.wait_ge(split_done, u + 1)
                for k in range(KT):
                    if k + 5 < KT:
                        square_sum(prep, k + 5, B[0])
                    pe.wait_ge(xl_done, ready * 8 + (k + 1))
                    mm = split_product(B[4][:, :], slot, k, xh[:, k, :], xl[:, k, :], k == 0, k == KT - 1)
                mm.then_inc(unit_used, 1)

            def unit_blocks(u, slot, bank, ks, hi=xh, lo=xl):
                for k in ks:
                    if k == 0:
                        pe.wait_ge(split_done, u + 1)
                    mm = split_product(bank[:, :], slot, k, hi[:, k, :], lo[:, k, :], k == 0, k == KT - 1)
                if ks[-1] == KT - 1:
                    mm.then_inc(unit_used, 1)

            def feed_forward(n, prep, ready, u0):
                first_unit(prep, ready, u0, 0)
                for j in range(1, 4):
                    unit_blocks(u0 + j, j % 2, B[4 + j], range(KT))
                with pe.Fori(1, FT // 2) as i:
                    for j in range(4):
                        pe.wait_ge(gu_evac, i * 4 + (n * 2 * FT + (j - 3)))
                        unit_blocks(i * 4 + (u0 + j), j % 2, B[4 + j], range(KT))

                def down(f, f0, at, first, last):
                    h, lo = acth[:, at, :], actl[:, at, :]
                    if not isinstance(at, int):
                        h, lo = h.rearrange("p a t -> p (a t)"), lo.rearrange("p a t -> p (a t)")
                    pe.wait_ge(act_done, f + 1 + n * FT)
                    pe.wait_ge(split_done, f + 1 + (u0 + 2 * FT))
                    for m in range(KT):
                        if first and m == 4:
                            pe.wait_ge(gu_evac, (n + 1) * (2 * FT))
                        mm = split_product(B[m][:, :], f0 % 2, m, h, lo, first, last)
                        if last and m < KT - 1:
                            mm.then_inc(acc_done, 1)
                    mm.then_inc(unit_used, 1)

                down(0, 0, 0, True, False)
                down(1, 1, 1, False, False)
                with pe.Fori(1, FT // 2 - 1) as i:
                    for e in range(2):
                        down(i * 2 + e, e, bass.ds(i * 2 + e, 1), False, False)
                down(FT - 2, 0, FT - 2, False, False)
                down(FT - 1, 1, FT - 1, False, True)

            def mixer1(l):
                u0 = l * U_LAYER + U_FFN
                first_unit(l * 3 + 1, l * 3 + 1, u0, 0)
                unit_blocks(u0 + 1, 1, B[5], range(KT))

                def rotate(pair, e, which):
                    pe.wait_ge(qk_raw, pair * 2 + (which + 1))
                    nc.tensor.matmul(B[6][:, :], rot[:, :], qkraw[:, which, :], start=True, stop=True)\
                        .then_inc(rot_done, 1)

                pe.wait_ge(pool_evac, l * 2 + 1)
                unit_blocks(u0 + 2, 0, B[4], range(KT))
                pe.wait_ge(pool_evac, l * 2 + 2)
                unit_blocks(u0 + 3, 1, B[5], range(KT))
                rotate(l * PAIRS, 0, 0)
                unit_blocks(u0 + 4, 0, B[4], range(KT))
                pe.wait_ge(rope_a, l * (2 * PAIRS) + 1)
                rotate(l * PAIRS, 0, 1)

                def pair_steps(j, e, more):
                    pair = l * PAIRS + j
                    step0 = pair * 8
                    u = u0 + 5 + j * 3
                    slot = (1 + e) % 2
                    work = [(n, k) for n in range(3) for k in range(KT)] if more else []

                    def fill(count):
                        for n, k in [work.pop(0) for _ in range(count if more else 0)]:
                            if k == 0:
                                if n == 1:
                                    pe.wait_ge(v_evac, pair + 1)
                                else:
                                    pe.wait_ge(qk_raw, pair * 2 + (2 if n == 0 else 3))
                            unit_blocks(u + n, (slot + n) % 2, B[4 + (slot + n) % 2], [k])

                    def scores(s):
                        h, i = HD * (s // 4), P * (s % 4)
                        if s == 0:
                            pe.wait_ge(rope_done, pair * 2 + 3)
                        pe.wait_ge(t_done, step0 + (s + 1))
                        nc.tensor.matmul(B[1 + s % 2][:, :], qk[h:h + HD, e, 0, i:i + P], qk[h:h + HD, e, 1, :],
                                         start=True, stop=True).then_inc(s_done, 1)

                    def turn(s):
                        pe.wait_ge(p_done, step0 + (s + 1))
                        pe.wait_ge(pte_done, step0 + (s + 1))
                        for kt in range(NQ):
                            tr = nc.tensor.transpose(B[(3, 0)[s % 2]][:, kt * P:(kt + 1) * P],
                                                     sc[:, s % 2, kt * P:(kt + 1) * P], ident[:, :])
                        tr.then_inc(tr_done, 1)

                    def values(s):
                        h, i = HD * (s // 4), P * (s % 4)
                        if s == 0:
                            pe.wait_ge(vtok_done, pair + 1)
                            pe.wait_ge(ml_done, l * 8 + j + 1)
                        pe.wait_ge(pte_done, step0 + (s + 3))
                        for kt in range(NQ):
                            mm = nc.tensor.matmul(B[7][h:h + HD, i:i + P], vtok[:, e, kt, h:h + HD],
                                                  pt[:, s % 2, kt * P:(kt + 1) * P],
                                                  start=(kt == 0), stop=(kt == NQ - 1))
                        mm.then_inc(pv_done, 1)

                    for s in range(8):
                        scores(s)
                        fill(2)
                        if s == 1:
                            pe.wait_ge(v_evac, pair + 1)
                            pe.wait_ge(rope_a, pair * 2 + 2)
                            for kt in range(NQ):
                                tr = nc.tensor.transpose(B[6][:, kt * P:(kt + 1) * P],
                                                         vraw[:, kt * P:(kt + 1) * P], ident[:, :])
                            tr.then_inc(vt_done, 1)
                        if s == 5 and more:
                            pe.wait_ge(vtok_done, pair + 1)
                            rotate(pair + 1, 1 - e, 0)
                        if s in (2, 4) and not more:
                            t = s // 2 - 1
                            for h in (0, HD):
                                mm = nc.tensor.matmul(B[4 + t][h:h + HD, :], poolw_now[h:h + HD, t, :],
                                                      padded[h:h + HD, t, PAD:PAD + T], start=True, stop=True)
                            mm.then_inc(poolmm_done, 1)
                        if s >= 2:
                            turn(s - 2)
                        if s >= 3:
                            values(s - 3)
                    fill(3)
                    turn(6)
                    values(5)
                    if more:
                        pe.wait_ge(rope_a, pair * 2 + 3)
                        rotate(pair + 1, 1 - e, 1)
                    fill(3)
                    turn(7)
                    values(6)
                    fill(2)
                    values(7)

                with pe.Fori(0, 2) as it:
                    for e in range(2):
                        pair_steps(it * 2 + e, e, True)
                pair_steps(4, 0, True)
                pair_steps(5, 1, False)

                pe.wait_ge(ml_done, l * 8 + 8)
                for m in range(KT):
                    unit_blocks(u0 + (U_PROJ + m), m % 2, B[m], range(KT - 1), mh1, ml1)
                    if m == 0:
                        pe.wait_ge(ml_done, l * 8 + 9)
                    unit_blocks(u0 + (U_PROJ + m), m % 2, B[m], [KT - 1], mh1, ml1)

            with pe.Fori(0, DEPTH) as l:
                feed_forward(l * 2, l * 3, l * 3, l * U_LAYER)
                mixer1(l)
                feed_forward(l * 2 + 1, l * 3 + 2, l * 3 + 2, l * U_LAYER + (U_FFN + U_PROJ + U_OUT))

            for m in range(KT):
                square_sum(6, m, B[0])
            u0 = U_BLOCK2
            first_unit(7, 6, u0, 0)
            unit_blocks(u0 + 1, 1, B[5], range(KT))
            with pe.Fori(0, 4) as i:
                for j in range(4):
                    pe.wait_ge(evac2, i * 4 + (j + 1))
                    unit_blocks(i * 4 + (u0 + 2 + j), j % 2, B[4 + (2 + j) % 4], range(KT))

            pe.wait_ge(wg_done, 1)
            for i in range(NQ):
                for k in range(KT):
                    a, b = xh[:, k, i * P:(i + 1) * P], xl[:, k, i * P:(i + 1) * P]
                    o = B[0][:, NGATE * i:NGATE * (i + 1)]
                    nc.tensor.matmul(o, a, wgh[:, k, :], start=(k == 0), stop=False)
                    nc.tensor.matmul(o, a, wgl[:, k, :], start=False, stop=False)
                    mm = nc.tensor.matmul(o, b, wgh[:, k, :], start=False, stop=(k == KT - 1))
            mm.then_inc(gate_mm, 1)

            def sum_squares2(n, src, bank):
                for t in range(4):
                    pe.wait_ge(sq2_done, 4 * n + t + 1)
                    mm = nc.tensor.matmul(bank[:, :], ones[:, :], src[:, t, :], start=(t == 0), stop=(t == 3))
                mm.then_inc(ss2_done, 1)

            sum_squares2(0, oall, B[1])
            for i in range(NQ):
                tr = nc.tensor.transpose(B[2][:, i * P:(i + 1) * P], rstd[:, i * P:(i + 1) * P], ident[:, :])
            tr.then_inc(rc_mm, 1)

            def hidden(which, bank):
                pe.wait_ge(blk_done, 4 * which + 4)
                pe.wait_ge((w1k_in, w1v_in)[which], 16)
                for m in range(2):
                    for s in range(SLABS):
                        mm = nc.tensor.matmul(bank[:, HD * m:HD * m + NKV * NCMP], w1[:, s, P * m:P * (m + 1)],
                                              blk[:, which, s, :], start=(s == 0), stop=(s == SLABS - 1))
                mm.then_inc(hid_mm, 1)

            hidden(0, B[3])
            pe.wait_ge(evac2, U_PROJ2)
            for n in range(2):
                for kt in range(NQ):
                    tr = nc.tensor.transpose(B[4 + n][:, kt * P:(kt + 1) * P], vs2[:, n, kt * P:(kt + 1) * P],
                                             ident[:, :])
                tr.then_inc(v2_mm, 1)
            pe.wait_ge(rstd2_done, 1)
            hidden(1, B[1])
            pe.wait_ge(hid_done, 1)
            pe.wait_ge(rcol_done, 1)
            for m in range(2):
                mm = nc.tensor.matmul(B[2][:, 0:NKV * NCMP], w2k[:, m, :], hid[:, 0, m, :],
                                      start=(m == 0), stop=(m == 1))
            mm.then_inc(cmp_mm, 1)

            for t in range(4):
                pe.wait_ge(vn_done, t + 1)
                if t >= 2:
                    pe.wait_ge(gt_done, t - 1)
                for c in range(NQ):
                    tr = nc.tensor.transpose(B[6 + t % 2][:, c * P:(c + 1) * P], gv[:, t, c * P:(c + 1) * P],
                                             ident[:, :])
                tr.then_inc(gt_mm, 1)
            pe.wait_ge(hid_done, 2)
            pe.wait_ge(gate_a, 1)
            for kv in range(NKV):
                for m in range(2):
                    mm = nc.tensor.matmul(B[0][0:NCMP, HD * kv:HD * (kv + 1)],
                                          hid[:, 1, m, NCMP * kv:NCMP * (kv + 1)], w2v[:, m, :],
                                          start=(m == 0), stop=(m == 1))
            mm.then_inc(cmp_mm, 1)
            pe.wait_ge(ws_done, 1)
            pe.wait_ge(v2_done, 2)
            for t in range(4):
                pe.wait_ge(gt_done, t + 1)
                if t >= 2:
                    pe.wait_ge(sv_add, t - 1)
                for h in range(2):
                    for c in range(NQ):
                        mm = nc.tensor.matmul(B[4 + t % 2][HD * h:HD * (h + 1), c * P:(c + 1) * P],
                                              gvtok[:, t, c, HD * h:HD * (h + 1)], wst[:, 2 * t + h, :],
                                              start=True, stop=True)
                mm.then_inc(sv_mm, 1)
            sum_squares2(1, oall, B[6])

            def turn2_(g, s):
                i, par = s % 4, s % 2
                G = g * 16 + s
                pe.wait_ge(p2_done, G * 2 + 2)
                pe.wait_ge(pte2_done, G * 2 + 2)
                for kt in range(i + 1):
                    nc.tensor.transpose(B[6][:, kt * P:(kt + 1) * P], sc2[:, par, 0, kt * P:(kt + 1) * P], ident[:, :])
                for kt in range(i + 1):
                    tr = nc.tensor.transpose(B[0][:, kt * P:(kt + 1) * P], sc2[:, par, 1, kt * P:(kt + 1) * P],
                                             ident[:, :])
                tr.then_inc(tr2_done, 1)

            def compressed_scores(g, hh):
                h = HD * (hh % 2)
                pe.wait_ge(cpt_done, g * 4 + (hh + 1))
                for i in range(NQ):
                    mm = nc.tensor.matmul(B[5][:, NCMP * i:NCMP * (i + 1)], qst[h:h + HD, hh // 2, i * P:(i + 1) * P],
                                          kcst[h:h + HD, :], start=True, stop=True)
                mm.then_inc(cs_done, 1)

            def compressed_turn(g, hh):
                pe.wait_ge(cp_done, g * 4 + (hh + 1))
                for i in range(NQ):
                    tr = nc.tensor.transpose(B[5][0:NCMP, i * P:(i + 1) * P], scc[:, i, :], ident[:, :])
                tr.then_inc(ctr_done, 1)

            def values2(g, s):
                h, i, par = HD * ((s // 4) % 2), s % 4, s % 2
                G = g * 16 + s
                if s % 8 == 0:
                    pe.wait_ge(o2_done, g * 2 + (s // 8 + 1))
                if i == 0:
                    pe.wait_ge(cpt_done, g * 4 + (s // 4 + 2))
                pe.wait_ge(pte2_done, G * 2 + 4)
                o = B[7][h:h + HD, i * P:(i + 1) * P]
                nc.tensor.matmul(o, vst[:, 0, 0, :], pt2[:, par, 0, 0:P], start=True, stop=False)
                for kt in range(1, i + 1):
                    nc.tensor.matmul(o, vst[:, 0, kt, :], pt2[:, par, 0, kt * P:(kt + 1) * P], start=False, stop=False)
                for kt in range(i + 1):
                    nc.tensor.matmul(o, vst[:, 1, kt, :], pt2[:, par, 1, kt * P:(kt + 1) * P], start=False, stop=False)
                nc.tensor.matmul(o, vcst[0:NCMP, :], ptc[0:NCMP, (s // 4) % 2, i * P:(i + 1) * P],
                                 start=False, stop=True)\
                    .then_inc(pv2_done, 1)

            with pe.Fori(0, NKV) as g:
                pe.wait_ge(staged, (g + 1) * STAGED)
                compressed_scores(g, 0)
                compressed_turn(g, 0)
                for s in range(16):
                    t2, h, i, par = s // 8, HD * ((s // 4) % 2), s % 4, s % 2
                    n = P * (i + 1)
                    pe.wait_ge(t2_done, g * 32 + (2 * s + 2))
                    q = qst[h:h + HD, t2, i * P:(i + 1) * P]
                    nc.tensor.matmul(B[1 + par][:, 0:n], q, kst[h:h + HD, 0, 0:n], start=True, stop=True)
                    nc.tensor.matmul(B[3 + par][:, 0:n], q, kst[h:h + HD, 1, 0:n], start=True, stop=True)\
                        .then_inc(s2_done, 1)
                    if i == 0 and s < 12:
                        compressed_scores(g, s // 4 + 1)
                    if s >= 1:
                        turn2_(g, s - 1)
                    if s >= 2:
                        values2(g, s - 2)
                    if i == 3 and s < 12:
                        compressed_turn(g, s // 4 + 1)
                turn2_(g, 15)
                values2(g, 14)
                values2(g, 15)
            sum_squares2(2, gu, B[1])
            pe.wait_ge(ml2_done, 8)
            for m in range(KT):
                unit_blocks(u0 + (U_PROJ2 + m), m % 2, B[m], range(KT), mh2, ml2)
            feed_forward(4, 8, 7, u0 + (U_PROJ2 + U_OUT))
            for m in range(KT):
                square_sum(9, m, B[0])

        @block.scalar
        def _(act):
            act.nop().then_inc(pte_done, 2)
            act.nop().then_inc(pte2_done, 2)
            act.nop().then_inc(cpt_done, 1)

            def squares(prep, m):
                act.wait_ge(x_done, prep * 8 + (m + 1))
                act.wait_ge(ss_done, prep * 8 + (m + 1))
                nc.scalar.activation(sq[:, m % 2, :], x[:, m, :], ACT.Square).then_inc(sq_done, 1)

            def root(prep):
                act.wait_ge(mean_done, prep + 1)
                nc.scalar.activation(rstd[:, :], rstd[:, :], ACT.Sqrt).then_inc(root_done, 1)

            def prepare(prep, gains_of):
                for m in range(KT):
                    squares(prep, m)
                    nc.scalar.activation(xh[:, m, :], x[:, m, :], ACT.Identity, scale=gains_of(m))\
                        .then_inc(xh_done, 1)
                root(prep)

            def feed_forward(n):
                with act.Fori(0, FT // 2) as i:
                    for e in range(2):
                        act.wait_ge(gu_evac, i * 4 + (n * 2 * FT + (2 * e + 1)))
                        nc.scalar.activation(gn[:, e, :], gn[:, e, :], ACT.Silu).then_inc(silu_done, 1)

            def raw_qk(l, pair, which, off, bank):
                act.wait_ge(unit_used, off + 3)
                nc.scalar.activation(qkraw[:, which, :], bank[:, :], ACT.Copy).then_inc(qk_raw, 1)

            def mixer1(l):
                u0 = l * U_LAYER + U_FFN
                raw_qk(l, l * PAIRS, 0, u0 + 2, B[4])
                raw_qk(l, l * PAIRS, 1, u0 + 3, B[5])

                def pair_steps(j, e, more):
                    pair = l * PAIRS + j
                    step0 = pair * 8
                    u = u0 + 5 + j * 3
                    slot = (1 + e) % 2

                    def copy_turn(s):
                        act.wait_ge(tr_done, step0 + (s + 3))
                        act.wait_ge(pv_done, step0 + (s + 1))
                        nc.scalar.activation(pt[:, s % 2, :], B[(3, 0)[s % 2]][:, :], ACT.Copy).then_inc(pte_done, 1)

                    for s in range(8):
                        act.wait_ge(neg_done, step0 + (s + 1))
                        nc.scalar.activation(sc[:, s % 2, :], sc[:, s % 2, :], ACT.Exp, bias=sneg[:, s:s + 1],
                                             scale=SCALE, accum_out=sden[:, s:s + 1]).then_inc(exp_done, 1)
                        if s == 2:
                            act.wait_ge(vt_done, pair + 1)
                            nc.scalar.activation(vtok[:, e, :, :], B[6][:, :].rearrange("p (k n) -> p k n", k=NQ),
                                                 ACT.Copy).then_inc(vtok_done, 1)
                        if s >= 2:
                            copy_turn(s - 2)
                        if s == 4 and more:
                            raw_qk(l, pair + 1, 0, u, B[4 + slot])
                        if s in (3, 5) and not more:
                            t = (s - 3) // 2
                            act.wait_ge(poolmm_done, l * 2 + (t + 1))
                            nc.scalar.activation(mh1[:, t, :], B[4 + t][:, :], ACT.Identity,
                                                 scale=poolscale_now[:, t:t + 1]).then_inc(mh_done, 1)
                    if more:
                        raw_qk(l, pair + 1, 1, u + 1, B[4 + (slot + 1) % 2])
                    copy_turn(6)
                    copy_turn(7)
                    act.wait_ge(pv_done, step0 + 10)

                with act.Fori(0, 2) as it:
                    for e in range(2):
                        pair_steps(it * 2 + e, e, True)
                        act.nop().then_inc(out_turn, 1)
                        nc.scalar.activation(mh1[:, bass.ds(it * 2 + (2 + e), 1), :].rearrange("p a t -> p (a t)"),
                                             B[7][:, :], ACT.Copy).then_inc(mh_done, 1)
                for j in (4, 5):
                    pair_steps(j, j % 2, j == 4)
                    nc.scalar.activation(mh1[:, 2 + j, :], B[7][:, :], ACT.Copy).then_inc(mh_done, 1)

            act.wait_ge(trig, 4)
            nc.scalar.activation(sin[:, :], sin[:, :], ACT.Sin).then_inc(trig_act, 1)
            act.wait_ge(trig, 7)
            nc.scalar.activation(cos[:, :], cos[:, :], ACT.Sin).then_inc(trig_act, 1)

            with act.Fori(0, DEPTH) as l:
                act.wait_ge(layer_set, (l + 1) * LAYER_COPIES)
                prepare(l * 3, lambda m: gain[:, 0, m:m + 1])
                feed_forward(l * 2)
                prepare(l * 3 + 1, lambda m: gain[:, 1, m:m + 1])
                mixer1(l)
                prepare(l * 3 + 2, lambda m: gain[:, 2, m:m + 1])
                feed_forward(l * 2 + 1)

            for m in range(KT):
                squares(6, m)
            root(6)
            prepare(7, lambda m: gains2[:, 1, m:m + 1])

            def gelu(n, buf):
                act.wait_ge(gelu_in, n + 1)
                nc.scalar.activation(buf, buf, ACT.Gelu_apprx_tanh).then_inc(gelu_done, 1)

            for t in range(4):
                gelu(t, gv[:, t, :])
            for t in range(4):
                act.wait_ge(gelu_done, t + 1)
                nc.scalar.activation(oall[:, t, :], gv[:, t, :], ACT.Square).then_inc(sq2_done, 1)
            for t in range(4):
                gelu(4 + t, gu[:, t, :])

            def root_of(n):
                act.wait_ge(mean2, n + 1)
                nc.scalar.activation(rstd2[:, :], rstd2[:, :], ACT.Sqrt).then_inc(root2, 1)

            def hidden(which, bank):
                act.wait_ge(hid_mm, which + 1)
                nc.scalar.activation(hid[:, which, :, :],
                                     bank[:, 0:2 * HD].rearrange("p (m n) -> p m n", m=2)[:, :, 0:NKV * NCMP],
                                     ACT.Gelu_apprx_tanh).then_inc(hid_done, 1)

            root_of(0)
            hidden(0, B[3])
            for n in range(2):
                act.wait_ge(v2_mm, n + 1)
                nc.scalar.activation(vall[:, n, :, :], B[4 + n][:, :].rearrange("p (k n) -> p k n", k=NQ), ACT.Copy)\
                    .then_inc(v2_done, 1)
            hidden(1, B[1])
            for t in range(4):
                act.wait_ge(gt_mm, t + 1)
                nc.scalar.activation(gvtok[:, t, :, :], B[6 + t % 2][:, :].rearrange("p (c n) -> p c n", c=NQ),
                                     ACT.Copy).then_inc(gt_done, 1)
            act.wait_ge(gate_b, 1)
            nc.scalar.activation(gates[:, :, :], gates[:, :, :], ACT.Sigmoid).then_inc(gates_done, 1)

            def normed(n, src, scratch, base):
                for t in range(4):
                    if n == 1:
                        act.wait_ge(a_done, t + 1)
                    nc.scalar.activation(scratch[:, t, :], src[:, t, :], ACT.Square).then_inc(sq2_done, 1)
                root_of(n)
                for t in range(4):
                    act.wait_ge(norm_mul, 4 * (n - 1) + t + 1)
                    nc.scalar.activation(mh2[:, base + t, :], src[:, t, :], ACT.Copy).then_inc(mh2_done, 1)

            normed(1, gu, oall, 0)

            def copy_turn2(g, s):
                i, par = s % 4, s % 2
                G = g * 16 + s
                n = P * (i + 1)
                act.wait_ge(tr2_done, G + 3)
                act.wait_ge(pv2_done, G + 1)
                nc.scalar.activation(pt2[:, par, 0, 0:n], B[6][:, 0:n], ACT.Copy).then_inc(pte2_done, 1)
                nc.scalar.activation(pt2[:, par, 1, 0:n], B[0][:, 0:n], ACT.Copy).then_inc(pte2_done, 1)

            def compressed_exp(g, hh):
                act.wait_ge(ct_done, g * 4 + (hh + 1))
                nc.scalar.activation(scc[:, :, :], scc[:, :, :], ACT.Exp, scale=SCALE).then_inc(ce_done, 1)

            def compressed_copy(g, hh):
                act.wait_ge(ctr_done, g * 4 + (hh + 2))
                if hh >= 2:
                    act.wait_ge(pv2_done, g * 16 + (4 * (hh - 1) + 2))
                nc.scalar.activation(ptc[0:NCMP, hh % 2, :], B[5][0:NCMP, :], ACT.Copy).then_inc(cpt_done, 1)

            with act.Fori(0, NKV) as g:
                compressed_exp(g, 0)
                compressed_copy(g, 0)
                for s in range(16):
                    i, par = s % 4, s % 2
                    n = P * (i + 1)
                    act.wait_ge(neg2_done, g * 16 + (s + 1))
                    for src, c in ((sc2[:, par, 0, 0:n], 0), (sc2[:, par, 1, 0:n], 1)):
                        nc.scalar.activation(src, src, ACT.Exp, bias=sneg2[:, par, c:c + 1], scale=SCALE,
                                             accum_out=sden2[:, par, c:c + 1]).then_inc(exp2_done, 1)
                    if s >= 1:
                        copy_turn2(g, s - 1)
                    if i == 1 and s < 12:
                        compressed_exp(g, s // 4 + 1)
                    if i == 3 and s < 12:
                        compressed_copy(g, s // 4 + 1)
                copy_turn2(g, 15)
            act.wait_ge(o2_done, 5)
            normed(2, oall, gu, 4)
            prepare(8, lambda m: gains2[:, 2, m:m + 1])
            feed_forward(4)
            for m in range(KT):
                squares(9, m)
            root(9)

        @block.vector
        def _(dve):
            V = nc.vector
            dve.nop().then_inc(t_done, 2)
            dve.nop().then_inc(ml_done, 1)
            dve.nop().then_inc(rope_done, 1)
            dve.nop().then_inc(t2_done, 4)
            dve.nop().then_inc(o2_done, 1)
            dve.wait_ge(x_in, 16)
            dve.nop().then_inc(x_done, KT)

            dve.wait_ge(const_in, 16 * N_CONST)
            dve.wait_ge(pos_in, 16)
            TURN = 6.283185307179586
            C1 = 6.28125
            C2 = 2029 / 2 ** 20
            C3 = TURN - C1 - C2
            MAGIC = 12582912.0
            PI = 3.1415925
            a, k = sin, cos
            V.tensor_copy(a[:, :], posi[:, :]).then_inc(trig, 1)
            dve.wait_ge(trig, 1)
            V.tensor_scalar(a[:, :], a[:, :], ropecol[:, 0:1], None, ALU.mult).then_inc(trig, 1)
            dve.wait_ge(trig, 2)
            V.tensor_scalar(k[:, :], a[:, :], 1.0 / TURN, MAGIC, ALU.mult, ALU.add).then_inc(tables_done, 1)
            dve.wait_ge(tables_done, 1)
            V.tensor_scalar(k[:, :], k[:, :], -MAGIC, None, ALU.add).then_inc(tables_done, 1)
            for n, c in enumerate((C1, C2, C3)):
                dve.wait_ge(tables_done, 2 + n)
                V.scalar_tensor_tensor(a[:, :], k[:, :], -c, a[:, :], ALU.mult, ALU.add).then_inc(tables_done, 1)
            dve.wait_ge(tables_done, 5)
            V.tensor_scalar(a[:, :], a[:, :], PI, -PI, ALU.min, ALU.max).then_inc(trig, 1)
            dve.wait_ge(trig, 3)
            V.tensor_scalar(k[:, :], a[:, :], TURN / 4, None, ALU.add).then_inc(trig, 1)
            dve.wait_ge(trig, 4)
            V.tensor_scalar(cosr[:, :], k[:, :], PI, -TURN, ALU.is_gt, ALU.mult).then_inc(trig, 1)
            dve.wait_ge(trig, 5)
            V.tensor_tensor(k[:, :], k[:, :], cosr[:, :], ALU.add).then_inc(trig, 1)
            dve.wait_ge(trig, 6)
            V.tensor_scalar(k[:, :], k[:, :], PI, -PI, ALU.min, ALU.max).then_inc(trig, 1)
            dve.wait_ge(trig_act, 2)
            V.tensor_scalar(cos[:, :], cos[:, :], ropecol[:, 1:2], ropecol[:, 2:3], ALU.mult, ALU.add)\
                .then_inc(tables_done, 1)
            V.tensor_scalar(sin[:, :], sin[:, :], ropecol[:, 1:2], None, ALU.mult).then_inc(tables_done, 1)
            dve.wait_ge(tables_done, 7)

            def inverse_rms(prep):
                dve.wait_ge(ss_done, prep * 8 + 10)
                V.tensor_scalar(rstd[:, :], B[0][:, :], 1.0 / D, EPS, ALU.mult, ALU.add).then_inc(mean_done, 1)
                dve.wait_ge(root_done, prep + 1)
                V.reciprocal(rstd[:, :], rstd[:, :]).then_inc(rstd_done, 1)
                dve.wait_ge(rstd_done, prep + 1)

            def low_part(ready, m, g):
                dve.wait_ge(xh_done, ready * 8 + (m + 1))
                V.scalar_tensor_tensor(xl[:, m, :], x[:, m, :], g, xh[:, m, :].bitcast(F32), ALU.mult, ALU.subtract)\
                    .then_inc(xl_done, 1)

            def update(m, factor, sem_, value):
                dve.wait_ge(sem_, value)
                V.scalar_tensor_tensor(x[:, m, :], B[m][:, :], factor, x[:, m, :], ALU.mult, ALU.add)\
                    .then_inc(x_done, 1)

            def updates(factor, done, ready=None, g=None):
                for m in range(KT):
                    update(m, factor, *done(m))
                    if g is not None and m >= 1:
                        low_part(ready, m - 1, g(m - 1))
                if g is not None:
                    low_part(ready, KT - 1, g(KT - 1))

            def feed_forward(n):
                def evacuate(f, e):
                    if not isinstance(f, int):
                        dve.wait_ge(act_done, f + (n * FT - 1))
                    for j, dst in ((0, gn), (1, un)):
                        dve.wait_ge(unit_used, f * 2 + (ffn_unit[0] + (j + 3)))
                        V.tensor_tensor(dst[:, e, :], B[4 + 2 * e + j][:, :], rstd[:, :], ALU.mult)\
                            .then_inc(gu_evac, 1)

                def finish(f, e, at):
                    h, lo = acth[:, at, :], actl[:, at, :]
                    if not isinstance(at, int):
                        h, lo = h.rearrange("p a t -> p (a t)"), lo.rearrange("p a t -> p (a t)")
                    dve.wait_ge(gu_evac, f * 2 + (n * 2 * FT + 2))
                    dve.wait_ge(silu_done, f + (n * FT + 1))
                    V.tensor_tensor(h, gn[:, e, :], un[:, e, :], ALU.mult).then_inc(act_part, 1)
                    V.tensor_tensor(un[:, e, :], gn[:, e, :], un[:, e, :], ALU.mult).then_inc(act_part, 1)
                    dve.wait_ge(act_part, f * 2 + (n * 2 * FT + 2))
                    V.tensor_tensor(lo, un[:, e, :], h.bitcast(F32), ALU.subtract).then_inc(act_done, 1)

                evacuate(0, 0)
                evacuate(1, 1)
                finish(0, 0, 0)
                with dve.Fori(1, FT // 2) as i:
                    evacuate(i * 2, 0)
                    finish(i * 2 - 1, 1, bass.ds(i * 2 - 1, 1))
                    evacuate(i * 2 + 1, 1)
                    finish(i * 2, 0, bass.ds(i * 2, 1))
                finish(FT - 1, 1, FT - 1)

            ffn_unit = [0]

            def down_done(n, u0):
                return lambda m: (acc_done, n * 7 + (m + 1)) if m < KT - 1 else (unit_used, u0 + (U_FFN + 2))

            def mixer1(l):
                u0 = l * U_LAYER + U_FFN
                V.tensor_tensor(cosr[:, :], cos[:, :], rstd[:, :], ALU.mult).then_inc(pool_step, 1)
                V.tensor_tensor(sinr[:, :], sin[:, :], rstd[:, :], ALU.mult).then_inc(pool_step, 1)
                V.memset(padded[:, :, :], 0.0).then_inc(pool_step, 1)
                V.memset(win[:, :, :], 0.0).then_inc(pool_step, 1)
                POOL_OPS = 4 + 10
                ps = l * POOL_OPS
                dve.wait_ge(pool_step, ps + 4)
                for t in range(2):
                    dve.wait_ge(unit_used, u0 + (t + 3))
                    V.tensor_tensor(padded[:, t, PAD:PAD + T], B[4 + t][:, :], rstd[:, :], ALU.mult)\
                        .then_inc(pool_evac, 1)

                def step(n):
                    dve.wait_ge(pool_step, ps + n)

                dve.wait_ge(pool_evac, l * 2 + 2)
                V.tensor_tensor(win[:, :, 1:PAD + T + PAD], padded[:, :, 0:PAD + T + PAD - 1],
                                padded[:, :, 1:PAD + T + PAD], ALU.add).then_inc(pool_step, 1)
                step(5)
                V.tensor_tensor(win16[0:P, PAD - 6:PAD + T + 6], win[:, 1, PAD - 7:PAD + T + 5],
                                win[:, 1, PAD - 5:PAD + T + 7], ALU.add).then_inc(pool_step, 1)
                step(6)
                V.tensor_tensor(win[HD:P, 1, PAD:PAD + T], win[HD:P, 0, PAD - 1:PAD + T - 1],
                                win[HD:P, 0, PAD + 1:PAD + T + 1], ALU.add).then_inc(pool_step, 1)
                step(7)
                V.tensor_tensor(win[HD:P, 0, PAD:PAD + T], win[HD:P, 1, PAD:PAD + T],
                                invcount[HD:P, 0, :], ALU.mult).then_inc(pool_step, 1)
                V.tensor_tensor(win[0:HD, 0, PAD:PAD + T], win[0:HD, 0, PAD:PAD + T],
                                invcount[0:HD, 0, :], ALU.mult).then_inc(pool_step, 1)
                step(9)
                V.tensor_tensor(win[:, 1, PAD - 4:PAD + T + 4], win16[:, PAD - 6:PAD + T + 2],
                                win16[:, PAD - 2:PAD + T + 6], ALU.add).then_inc(pool_step, 1)
                step(10)
                V.tensor_tensor(win16[HD:P, PAD:PAD + T], win[HD:P, 1, PAD - 4:PAD + T - 4],
                                win[HD:P, 1, PAD + 4:PAD + T + 4], ALU.add).then_inc(pool_step, 1)
                V.tensor_tensor(win[0:HD, 1, PAD:PAD + T], win[0:HD, 1, PAD:PAD + T],
                                invcount[0:HD, 1, :], ALU.mult).then_inc(pool_step, 1)
                step(12)
                V.tensor_tensor(win[HD:P, 1, PAD:PAD + T], win16[HD:P, PAD:PAD + T],
                                invcount[HD:P, 1, :], ALU.mult).then_inc(pool_step, 1)
                step(13)
                V.tensor_tensor(padded[:, :, PAD:PAD + T], win[:, :, PAD:PAD + T], padded[:, :, PAD:PAD + T],
                                ALU.subtract).then_inc(pool_step, 1)
                step(14)

                def rope(pair, e, which):
                    n = pair * 2 + which
                    dve.wait_ge(rope_done, n + 1)
                    dve.wait_ge(rot_done, n + 1)
                    V.tensor_tensor(ropet[:, 0, :], B[6][:, :], sinr[:, :], ALU.mult).then_inc(rope_a, 1)
                    V.tensor_tensor(ropet[:, 1, :], qkraw[:, which, :], cosr[:, :], ALU.mult).then_inc(rope_b, 1)
                    dve.wait_ge(rope_b, n + 1)
                    dve.wait_ge(rope_a, n + 1)
                    V.tensor_tensor(qk[:, e, which, :], ropet[:, 0, :], ropet[:, 1, :], ALU.add)\
                        .then_inc(rope_done, 1)

                def v_out(u, bank):
                    dve.wait_ge(unit_used, u + 3)
                    V.tensor_tensor(vraw[:, :], bank[:, :], rstd[:, :], ALU.mult).then_inc(v_evac, 1)

                rope(l * PAIRS, 0, 0)
                rope(l * PAIRS, 0, 1)
                v_out(u0 + 4, B[4])

                def pair_steps(j, e, more):
                    pair = l * PAIRS + j
                    step0 = pair * 8
                    u = u0 + 5 + j * 3
                    slot = (1 + e) % 2

                    def normalise(s):
                        dve.wait_ge(exp_done, step0 + (s + 1))
                        V.reciprocal(srec[:, s:s + 1], sden[:, s:s + 1]).then_inc(rec_done, 1)
                        dve.wait_ge(rec_done, step0 + (s + 1))
                        V.tensor_scalar(sc[:, s % 2, :], sc[:, s % 2, :], srec[:, s:s + 1], None, ALU.mult)\
                            .then_inc(p_done, 1)

                    for s in range(8):
                        i = s % 4
                        dve.wait_ge(s_done, step0 + (s + 1))
                        dve.wait_ge(tr_done, step0 + (s + 1))
                        dve.nop().then_inc(dve_turn, 1)
                        off = 384 - P * i
                        V.tensor_tensor_reduce(sc[:, s % 2, :], B[1 + s % 2][:, :], band[:, off:off + T], 1.0,
                                               -3.0e38, ALU.add, ALU.max, smax[:, s:s + 1]).then_inc(t_done, 1)
                        dve.wait_ge(t_done, step0 + (s + 3))
                        V.tensor_scalar(sneg[:, s:s + 1], smax[:, s:s + 1], -SCALE, None, ALU.mult)\
                            .then_inc(neg_done, 1)
                        if s >= 1:
                            normalise(s - 1)
                        if s == 6 and more:
                            rope(pair + 1, 1 - e, 0)
                        if s in (4, 6) and not more:
                            t = s // 2 - 2
                            dve.wait_ge(mh_done, l * 8 + (t + 6))
                            V.scalar_tensor_tensor(ml1[:, t, :], B[4 + t][:, :], poolscale_now[:, t:t + 1],
                                                   mh1[:, t, :].bitcast(F32), ALU.mult, ALU.subtract)\
                                .then_inc(ml_done, 1)
                    normalise(7)
                    if more:
                        rope(pair + 1, 1 - e, 1)
                        v_out(u + 2, B[4 + slot])

                def output(done, at):
                    h, lo = mh1[:, at, :], ml1[:, at, :]
                    if not isinstance(at, int):
                        h, lo = h.rearrange("p a t -> p (a t)"), lo.rearrange("p a t -> p (a t)")
                    dve.wait_ge(mh_done, done)
                    V.tensor_tensor(lo, B[7][:, :], h.bitcast(F32), ALU.subtract).then_inc(ml_done, 1)

                with dve.Fori(0, 2) as it:
                    for e in range(2):
                        pair_steps(it * 2 + e, e, True)
                        output(l * 8 + it * 2 + (e + 1), bass.ds(it * 2 + (2 + e), 1))
                pair_steps(4, 0, True)
                output(l * 8 + 5, 6)
                pair_steps(5, 1, False)
                output(l * 8 + 8, 7)

            with dve.Fori(0, DEPTH) as l:
                V.tensor_copy(gain[:, :, :], gains[:, bass.ds(l, 1), :, :].rearrange("p a n k -> p (a n) k"))\
                    .then_inc(layer_set, 1)
                V.tensor_copy(poolw_now[:, :, :], poolw[:, bass.ds(l, 1), :, :].rearrange("p a n k -> p (a n) k"))\
                    .then_inc(layer_set, 1)
                V.tensor_copy(poolscale_now[:, :], poolscale[:, bass.ds(l, 1), :].rearrange("p a n -> p (a n)"))\
                    .then_inc(layer_set, 1)
                dve.wait_ge(layer_set, (l + 1) * LAYER_COPIES)
                for m in range(KT):
                    low_part(l * 3, m, gain[:, 0, m:m + 1])
                inverse_rms(l * 3)
                ffn_unit[0] = l * U_LAYER
                feed_forward(l * 2)
                updates(0.5, down_done(l * 2, l * U_LAYER), l * 3 + 1, lambda m: gain[:, 1, m:m + 1])
                inverse_rms(l * 3 + 1)
                mixer1(l)
                uo = l * U_LAYER + (U_FFN + U_PROJ)
                updates(1.0, lambda m: (unit_used, uo + (m + 3)), l * 3 + 2, lambda m: gain[:, 2, m:m + 1])
                inverse_rms(l * 3 + 2)
                ffn_unit[0] = l * U_LAYER + (U_FFN + U_PROJ + U_OUT)
                feed_forward(l * 2 + 1)
                updates(0.5, down_done(l * 2 + 1, l * U_LAYER + (U_FFN + U_PROJ + U_OUT)))

            inverse_rms(6)
            for m in range(KT):
                V.scalar_tensor_tensor(x[:, m, :], x[:, m, :], gains2[:, 0, m:m + 1], rstd[:, :], ALU.mult, ALU.mult)\
                    .then_inc(x_done, 1)
            for m in range(KT):
                dve.wait_ge(x_done, 8 * 7 + m + 1)
                low_part(6, m, gains2[:, 1, m:m + 1])
            inverse_rms(7)
            u0 = U_BLOCK2
            dve.wait_ge(const2_in, 16 * N_CONST2)
            V.tensor_copy(wgh[:, :, :], wg[:, :, :]).then_inc(wg_part, 1)
            dve.wait_ge(wg_part, 1)
            V.tensor_tensor(wgl[:, :, :], wg[:, :, :], wgh[:, :, :].bitcast(F32), ALU.subtract).then_inc(wg_done, 1)
            V.tensor_tensor(wst[:, :, :], wst[:, :, :],
                            causal[:, :].rearrange("p (a n) -> p a n", a=1).to_broadcast([P, 8, P]), ALU.mult)\
                .then_inc(ws_done, 1)

            def bank(n):
                dve.wait_ge(unit_used, u0 + n + 3)
                return B[4 + n % 4]

            def scaled(n, dst, last):
                V.tensor_tensor(dst, bank(n)[:, :], rstd[:, :], ALU.mult).then_inc(last, 1)

            halves = [0]
            for n in range(U_PROJ2):
                if n < 4:
                    scaled(n, gv[:, n, :], gelu_in)
                    dve.wait_ge(gelu_in, n + 1)
                elif n < 6:
                    which = n - 4
                    b = bank(n)
                    if which:
                        dve.wait_ge(blk_done, 4)
                    for kv in range(NKV):
                        r = slice(HD * kv, HD * kv + HD)
                        V.tensor_tensor(shifted[0:HD, kv, :], b[r, :], rstd[0:HD, :], ALU.mult).then_inc(shift_done, 1)
                        V.tensor_tensor(shifted[HD:P, kv, 0:T - 1], b[r, 1:T], rstd[HD:P, 1:T], ALU.mult)\
                            .then_inc(shift_done, 1)
                    dve.wait_ge(shift_done, 4 * which + 4)
                    for kv in range(NKV):
                        v = shifted[:, kv, :].rearrange("p (n s two) -> p s n two", s=8, two=2)
                        for half in range(2):
                            V.tensor_tensor(blk[:, which, 8 * half:8 * half + 8, NCMP * kv:NCMP * (kv + 1)],
                                            v[:, :, half:half + NCMP, 0],
                                            poscol[:, which, 8 * half:8 * half + 8]
                                            .rearrange("p (s a) -> p s a", a=1).to_broadcast([P, 8, NCMP]), ALU.add)\
                                .then_inc(blk_done, 1)
                elif n < 8:
                    b = bank(n)
                    for kv in range(NKV):
                        for half in range(2):
                            V.tensor_tensor(kdup[HD * half:HD * half + HD, n - 6, kv, :],
                                            b[HD * kv:HD * kv + HD, :], rstd[HD * half:HD * half + HD, :], ALU.mult)\
                                .then_inc(half2, 1)
                            halves[0] += 1
                    dve.wait_ge(half2, halves[0])
                elif n < 10:
                    scaled(n, vs2[:, n - 8, :], half2)
                    halves[0] += 1
                    dve.wait_ge(half2, halves[0])
                elif n < 14:
                    scaled(n, qall[:, n - 10, :], half2)
                    halves[0] += 1
                    dve.wait_ge(half2, halves[0])
                else:
                    scaled(n, gu[:, n - 14, :], gelu_in)
                    dve.wait_ge(gelu_in, 4 + n - 14 + 1)
                dve.nop().then_inc(evac2, 1)

            def inverse_rms2(n, b, width):
                dve.wait_ge(ss2_done, n + 1)
                V.tensor_scalar(rstd2[:, :], b[:, :], 1.0 / width, EPS, ALU.mult, ALU.add).then_inc(mean2, 1)
                dve.wait_ge(root2, n + 1)
                V.reciprocal(rstd2[:, :], rstd2[:, :]).then_inc(rstd2_done, 1)
                dve.wait_ge(rstd2_done, n + 1)

            inverse_rms2(0, B[1], 512)
            for t in range(4):
                V.scalar_tensor_tensor(gv[:, t, :], gv[:, t, :], vec2[:, 0, t:t + 1], rstd2[:, :], ALU.mult, ALU.mult)\
                    .then_inc(vn_done, 1)
            dve.wait_ge(rc_mm, 1)
            V.tensor_copy(rcol[:, :], B[2][:, :].rearrange("p (i n) -> p i n", i=NQ)[:, :, 0]).then_inc(rcol_done, 1)
            dve.wait_ge(rcol_done, 1)
            dve.wait_ge(gate_mm, 1)
            V.tensor_tensor(gates[:, :, :], B[0][:, 0:NQ * NGATE].rearrange("p (i n) -> p i n", i=NQ),
                            rcol[:, :].rearrange("p (i a) -> p i a", a=1).to_broadcast([P, NQ, NGATE]), ALU.mult)\
                .then_inc(gate_a, 1)
            dve.wait_ge(gate_a, 1)
            V.tensor_tensor(gates[:, :, :], gates[:, :, :],
                            gateb[:, :].rearrange("p (a n) -> p a n", a=1).to_broadcast([P, NQ, NGATE]), ALU.add)\
                .then_inc(gate_b, 1)
            dve.wait_ge(cmp_mm, 1)
            V.tensor_copy(kcall[:, :, :], B[2][:, 0:NKV * NCMP].rearrange("p (a n) -> p a n", a=NKV))\
                .then_inc(cmp_done, 1)
            dve.wait_ge(cmp_mm, 2)
            V.tensor_copy(vcall[0:NCMP, :, :], B[0][0:NCMP, 0:NKV * HD].rearrange("p (a n) -> p a n", a=NKV))\
                .then_inc(cmp_done, 1)
            dve.wait_ge(gelu_done, 8)
            for t in range(4):
                dve.wait_ge(sv_mm, t + 1)
                b = B[4 + t % 2]
                if t >= 2:
                    dve.wait_ge(a_done, t - 1)
                V.tensor_tensor(svt(t), b[:, :].rearrange("p (c n) -> p c n", c=NQ),
                                bsb[:, t:t + 1, :].to_broadcast([P, NQ, P]), ALU.add).then_inc(sv_add, 1)
                dve.wait_ge(sv_add, t + 1)
                V.tensor_tensor(gu[:, t, :], gu[:, t, :], vs2[:, t % 2, :], ALU.mult)\
                    .then_inc(a_done, 1)

            def normed(n, src, base):
                for t in range(4):
                    V.scalar_tensor_tensor(src[:, t, :], src[:, t, :], vec2[:, n, t:t + 1], rstd2[:, :],
                                           ALU.mult, ALU.mult).then_inc(norm_mul, 1)
                for t in range(4):
                    dve.wait_ge(norm_mul, 4 * (n - 1) + t + 1)
                    dve.wait_ge(mh2_done, 4 * (n - 1) + t + 1)
                    V.tensor_tensor(ml2[:, base + t, :], src[:, t, :], mh2[:, base + t, :].bitcast(F32), ALU.subtract)\
                        .then_inc(ml2_done, 1)

            inverse_rms2(1, B[6], 512)
            normed(1, gu, 0)

            dve.wait_ge(gates_done, 1)
            dve.wait_ge(cmp_done, 2)
            dve.wait_ge(v2_done, 2)
            with dve.Fori(0, NKV) as g:
                dve.wait_ge(pv2_done, g * 16 + 2)
                dve.nop().then_inc(stage_open, 1)
                for n in range(2):
                    V.tensor_copy(kst[:, n, :], kdup[:, n, bass.ds(g, 1), :].rearrange("p a t -> p (a t)"))\
                        .then_inc(staged, 1)
                    V.tensor_copy(vst[:, n, :, :], vall[:, n, :, bass.ds(g * HD, HD)]).then_inc(staged, 1)
                    V.tensor_copy(qst[:, n, :], qall[:, bass.ds(g * 2 + n, 1), :].rearrange("p a t -> p (a t)"))\
                        .then_inc(staged, 1)
                V.tensor_copy(kcst[:, :], kcall[:, bass.ds(g, 1), :].rearrange("p a t -> p (a t)")).then_inc(staged, 1)
                V.tensor_copy(vcst[0:NCMP, :], vcall[0:NCMP, bass.ds(g, 1), :].rearrange("p a t -> p (a t)"))\
                    .then_inc(staged, 1)
                V.tensor_copy(gst[:, :, :, :], gates[:, :, :].rearrange("p i (n h) -> p i n h", n=3)
                              [:, :, :, bass.ds(g * 4, 4)]).then_inc(staged, 1)
                dve.wait_ge(staged, (g + 1) * STAGED)

                def normalise2(s):
                    i, par, hh = s % 4, s % 2, s // 4
                    n = P * (i + 1)
                    G = g * 16 + s
                    dve.wait_ge(exp2_done, G * 2 + 2)
                    V.reciprocal(srec2[:, par, :], sden2[:, par, :]).then_inc(rec2_done, 1)
                    dve.wait_ge(rec2_done, G + 1)
                    V.tensor_tensor(coef2[:, par, :], srec2[:, par, :], gst[:, i, 1:3, hh], ALU.mult)\
                        .then_inc(coef2_done, 1)
                    dve.wait_ge(coef2_done, G + 1)
                    for c in range(2):
                        V.tensor_scalar(sc2[:, par, c, 0:n], sc2[:, par, c, 0:n], coef2[:, par, c:c + 1], None,
                                        ALU.mult).then_inc(p2_done, 1)

                def wide(v):
                    return v.rearrange("p (i a) -> p i a", a=1).to_broadcast([P, NQ, NCMP])

                def compressed_max(hh):
                    H = g * 4 + hh
                    dve.wait_ge(cs_done, H + 1)
                    dve.wait_ge(ctr_done, H + 1)
                    V.tensor_tensor(scc[:, :, :], B[5][:, 0:NQ * NCMP].rearrange("p (i n) -> p i n", i=NQ),
                                    cmpbias[:, :, :], ALU.add).then_inc(ct_step, 1)
                    dve.wait_ge(ct_step, H * 2 + 1)
                    V.reduce_max(cmax[:, :], scc[:, :, :], mybir.AxisListType.X).then_inc(ct_step, 1)
                    dve.wait_ge(ct_step, H * 2 + 2)
                    V.tensor_tensor(scc[:, :, :], scc[:, :, :], wide(cmax[:, :]), ALU.subtract).then_inc(ct_done, 1)

                def compressed_normalise(hh):
                    H = g * 4 + hh
                    dve.wait_ge(ce_done, H + 1)
                    V.reduce_sum(cden[:, :], scc[:, :, :], mybir.AxisListType.X).then_inc(cn_step, 1)
                    dve.wait_ge(cn_step, H * 4 + 1)
                    V.reciprocal(cden[:, :], cden[:, :]).then_inc(cn_step, 1)
                    dve.wait_ge(cn_step, H * 4 + 2)
                    V.tensor_tensor(cden[:, :], cden[:, :], gst[:, :, 0, hh], ALU.mult).then_inc(cn_step, 1)
                    dve.wait_ge(cn_step, H * 4 + 3)
                    V.tensor_tensor(scc[:, :, :], scc[:, :, :], wide(cden[:, :]), ALU.mult).then_inc(cn_step, 1)
                    dve.wait_ge(cn_step, H * 4 + 4)
                    V.tensor_tensor(scc[:, :, :], scc[:, :, :], cmpseen[:, :, :], ALU.mult).then_inc(cp_done, 1)

                def output2(t2, done):
                    dve.wait_ge(pv2_done, done)
                    V.tensor_scalar(oall[:, bass.ds(g * 2 + t2, 1), :].rearrange("p a t -> p (a t)"), B[7][:, :],
                                    1.0, None, ALU.mult).then_inc(o2_done, 1)

                compressed_max(0)
                compressed_normalise(0)

                for s in range(16):
                    i, par = s % 4, s % 2
                    n = P * (i + 1)
                    off = 384 - P * i
                    G = g * 16 + s
                    dve.wait_ge(s2_done, G + 1)
                    dve.wait_ge(tr2_done, G + 1)
                    dve.nop().then_inc(turn2, 1)
                    for c in range(2):
                        V.tensor_tensor_reduce(sc2[:, par, c, 0:n], B[1 + 2 * c + par][:, 0:n], tri[:, off:off + n],
                                               1.0, -3.0e38, ALU.add, ALU.max, smax2[:, par, c:c + 1])\
                            .then_inc(t2_done, 1)
                    dve.wait_ge(t2_done, G * 2 + 6)
                    V.tensor_scalar(sneg2[:, par, :], smax2[:, par, :], -SCALE, None, ALU.mult).then_inc(neg2_done, 1)
                    if s >= 1:
                        normalise2(s - 1)
                    if i == 0 and s < 12:
                        compressed_max(s // 4 + 1)
                    if i == 2 and s < 12:
                        compressed_normalise(s // 4 + 1)
                    if s == 10:
                        output2(0, g * 16 + 10)
                normalise2(15)
                output2(1, g * 16 + 18)
            inverse_rms2(2, B[1], 512)
            normed(2, oall, 4)
            uo = U_BLOCK2 + U_PROJ2
            updates(1.0, lambda m: (unit_used, uo + m + 3), 7, lambda m: gains2[:, 2, m:m + 1])
            inverse_rms(8)
            ffn_unit[0] = uo + U_OUT
            feed_forward(4)
            updates(1.0, down_done(4, uo + U_OUT))
            inverse_rms(9)
            for m in range(KT):
                V.scalar_tensor_tensor(x[:, m, :], x[:, m, :], gains2[:, 3, m:m + 1], rstd[:, :], ALU.mult, ALU.mult)\
                    .then_inc(fin_done, 1)


def lay_out(inputs):
    a = {k: np.asarray(v) for k, v in inputs.items()}

    def cols(w, c):
        return w[:, c:c + P].reshape(8, P, P).transpose(1, 0, 2)

    units = []

    def ffn(g, u, dn):
        for f in range(FT):
            units.append(cols(g, f * P))
            units.append(cols(u, f * P))
        for f in range(FT):
            units.append(dn[f * P:(f + 1) * P].reshape(P, 8, P))

    for l in range(DEPTH):
        ffn(a["ffn1_w_gate"][l], a["ffn1_w_up"][l], a["ffn1_w_down"][l])
        w = a["w_in"][l]
        units += [cols(w, 0), cols(w, P)]
        for j in range(PAIRS):
            units += [cols(w, POOL_W + n * PAIRS * P + j * P) for n in range(3)]
        units += [cols(a["w_out"][l], m * P) for m in range(KT)]
        ffn(a["ffn2_w_gate"][l], a["ffn2_w_up"][l], a["ffn2_w_down"][l])
    w = a["w_in_2"][0]
    units += [cols(w, c * P) for c in ORDER2]
    units += [cols(a["w_o_2"][0], m * P) for m in range(KT)]
    ffn(a["w_gate_2"][0], a["w_up_2"][0], a["w_down_2"][0])
    assert len(units) == U_ALL
    stream = np.empty((U_ALL // 2, P, 2, 8 * P), np.float32)
    for u, unit in enumerate(units):
        stream[u // 2, :, u % 2] = unit.reshape(P, 8 * P)

    def tiles(v):
        v = v.reshape(*v.shape[:-1], -1, P)
        return np.moveaxis(v, -1, 0)

    out = {
        "x": a["x"][0].T.reshape(KT, P, T).transpose(1, 0, 2),
        "positions": a["positions"].reshape(1, T),
        "stream": stream,
        "gains": tiles(np.stack([a["ffn1_norm"], a["mix_norm"], a["ffn2_norm"]], 1)),
        "gains2": tiles(np.stack([a["final_norm"], a["norm_mix_w_2"][0], a["norm_ffn_w_2"][0], a["final_norm_w_2"]])),
        "poolw": a["pool_w"].reshape(DEPTH, 2, P, HD).transpose(2, 0, 1, 3),
        "poolscale": tiles(a["pool_scale"]),
        "ws_2": a["gmlp_ws_2"][0].transpose(2, 0, 1),
        "bs_2": a["gmlp_bs_2"][0].reshape(4, 2, P).transpose(1, 0, 2),
        "wg_2": w[:, U_PROJ2 * P:].reshape(8, P, NGATE).transpose(1, 0, 2),
        "gate_b_2": np.broadcast_to(a["gate_b_2"], (P, NGATE)),
        "vec_2": tiles(np.concatenate([a["gmlp_norm_w_2"], a["out_norm_a_w_2"], a["out_norm_b_w_2"]])),
        "pos_2": np.stack([a["cmp_pos_k_2"][0], a["cmp_pos_v_2"][0]]).reshape(2, SLABS, P).transpose(2, 0, 1),
        "w1k_2": a["cmp_k_w1_2"][0].reshape(SLABS, P, CH).transpose(1, 0, 2),
        "w1v_2": a["cmp_v_w1_2"][0].reshape(SLABS, P, CH).transpose(1, 0, 2),
        "w2k_2": a["cmp_k_w2_2"][0].reshape(2, P, HD).transpose(1, 0, 2),
        "w2v_2": a["cmp_v_w2_2"][0].reshape(2, P, HD).transpose(1, 0, 2),
    }
    out.update(shape_constants())
    return {k: np.ascontiguousarray(v) for k, v in out.items()}


def kernel(**inputs):
    import concourse.bacc as bacc
    from concourse.bass_utils import run_bass_kernel_spmd as run

    nc = bacc.Bacc("TRN2", target_bir_lowering=False, num_devices=1)
    arrays = {"in_" + k: v for k, v in lay_out(inputs).items()}
    d = {k[3:]: nc.dram_tensor(k, v.shape, mybir.dt.from_np(v.dtype), kind="ExternalInput").ap()
         for k, v in arrays.items()}
    d["out"] = nc.dram_tensor("out_dram", (P, KT, T), F32, kind="ExternalOutput").ap()
    build(nc, d)
    r = run(nc, [arrays], core_ids=[0])
    y = r.results[0]["out_dram"]
    return np.ascontiguousarray(y.transpose(1, 0, 2).reshape(D, T).T).reshape(1, T, D)
```

```python
from contextlib import ExitStack

import numpy as np

import concourse.bass as bass
from concourse import mybir

F32 = mybir.dt.float32
F32R = mybir.dt.float32r
I32 = mybir.dt.int32
ALU = mybir.AluOpType
ACT = mybir.ActivationFunctionType

P = 128
T = 512
D = 1024
KT = D // P
DEPTH = 2
DFF = 2816
FT = DFF // P
NQ = T // P
HD = 64
EPS = 1e-6
SCALE = HD ** -0.5
NEG = -1e30

POOL_W = 256
PAIRS = 6
WINDOWS = (2, 4, 8, 16)
PAD = 8
POOL_OPS = 4 + 10
NKV = 2
NCMP = (T - 32) // 16 + 1
CH = 256
NGATE = 24
SLABS = 16

U_FFN = 3 * FT
U_PROJ = 2 + 3 * PAIRS
U_OUT = KT
U_LAYER = 2 * U_FFN + U_PROJ + U_OUT
U_PROJ2 = 18
U_BLOCK2 = DEPTH * U_LAYER
U_ALL = U_BLOCK2 + U_PROJ2 + U_OUT + U_FFN
ORDER2 = [4, 5, 6, 7, 12, 13, 14, 16, 15, 17, 8, 9, 10, 11, 0, 1, 2, 3]

HEAD_ORDER = np.r_[0:8, 16:40, 8:16, 40:64]
ROPE_READS = 5
TILES2 = (3, 0, 2, 1)


def shape_constants():
    p = np.arange(P)[:, None]
    c = np.arange(T + 384)[None, :]
    d = c - 384 - p
    count = (np.abs(d) <= 64) * 1 + ((d % 4 == 0) & (np.abs(d) <= 256)) + (d % 16 == 0)
    band = np.where(count > 0, np.log(np.maximum(count, 1)) / SCALE, NEG)
    tri = np.where(c[:, :T] - 384 <= p, 0.0, NEG)
    tq = (np.arange(NQ)[None, :, None] * P + np.arange(P)[:, None, None])
    seen = (16 * np.arange(NCMP)[None, None, :] + 31) <= tq
    pos = np.arange(T)
    inv = np.zeros((P, 2, T))
    for g, w in enumerate(WINDOWS):
        lo = np.maximum(pos - w // 2, 0)
        hi = np.minimum(pos + w - 1 - w // 2, T - 1)
        inv[64 * (g % 2):64 * (g % 2) + 64, g // 2, :] = 1.0 / (hi - lo + 1)
    dim = np.tile(HEAD_ORDER, 2)
    freq = np.where(dim < 16, np.float32(500000.0) ** (-(2 * (dim % 8)).astype(np.float32) / np.float32(16)), 0.0)
    cols = np.stack([freq, dim < 16, dim >= 16, (dim < 8) * 1.0 - ((dim >= 8) & (dim < 16))], 1)
    out = {
        "c_band": band, "c_tri": tri, "c_cmpbias": np.where(seen, 0.0, NEG), "c_cmpseen": seen,
        "c_ident": np.eye(P), "c_ones": np.ones((P, P)), "c_invcount": inv,
        "c_causal": p <= np.arange(P)[None, :], "c_rope": cols,
    }
    return {k: np.ascontiguousarray(v.astype(np.float32)) for k, v in out.items()}


def build(nc, d):
    ctx = ExitStack()
    with ctx:
        def sem(name):
            return ctx.enter_context(nc.semaphore(name))

        def sb(name, shape, dt=F32, at=ctx):
            return at.enter_context(nc.sbuf_tensor(name, shape, dt))

        parts = ExitStack()
        xh = sb("xh", [P, KT, T], F32R, at=parts)
        xl = sb("xl", [P, KT, T], F32R, at=parts)
        parts.close()
        sc2 = sb("sc2", [P, 4, 2, T])
        pt2 = sb("pt2", [P, 2, 2, T])
        kst = sb("kst", [P, 2, T])
        vst = sb("vst", [P, 2, NQ, HD])
        parts_rest = sb("parts_rest", [P, T])
        x = sb("x", [P, KT, T])
        raw = sb("raw", [P, 2, 2, 8 * P])
        wh = sb("wh", [P, 2, 8, P], F32R)
        wl = sb("wl", [P, 2, 8, P], F32R)
        sq = sb("sq", [P, 2, T])
        rstd = sb("rstd", [P, T])
        ident = sb("ident", [P, P])
        ones = sb("ones", [P, P])
        gains = sb("gains", [P, DEPTH, 3, KT])
        gains2 = sb("gains2", [P, 4, KT])
        gain = sb("gain", [P, 3, KT])

        block1 = ExitStack()
        cos = sb("cos", [P, T], at=block1)
        sin = sb("sin", [P, T], at=block1)
        band = sb("band", [P, T + 384], at=block1)
        invcount = sb("invcount", [P, 2, T], at=block1)
        ropecol = sb("ropecol", [P, 4], at=block1)
        poolw = sb("poolw", [P, DEPTH, 2, HD], at=block1)
        poolscale = sb("poolscale", [P, DEPTH, 2], at=block1)
        poolw_now = sb("poolw_now", [P, 2, HD], at=block1)
        poolscale_now = sb("poolscale_now", [P, 2], at=block1)

        mix1 = ExitStack()
        posi = sb("posi", [P, T], I32, at=mix1)
        cosr = sb("cosr", [P, T], at=mix1)
        sinr = sb("sinr", [P, T], at=mix1)
        mh1 = sb("mh1", [P, KT, T], F32R, at=mix1)
        ml1 = sb("ml1", [P, KT, T], F32R, at=mix1)
        vraw = sb("vraw", [P, T], at=mix1)
        qk = sb("qk", [P, 2, T], at=mix1)
        qs = sb("qs", [P, 2, 2, T], F32R, at=mix1)
        ks = sb("ks", [P, 2, 2, T], F32R, at=mix1)
        kl = sb("kl", [P, 2, T], F32R, at=mix1)
        vtok = sb("vtok", [P, 2, NQ, P], at=mix1)
        sc = sb("sc", [P, 4, T], at=mix1)
        pt = sb("pt", [P, 2, T], at=mix1)
        otok = sb("otok", [P, 8, HD], at=mix1)
        ropet = sb("ropet", [P, 2, T], at=mix1)
        padded = sb("padded", [P, 2, PAD + T + PAD], at=mix1)
        win = sb("win", [P, 2, PAD + T + PAD], at=mix1)
        win16 = sb("win16", [P, PAD + T + PAD], at=mix1)
        smax = sb("smax", [P, 8], at=mix1)
        sneg = sb("sneg", [P, 8], at=mix1)
        sden = sb("sden", [P, 8], at=mix1)
        srec = sb("srec", [P, 8], at=mix1)
        mix1.close()

        ffn = ExitStack()
        acth = sb("acth", [P, FT, T], F32R, at=ffn)
        actl = sb("actl", [P, FT, T], F32R, at=ffn)
        gn = sb("gn", [P, 2, T], at=ffn)
        un = sb("un", [P, 2, T], at=ffn)
        ffn.close()
        block1.close()

        mix2 = ExitStack()
        gu = sb("gu", [P, 4, T], at=mix2)
        bsb = sb("bsb", [P, 4, P], at=mix2)
        causal = sb("causal", [P, P], at=mix2)
        tri = sb("tri", [P, T], at=mix2)
        cmpbias = sb("cmpbias", [P, NQ, NCMP], at=mix2)
        cmpseen = sb("cmpseen", [P, NQ, NCMP], at=mix2)
        wg = sb("wg", [P, KT, NGATE], at=mix2)
        wgh = sb("wgh", [P, KT, NGATE], F32R, at=mix2)
        wgl = sb("wgl", [P, KT, NGATE], F32R, at=mix2)
        gateb = sb("gateb", [P, NGATE], at=mix2)
        gates = sb("gates", [P, NQ, NGATE], at=mix2)
        rcol = sb("rcol", [P, NQ], at=mix2)
        vec2 = sb("vec2", [P, 3, 4], at=mix2)
        poscol = sb("poscol", [P, 2, SLABS], at=mix2)
        w2k = sb("w2k", [P, 2, P], at=mix2)
        w2v = sb("w2v", [P, 2, HD], at=mix2)
        kdup = sb("kdup", [P, 2, NKV, T], at=mix2)
        vall = sb("vall", [P, 2, NQ, P], at=mix2)
        qall = sb("qall", [P, 4, T], at=mix2)
        oall = sb("oall", [P, 4, T], at=mix2)
        kcall = sb("kcall", [P, NKV, NCMP], at=mix2)
        vcall = sb("vcall", [P, NKV, HD], at=mix2)
        rstd2 = sb("rstd2", [P, T], at=mix2)

        comp = ExitStack()
        gv = sb("gv", [P, 4, T], at=comp)
        gvtok = sb("gvtok", [P, 4, NQ, P], at=comp)
        wst = sb("wst", [P, 8, P], at=comp)
        vs2 = sb("vs2", [P, 2, T], at=comp)

        def svt(t):
            return vs2[:, t % 2, :].rearrange("p (c n) -> p c n", c=NQ)
        w1 = sb("w1", [P, SLABS, CH], at=comp)
        shifted = sb("shifted", [P, NKV, T], at=comp)
        blk = sb("blk", [P, 2, SLABS, NKV * NCMP], at=comp)
        hid = sb("hid", [P, 2, 2, NKV * NCMP], at=comp)
        comp.close()
        attn2 = ExitStack()
        mh2 = sb("mh2", [P, KT, T], F32R, at=attn2)
        ml2 = sb("ml2", [P, KT, T], F32R, at=attn2)
        qs2 = sb("qs2", [P, 4, T], F32R, at=attn2)
        kh2 = sb("kh2", [P, 2, T], F32R, at=attn2)
        kl2 = sb("kl2", [P, 2, T], F32R, at=attn2)
        qst = sb("qst", [P, 2, T], at=attn2)
        kcst = sb("kcst", [P, NCMP], at=attn2)
        vcst = sb("vcst", [P, HD], at=attn2)
        gst = sb("gst", [P, NQ, 3, 4], at=attn2)
        scc = sb("scc", [P, NQ, NCMP], at=attn2)
        ptc = sb("ptc", [P, 2, T], at=attn2)
        smax2 = sb("smax2", [P, 2, 2], at=attn2)
        sneg2 = sb("sneg2", [P, 2, 2], at=attn2)
        sden2 = sb("sden2", [P, 2, 2], at=attn2)
        srec2 = sb("srec2", [P, 2, 2], at=attn2)
        coef2 = sb("coef2", [P, 2, 2], at=attn2)
        cmax = sb("cmax", [P, NQ], at=attn2)
        cden = sb("cden", [P, NQ], at=attn2)
        attn2.close()
        mix2.close()

        B = [ctx.enter_context(nc.psum_tensor(f"bank{i}", [P, T], F32)) for i in range(8)]

        raw_in = [sem("raw_in0"), sem("raw_in1")]
        x_in = sem("x_in")
        const_in = sem("const_in")
        const2_in = sem("const2_in")
        pos_in = sem("pos_in")
        w1k_in = sem("w1k_in")
        w1v_in = sem("w1v_in")
        out_done = sem("out_done")
        split_begun = sem("split_begun")
        hi_split = sem("hi_split")
        split_done = sem("split_done")
        unit_used = sem("unit_used")
        x_done = sem("x_done")
        sq_done = sem("sq_done")
        ss_done = sem("ss_done")
        xh_done = sem("xh_done")
        xl_done = sem("xl_done")
        mean_done = sem("mean_done")
        root_done = sem("root_done")
        rstd_done = sem("rstd_done")
        layer_set = sem("layer_set")
        gu_evac = sem("gu_evac")
        silu_done = sem("silu_done")
        act_part = sem("act_part")
        act_done = sem("act_done")
        acc_done = sem("acc_done")
        trig = sem("trig")
        trig_act = sem("trig_act")
        tables_done = sem("tables_done")
        pool_step = sem("pool_step")
        pool_evac = sem("pool_evac")
        proj_read = sem("proj_read")
        qk_hi = sem("qk_hi")
        qk_lo = sem("qk_lo")
        v_evac = sem("v_evac")
        rope_a = sem("rope_a")
        rope_done = sem("rope_done")
        vt_done = sem("vt_done")
        vtok_done = sem("vtok_done")
        s_done = sem("s_done")
        dve_turn = sem("dve_turn")
        t_done = sem("t_done")
        neg_done = sem("neg_done")
        exp_done = sem("exp_done")
        rec_done = sem("rec_done")
        otok_done = sem("otok_done")
        ot_done = sem("ot_done")
        tr_done = sem("tr_done")
        pte_done = sem("pte_done")
        pv_done = sem("pv_done")
        poolmm_done = sem("poolmm_done")
        out_turn = sem("out_turn")
        pe_turn = sem("pe_turn")
        mh_done = sem("mh_done")
        ml_done = sem("ml_done")
        evac2 = sem("evac2")
        half2 = sem("half2")
        gelu_in = sem("gelu_in")
        gelu_done = sem("gelu_done")
        sq2_done = sem("sq2_done")
        ss2_done = sem("ss2_done")
        mean2 = sem("mean2")
        root2 = sem("root2")
        rstd2_done = sem("rstd2_done")
        wg_part = sem("wg_part")
        wg_done = sem("wg_done")
        gate_mm = sem("gate_mm")
        gate_a = sem("gate_a")
        gate_b = sem("gate_b")
        gates_done = sem("gates_done")
        rc_mm = sem("rc_mm")
        rcol_done = sem("rcol_done")
        shift_done = sem("shift_done")
        blk_done = sem("blk_done")
        hid_mm = sem("hid_mm")
        hid_done = sem("hid_done")
        cmp_mm = sem("cmp_mm")
        cmp_done = sem("cmp_done")
        v2_mm = sem("v2_mm")
        v2_done = sem("v2_done")
        vn_done = sem("vn_done")
        gt_mm = sem("gt_mm")
        gt_done = sem("gt_done")
        ws_done = sem("ws_done")
        sv_mm = sem("sv_mm")
        sv_add = sem("sv_add")
        a_done = sem("a_done")
        norm_mul = sem("norm_mul")
        mh2_done = sem("mh2_done")
        ml2_done = sem("ml2_done")
        stage_open = sem("stage_open")
        staged = sem("staged")
        s2_done = sem("s2_done")
        turn2 = sem("turn2")
        t2_done = sem("t2_done")
        neg2_done = sem("neg2_done")
        exp2_done = sem("exp2_done")
        rec2_done = sem("rec2_done")
        coef2_done = sem("coef2_done")
        p2_done = sem("p2_done")
        cs_done = sem("cs_done")
        ct_step = sem("ct_step")
        ct_done = sem("ct_done")
        ce_done = sem("ce_done")
        cn_step = sem("cn_step")
        cp_done = sem("cp_done")
        ctr_done = sem("ctr_done")
        cpt_done = sem("cpt_done")
        tr2_done = sem("tr2_done")
        pte2_done = sem("pte2_done")
        pv2_done = sem("pv2_done")
        hi2_done = sem("hi2_done")
        lo2_done = sem("lo2_done")
        o2_done = sem("o2_done")
        fin_done = sem("fin_done")

        N_CONST = 9
        N_CONST2 = 14
        STAGED = 9
        LAYER_COPIES = 3

        block = ctx.enter_context(nc.Block())

        @block.sync
        def _(sp):
            sp.dma_start(x[:, :, :], d["x"]).then_inc(x_in, 16)
            for dst, name in ((ident, "c_ident"), (ones, "c_ones"), (band, "c_band"),
                              (invcount, "c_invcount"), (ropecol, "c_rope"), (poolw, "poolw"),
                              (poolscale, "poolscale"), (gains, "gains"), (gains2, "gains2")):
                sp.dma_start(dst[tuple([slice(None)] * len(dst.shape))], d[name]).then_inc(const_in, 16)

            def load_pair(pair, e, first):
                if not first:
                    sp.wait_ge(split_done, pair * 2 - 2)
                sp.dma_start(raw[:, e, :, :], d["stream"][pair]).then_inc(raw_in[e], 16)

            for e in range(2):
                load_pair(e, e, True)
            sp.dma_start(posi[:, :], d["positions"].to_broadcast([P, T])).then_inc(pos_in, 16)
            with sp.Fori(1, U_BLOCK2 // 4 + 1) as i:
                for e in range(2):
                    load_pair(i * 2 + e, e, False)

            sp.wait_ge(x_done, 8 * 8)
            for dst, name in ((wst, "ws_2"), (causal, "c_causal"), (tri, "c_tri"), (cmpbias, "c_cmpbias"),
                              (cmpseen, "c_cmpseen"), (wg, "wg_2"), (gateb, "gate_b_2"), (vec2, "vec_2"),
                              (poscol, "pos_2"), (w2v, "w2v_2")):
                sp.dma_start(dst[tuple([slice(None)] * len(dst.shape))], d[name]).then_inc(const2_in, 16)
            for half in range(2):
                sp.dma_start(w2k[:, :, HD * half:HD * half + HD], d["w2k_2"]).then_inc(const2_in, 16)
                sp.dma_start(bsb[HD * half:HD * half + HD, :, :],
                             d["bs_2"][half:half + 1].to_broadcast([HD, 4, P])).then_inc(const2_in, 16)
            sp.dma_start(w1[:, :, :], d["w1k_2"]).then_inc(w1k_in, 16)

            with sp.Fori(U_BLOCK2 // 4 + 1, U_BLOCK2 // 4 + 5) as i:
                for e in range(2):
                    load_pair(i * 2 + e, e, False)
            sp.wait_ge(hid_mm, 1)
            sp.dma_start(w1[:, :, :], d["w1v_2"]).then_inc(w1v_in, 16)
            with sp.Fori(U_BLOCK2 // 4 + 5, U_ALL // 4) as i:
                for e in range(2):
                    load_pair(i * 2 + e, e, False)
            sp.wait_ge(fin_done, KT)
            sp.dma_start(d["out"], x[:, :, :]).then_inc(out_done, 16)
            sp.wait_ge(out_done, 16)

        @block.gpsimd
        def _(pool):
            with pool.Fori(0, U_ALL // 4) as i:
                for e in range(2):
                    for h in range(2):
                        u = i * 4 + (2 * e + h)
                        if h == 0:
                            pool.wait_ge(raw_in[e], i * 16 + 16)
                        pool.wait_ge(unit_used, u + 1)
                        nc.gpsimd.nop().then_inc(split_begun, 1)
                        src = raw[:, e, h, :].rearrange("p (k n) -> p k n", k=8)
                        nc.gpsimd.tensor_scalar(wh[:, h, :, :], src, 1.0, 1.0, ALU.mult, ALU.mult)\
                            .then_inc(hi_split, 1)
                        pool.wait_ge(hi_split, u + 1)
                        nc.gpsimd.tensor_tensor(wl[:, h, :, :], src, wh[:, h, :, :].bitcast(F32),
                                                ALU.subtract).then_inc(split_done, 1)

        @block.tensor
        def _(pe):
            pe.nop().then_inc(unit_used, 2)
            pe.nop().then_inc(ss_done, 2)
            pe.nop().then_inc(tr_done, 4)
            pe.nop().then_inc(pv_done, 2)
            pe.nop().then_inc(tr2_done, 4)
            pe.nop().then_inc(pv2_done, 2)
            pe.nop().then_inc(ctr_done, 1)
            pe.wait_ge(const_in, 16 * N_CONST)

            def split_product(bank, slot, k, rh, rl, start, stop):
                mm = nc.tensor.matmul(bank, wh[:, slot, k, :], rh, start=start, stop=False)
                mm = nc.tensor.matmul(bank, wh[:, slot, k, :], rl, start=False, stop=False)
                return nc.tensor.matmul(bank, wl[:, slot, k, :], rh, start=False, stop=stop)

            def square_sum(prep, m, bank):
                pe.wait_ge(sq_done, prep * 8 + (m + 1))
                nc.tensor.matmul(bank[:, :], ones[:, :], sq[:, m % 2, :], start=(m == 0), stop=(m == KT - 1))\
                    .then_inc(ss_done, 1)

            def first_unit(prep, ready, u, slot):
                for m in range(5):
                    square_sum(prep, m, B[0])
                pe.wait_ge(split_done, u + 1)
                for k in range(KT):
                    if k + 5 < KT:
                        square_sum(prep, k + 5, B[0])
                    pe.wait_ge(xl_done, ready * 8 + (k + 1))
                    mm = split_product(B[4][:, :], slot, k, xh[:, k, :], xl[:, k, :], k == 0, k == KT - 1)
                mm.then_inc(unit_used, 1)

            def unit_blocks(u, slot, bank, ks, hi=xh, lo=xl):
                for k in ks:
                    if k == 0:
                        pe.wait_ge(split_done, u + 1)
                    mm = split_product(bank[:, :], slot, k, hi[:, k, :], lo[:, k, :], k == 0, k == KT - 1)
                if ks[-1] == KT - 1:
                    mm.then_inc(unit_used, 1)

            def feed_forward(n, prep, ready, u0):
                first_unit(prep, ready, u0, 0)
                for j in range(1, 4):
                    unit_blocks(u0 + j, j % 2, B[4 + j], range(KT))
                with pe.Fori(1, FT // 2) as i:
                    for j in range(4):
                        pe.wait_ge(gu_evac, i * 4 + (n * 2 * FT + (j - 3)))
                        unit_blocks(i * 4 + (u0 + j), j % 2, B[4 + j], range(KT))

                def down(f, f0, at, first, last):
                    h, lo = acth[:, at, :], actl[:, at, :]
                    if not isinstance(at, int):
                        h, lo = h.rearrange("p a t -> p (a t)"), lo.rearrange("p a t -> p (a t)")
                    pe.wait_ge(act_done, f + 1 + n * FT)
                    pe.wait_ge(split_done, f + 1 + (u0 + 2 * FT))
                    for m in range(KT):
                        if first and m == 4:
                            pe.wait_ge(gu_evac, (n + 1) * (2 * FT))
                        mm = split_product(B[m][:, :], f0 % 2, m, h, lo, first, last)
                        if last and m < KT - 1:
                            mm.then_inc(acc_done, 1)
                    mm.then_inc(unit_used, 1)

                down(0, 0, 0, True, False)
                down(1, 1, 1, False, False)
                with pe.Fori(1, FT // 2 - 1) as i:
                    for e in range(2):
                        down(i * 2 + e, e, bass.ds(i * 2 + e, 1), False, False)
                down(FT - 2, 0, FT - 2, False, False)
                down(FT - 1, 1, FT - 1, False, True)

            def mixer1(l):
                u0 = l * U_LAYER + U_FFN
                first_unit(l * 3 + 1, l * 3 + 1, u0, 0)
                unit_blocks(u0 + 1, 1, B[5], range(KT))

                for n in range(2, 5):
                    pe.wait_ge(proj_read, l * U_PROJ + (n - 1))
                    unit_blocks(u0 + n, n % 2, B[4 + n % 2], range(KT))

                def turn_back(pair):
                    pe.wait_ge(otok_done, pair + 2)
                    for i in range(NQ):
                        tr = nc.tensor.transpose(B[6][:, i * P:(i + 1) * P],
                                                 otok[:, 2 * i:2 * i + 2, :].rearrange("p h d -> p (h d)"), ident[:, :])
                    tr.then_inc(ot_done, 1)

                def pair_steps(j, e, more):
                    pair = l * PAIRS + j
                    step0 = pair * 8
                    u = u0 + 5 + j * 3
                    slot = (1 + e) % 2
                    work = [(n, k) for n in range(3) for k in range(KT)] if more else []

                    def fill(count):
                        for n, k in [work.pop(0) for _ in range(count if more else 0)]:
                            if k == 0:
                                pe.wait_ge(proj_read, l * U_PROJ + j * 3 + (4 + n))
                            unit_blocks(u + n, (slot + n) % 2, B[4 + (slot + n) % 2], [k])

                    def scores(s):
                        a, i = s // 4, P * (s % 4)
                        h = HD * a
                        if s == 0:
                            pe.wait_ge(qk_lo, pair * 4 + 4)
                        pe.wait_ge(t_done, step0 + (s + 1))
                        nc.tensor.matmul(B[1 + s % 2][:, :], qs[:, e, a, i:i + P], ks[:, e, a, :],
                                         start=True, stop=False)
                        nc.tensor.matmul(B[1 + s % 2][:, :], qs[h:h + HD, e, a, i:i + P], kl[h:h + HD, e, :],
                                         start=False, stop=True).then_inc(s_done, 1)

                    def turn(s):
                        pe.wait_ge(exp_done, step0 + (s + 1))
                        pe.wait_ge(pte_done, step0 + (s + 1))
                        for kt in range(NQ):
                            tr = nc.tensor.transpose(B[(3, 0)[s % 2]][:, kt * P:(kt + 1) * P],
                                                     sc[:, s % 4, kt * P:(kt + 1) * P], ident[:, :])
                        tr.then_inc(tr_done, 1)

                    def values(s):
                        a, i = s // 4, s % 4
                        if s == 0:
                            pe.wait_ge(vtok_done, pair + 1)
                            pe.wait_ge(otok_done, pair + 1)
                        pe.wait_ge(pte_done, step0 + (s + 3))
                        c = HD * (2 * i + a)
                        for kt in range(NQ):
                            mm = nc.tensor.matmul(B[7][:, c:c + HD], pt[:, s % 2, kt * P:(kt + 1) * P],
                                                  vtok[:, e, kt, HD * a:HD * (a + 1)],
                                                  start=(kt == 0), stop=(kt == NQ - 1))
                        mm.then_inc(pv_done, 1)

                    for s in range(8):
                        scores(s)
                        fill((3, 3, 3, 2, 2, 2, 1, 1)[s])
                        if s == 1:
                            pe.wait_ge(v_evac, pair + 1)
                            pe.wait_ge(ml_done, l * 8 + j + 1)
                            for kt in range(NQ):
                                tr = nc.tensor.transpose(B[6][:, kt * P:(kt + 1) * P],
                                                         vraw[:, kt * P:(kt + 1) * P], ident[:, :])
                            tr.then_inc(vt_done, 1)
                        if s in (2, 4) and not more:
                            t = s // 2 - 1
                            pe.wait_ge(pool_step, (l + 1) * POOL_OPS)
                            pe.wait_ge(proj_read, (l + 1) * U_PROJ)
                            pe.nop().then_inc(pe_turn, 1)
                            for h in (0, HD):
                                mm = nc.tensor.matmul(B[4 + t][h:h + HD, :], poolw_now[h:h + HD, t, :],
                                                      padded[h:h + HD, t, PAD:PAD + T], start=True, stop=True)
                            mm.then_inc(poolmm_done, 1)
                        if s >= 2:
                            turn(s - 2)
                        if s >= 3:
                            values(s - 3)
                    fill(2)
                    turn(6)
                    values(5)
                    fill(2)
                    turn(7)
                    values(6)
                    fill(1)
                    values(7)
                    fill(2)
                    if more:
                        turn_back(pair)

                with pe.Fori(0, 2) as it:
                    for e in range(2):
                        pair_steps(it * 2 + e, e, True)
                pair_steps(4, 0, True)
                pair_steps(5, 1, False)

                def out_blocks(m, ks_):
                    unit_blocks(u0 + (U_PROJ + m), m % 2, B[m], ks_, mh1, ml1)

                pe.wait_ge(ml_done, l * 8 + 8)
                out_blocks(0, range(KT - 1))
                turn_back(l * PAIRS + 5)
                out_blocks(1, range(KT - 1))
                pe.wait_ge(ml_done, l * 8 + 9)
                out_blocks(0, [KT - 1])
                out_blocks(1, [KT - 1])
                for m in range(2, KT):
                    out_blocks(m, range(KT))

            with pe.Fori(0, DEPTH) as l:
                feed_forward(l * 2, l * 3, l * 3, l * U_LAYER)
                mixer1(l)
                feed_forward(l * 2 + 1, l * 3 + 2, l * 3 + 2, l * U_LAYER + (U_FFN + U_PROJ + U_OUT))

            for m in range(KT):
                square_sum(6, m, B[0])
            u0 = U_BLOCK2
            first_unit(7, 6, u0, 0)
            unit_blocks(u0 + 1, 1, B[5], range(KT))
            with pe.Fori(0, 4) as i:
                for j in range(4):
                    pe.wait_ge(evac2, i * 4 + (j + 1))
                    unit_blocks(i * 4 + (u0 + 2 + j), j % 2, B[4 + (2 + j) % 4], range(KT))

            pe.wait_ge(wg_done, 1)
            for i in range(NQ):
                for k in range(KT):
                    a, b = xh[:, k, i * P:(i + 1) * P], xl[:, k, i * P:(i + 1) * P]
                    o = B[0][:, NGATE * i:NGATE * (i + 1)]
                    nc.tensor.matmul(o, a, wgh[:, k, :], start=(k == 0), stop=False)
                    nc.tensor.matmul(o, a, wgl[:, k, :], start=False, stop=False)
                    mm = nc.tensor.matmul(o, b, wgh[:, k, :], start=False, stop=(k == KT - 1))
            mm.then_inc(gate_mm, 1)

            def sum_squares2(n, src, bank):
                for t in range(4):
                    pe.wait_ge(sq2_done, 4 * n + t + 1)
                    mm = nc.tensor.matmul(bank[:, :], ones[:, :], src[:, t, :], start=(t == 0), stop=(t == 3))
                mm.then_inc(ss2_done, 1)

            sum_squares2(0, oall, B[1])
            for i in range(NQ):
                tr = nc.tensor.transpose(B[2][:, i * P:(i + 1) * P], rstd[:, i * P:(i + 1) * P], ident[:, :])
            tr.then_inc(rc_mm, 1)

            def hidden(which, bank):
                pe.wait_ge(blk_done, 4 * which + 4)
                pe.wait_ge((w1k_in, w1v_in)[which], 16)
                for m in range(2):
                    for s in range(SLABS):
                        mm = nc.tensor.matmul(bank[:, HD * m:HD * m + NKV * NCMP], w1[:, s, P * m:P * (m + 1)],
                                              blk[:, which, s, :], start=(s == 0), stop=(s == SLABS - 1))
                mm.then_inc(hid_mm, 1)

            hidden(0, B[3])
            pe.wait_ge(evac2, U_PROJ2)
            for n in range(2):
                for kt in range(NQ):
                    tr = nc.tensor.transpose(B[4 + n][:, kt * P:(kt + 1) * P], vs2[:, n, kt * P:(kt + 1) * P],
                                             ident[:, :])
                tr.then_inc(v2_mm, 1)
            pe.wait_ge(rstd2_done, 1)
            hidden(1, B[1])
            pe.wait_ge(hid_done, 1)
            pe.wait_ge(rcol_done, 1)
            for m in range(2):
                mm = nc.tensor.matmul(B[2][:, 0:NKV * NCMP], w2k[:, m, :], hid[:, 0, m, :],
                                      start=(m == 0), stop=(m == 1))
            mm.then_inc(cmp_mm, 1)

            for t in range(4):
                pe.wait_ge(vn_done, t + 1)
                if t >= 2:
                    pe.wait_ge(gt_done, t - 1)
                for c in range(NQ):
                    tr = nc.tensor.transpose(B[6 + t % 2][:, c * P:(c + 1) * P], gv[:, t, c * P:(c + 1) * P],
                                             ident[:, :])
                tr.then_inc(gt_mm, 1)
            pe.wait_ge(hid_done, 2)
            pe.wait_ge(gate_a, 1)
            for kv in range(NKV):
                for m in range(2):
                    mm = nc.tensor.matmul(B[0][0:NCMP, HD * kv:HD * (kv + 1)],
                                          hid[:, 1, m, NCMP * kv:NCMP * (kv + 1)], w2v[:, m, :],
                                          start=(m == 0), stop=(m == 1))
            mm.then_inc(cmp_mm, 1)
            pe.wait_ge(ws_done, 1)
            pe.wait_ge(v2_done, 2)
            for t in range(4):
                pe.wait_ge(gt_done, t + 1)
                if t >= 2:
                    pe.wait_ge(sv_add, t - 1)
                for h in range(2):
                    for c in range(NQ):
                        mm = nc.tensor.matmul(B[4 + t % 2][HD * h:HD * (h + 1), c * P:(c + 1) * P],
                                              gvtok[:, t, c, HD * h:HD * (h + 1)], wst[:, 2 * t + h, :],
                                              start=True, stop=True)
                mm.then_inc(sv_mm, 1)
            sum_squares2(1, oall, B[6])

            def turn2_(g, s):
                i = TILES2[s % 4]
                G = g * 16 + s
                pe.wait_ge(p2_done, G * 2 + 2)
                pe.wait_ge(pte2_done, G * 2 + 2)
                for c, bank in ((0, B[6]), (1, B[0])):
                    for kt in range(i + 1):
                        tr = nc.tensor.transpose(bank[:, kt * P:(kt + 1) * P], sc2[:, s % 4, c, kt * P:(kt + 1) * P],
                                                 ident[:, :])
                tr.then_inc(tr2_done, 1)

            def compressed_scores(g, hh):
                h = HD * (hh % 2)
                pe.wait_ge(cpt_done, g * 4 + (hh + 1))
                for i in range(NQ):
                    mm = nc.tensor.matmul(B[5][:, NCMP * i:NCMP * (i + 1)], qst[h:h + HD, hh // 2, i * P:(i + 1) * P],
                                          kcst[h:h + HD, :], start=True, stop=True)
                mm.then_inc(cs_done, 1)

            def compressed_turn(g, hh):
                pe.wait_ge(cp_done, g * 4 + (hh + 1))
                for i in range(NQ):
                    tr = nc.tensor.transpose(B[5][0:NCMP, i * P:(i + 1) * P], scc[:, i, :], ident[:, :])
                tr.then_inc(ctr_done, 1)

            def values2(g, s):
                hh, i = s // 4, TILES2[s % 4]
                h = HD * (hh % 2)
                G = g * 16 + s
                if s % 8 == 0:
                    pe.wait_ge(o2_done, g * 2 + (s // 8 + 1))
                if s % 4 == 0:
                    pe.wait_ge(cpt_done, g * 4 + (hh + 2))
                pe.wait_ge(pte2_done, G * 2 + 4)
                o = B[7][h:h + HD, i * P:(i + 1) * P]
                for c in range(2):
                    for kt in range(i + 1):
                        nc.tensor.matmul(o, vst[:, c, kt, :], pt2[:, s % 2, c, kt * P:(kt + 1) * P],
                                         start=(c == 0 and kt == 0), stop=False)
                nc.tensor.matmul(o, vcst[0:NCMP, :], ptc[0:NCMP, hh % 2, i * P:(i + 1) * P],
                                 start=False, stop=True).then_inc(pv2_done, 1)

            with pe.Fori(0, NKV) as g:
                pe.wait_ge(staged, (g + 1) * STAGED)
                compressed_scores(g, 0)
                pe.wait_ge(lo2_done, (g + 1) * 6)
                for s in range(16):
                    hh, i, par = s // 4, TILES2[s % 4], s % 2
                    h = HD * (hh % 2)
                    n = P * (i + 1)
                    pe.wait_ge(t2_done, g * 32 + (2 * s + 2))
                    for c in range(2):
                        o = B[1 + 2 * c + par][:, 0:n]
                        nc.tensor.matmul(o, qs2[:, hh, i * P:(i + 1) * P], kh2[:, c, 0:n], start=True, stop=False)
                        mm = nc.tensor.matmul(o, qs2[h:h + HD, hh, i * P:(i + 1) * P], kl2[h:h + HD, c, 0:n],
                                              start=False, stop=True)
                    mm.then_inc(s2_done, 1)
                    if s == 1:
                        compressed_turn(g, 0)
                    if s % 4 == 0 and 0 < s:
                        compressed_scores(g, s // 4)
                    if s >= 2:
                        turn2_(g, s - 2)
                    if s >= 3:
                        values2(g, s - 3)
                    if s % 4 == 2 and s > 4:
                        compressed_turn(g, s // 4)
                turn2_(g, 14)
                values2(g, 13)
                turn2_(g, 15)
                values2(g, 14)
                values2(g, 15)
            sum_squares2(2, gu, B[1])
            pe.wait_ge(ml2_done, 8)
            for m in range(KT):
                unit_blocks(u0 + (U_PROJ2 + m), m % 2, B[m], range(KT), mh2, ml2)
            feed_forward(4, 8, 7, u0 + (U_PROJ2 + U_OUT))
            for m in range(KT):
                square_sum(9, m, B[0])

        @block.scalar
        def _(act):
            act.nop().then_inc(pte_done, 2)
            act.nop().then_inc(pte2_done, 2)
            act.nop().then_inc(cpt_done, 1)

            def squares(prep, m):
                act.wait_ge(x_done, prep * 8 + (m + 1))
                act.wait_ge(ss_done, prep * 8 + (m + 1))
                nc.scalar.activation(sq[:, m % 2, :], x[:, m, :], ACT.Square).then_inc(sq_done, 1)

            def root(prep):
                act.wait_ge(mean_done, prep + 1)
                nc.scalar.activation(rstd[:, :], rstd[:, :], ACT.Sqrt).then_inc(root_done, 1)

            def prepare(prep, gains_of):
                for m in range(KT):
                    squares(prep, m)
                    nc.scalar.activation(xh[:, m, :], x[:, m, :], ACT.Identity, scale=gains_of(m))\
                        .then_inc(xh_done, 1)
                root(prep)

            def feed_forward(n):
                with act.Fori(0, FT // 2) as i:
                    for e in range(2):
                        act.wait_ge(gu_evac, i * 4 + (n * 2 * FT + (2 * e + 1)))
                        nc.scalar.activation(gn[:, e, :], gn[:, e, :], ACT.Silu).then_inc(silu_done, 1)

            def high_q(pair, e):
                act.wait_ge(rope_done, pair * 2 + 1)
                for a in range(2):
                    r = slice(HD * a, HD * (a + 1))
                    nc.scalar.activation(qs[r, e, a, :], qk[r, 0, :], ACT.Copy).then_inc(qk_hi, 1)

            def high_k(pair, e):
                act.wait_ge(rope_done, pair * 2 + 2)
                for a in range(2):
                    for b in (a, 1 - a):
                        nc.scalar.activation(ks[HD * b:HD * (b + 1), e, a, :], qk[HD * a:HD * (a + 1), 1, :], ACT.Copy)\
                            .then_inc(qk_hi, 1)

            def mixer1(l):
                high_q(l * PAIRS, 0)
                high_k(l * PAIRS, 0)

                def pair_steps(j, e, more):
                    pair = l * PAIRS + j
                    step0 = pair * 8

                    def copy_turn(s):
                        act.wait_ge(tr_done, step0 + (s + 5))
                        act.wait_ge(pv_done, step0 + (s + 1))
                        nc.scalar.activation(pt[:, s % 2, :], B[(3, 0)[s % 2]][:, :], ACT.Copy).then_inc(pte_done, 1)

                    for s in range(8):
                        act.wait_ge(neg_done, step0 + (s + 1))
                        c = 2 * (s % 4) + s // 4
                        nc.scalar.activation(sc[:, s % 4, :], sc[:, s % 4, :], ACT.Exp, bias=sneg[:, s:s + 1],
                                             scale=SCALE, accum_out=sden[:, c:c + 1]).then_inc(exp_done, 1)
                        if s == 2:
                            act.wait_ge(vt_done, pair + 1)
                            nc.scalar.activation(vtok[:, e, :, :], B[6][:, :].rearrange("p (k n) -> p k n", k=NQ),
                                                 ACT.Copy).then_inc(vtok_done, 1)
                        if s >= 2:
                            copy_turn(s - 2)
                        if s == 4 and more:
                            high_q(pair + 1, 1 - e)
                        if s in (3, 5) and not more:
                            t = (s - 3) // 2
                            act.wait_ge(poolmm_done, l * 2 + (t + 1))
                            nc.scalar.activation(mh1[:, t, :], B[4 + t][:, :], ACT.Identity,
                                                 scale=poolscale_now[:, t:t + 1]).then_inc(mh_done, 1)
                    copy_turn(6)
                    if more:
                        high_k(pair + 1, 1 - e)
                    copy_turn(7)
                    act.wait_ge(ot_done, pair + 1)

                with act.Fori(0, 2) as it:
                    for e in range(2):
                        pair_steps(it * 2 + e, e, True)
                        act.nop().then_inc(out_turn, 1)
                        nc.scalar.activation(mh1[:, bass.ds(it * 2 + (2 + e), 1), :].rearrange("p a t -> p (a t)"),
                                             B[6][:, :], ACT.Copy).then_inc(mh_done, 1)
                for j in (4, 5):
                    pair_steps(j, j % 2, j == 4)
                    nc.scalar.activation(mh1[:, 2 + j, :], B[6][:, :], ACT.Copy).then_inc(mh_done, 1)

            act.wait_ge(trig, 4)
            nc.scalar.activation(sin[:, :], sin[:, :], ACT.Sin).then_inc(trig_act, 1)
            act.wait_ge(trig, 7)
            nc.scalar.activation(cos[:, :], cos[:, :], ACT.Sin).then_inc(trig_act, 1)

            with act.Fori(0, DEPTH) as l:
                act.wait_ge(layer_set, (l + 1) * LAYER_COPIES)
                prepare(l * 3, lambda m: gain[:, 0, m:m + 1])
                feed_forward(l * 2)
                prepare(l * 3 + 1, lambda m: gain[:, 1, m:m + 1])
                mixer1(l)
                prepare(l * 3 + 2, lambda m: gain[:, 2, m:m + 1])
                feed_forward(l * 2 + 1)

            for m in range(KT):
                squares(6, m)
            root(6)
            prepare(7, lambda m: gains2[:, 1, m:m + 1])

            def gelu(n, buf):
                act.wait_ge(gelu_in, n + 1)
                nc.scalar.activation(buf, buf, ACT.Gelu_apprx_tanh).then_inc(gelu_done, 1)

            for t in range(4):
                gelu(t, gv[:, t, :])
            for t in range(4):
                act.wait_ge(gelu_done, t + 1)
                nc.scalar.activation(oall[:, t, :], gv[:, t, :], ACT.Square).then_inc(sq2_done, 1)
            for t in range(4):
                gelu(4 + t, gu[:, t, :])

            def root_of(n):
                act.wait_ge(mean2, n + 1)
                nc.scalar.activation(rstd2[:, :], rstd2[:, :], ACT.Sqrt).then_inc(root2, 1)

            def hidden(which, bank):
                act.wait_ge(hid_mm, which + 1)
                nc.scalar.activation(hid[:, which, :, :],
                                     bank[:, 0:2 * HD].rearrange("p (m n) -> p m n", m=2)[:, :, 0:NKV * NCMP],
                                     ACT.Gelu_apprx_tanh).then_inc(hid_done, 1)

            root_of(0)
            hidden(0, B[3])
            for n in range(2):
                act.wait_ge(v2_mm, n + 1)
                nc.scalar.activation(vall[:, n, :, :], B[4 + n][:, :].rearrange("p (k n) -> p k n", k=NQ), ACT.Copy)\
                    .then_inc(v2_done, 1)
            hidden(1, B[1])
            for t in range(4):
                act.wait_ge(gt_mm, t + 1)
                nc.scalar.activation(gvtok[:, t, :, :], B[6 + t % 2][:, :].rearrange("p (c n) -> p c n", c=NQ),
                                     ACT.Copy).then_inc(gt_done, 1)
            act.wait_ge(gate_b, 1)
            nc.scalar.activation(gates[:, :, :], gates[:, :, :], ACT.Sigmoid).then_inc(gates_done, 1)

            def normed(n, src, scratch, base):
                for t in range(4):
                    if n == 1:
                        act.wait_ge(a_done, t + 1)
                    nc.scalar.activation(scratch[:, t, :], src[:, t, :], ACT.Square).then_inc(sq2_done, 1)
                root_of(n)
                for t in range(4):
                    act.wait_ge(norm_mul, 4 * (n - 1) + t + 1)
                    nc.scalar.activation(mh2[:, base + t, :], src[:, t, :], ACT.Copy).then_inc(mh2_done, 1)

            normed(1, gu, oall, 0)

            def copy_turn2(g, s):
                G = g * 16 + s
                n = P * (TILES2[s % 4] + 1)
                act.wait_ge(tr2_done, G + 5)
                act.wait_ge(pv2_done, G + 1)
                for c, bank in ((0, B[6]), (1, B[0])):
                    nc.scalar.activation(pt2[:, s % 2, c, 0:n], bank[:, 0:n], ACT.Copy).then_inc(pte2_done, 1)

            def compressed_exp(g, hh):
                act.wait_ge(ct_done, g * 4 + (hh + 1))
                nc.scalar.activation(scc[:, :, :], scc[:, :, :], ACT.Exp, scale=SCALE).then_inc(ce_done, 1)

            def compressed_copy(g, hh):
                act.wait_ge(ctr_done, g * 4 + (hh + 2))
                if hh >= 2:
                    act.wait_ge(pv2_done, g * 16 + (4 * (hh - 1) + 2))
                nc.scalar.activation(ptc[0:NCMP, hh % 2, :], B[5][0:NCMP, :], ACT.Copy).then_inc(cpt_done, 1)

            with act.Fori(0, NKV) as g:
                act.wait_ge(staged, (g + 1) * STAGED)
                for n in range(2):
                    nc.scalar.activation(kh2[:, n, :], kst[:, n, :], ACT.Copy).then_inc(hi2_done, 1)
                for hd in range(4):
                    r = slice(HD * (hd % 2), HD * (hd % 2 + 1))
                    nc.scalar.activation(qs2[r, hd, :], qst[r, hd // 2, :], ACT.Copy).then_inc(hi2_done, 1)
                compressed_exp(g, 0)
                for s in range(16):
                    n = P * (TILES2[s % 4] + 1)
                    act.wait_ge(neg2_done, g * 16 + (s + 1))
                    for c in range(2):
                        src = sc2[:, s % 4, c, 0:n]
                        nc.scalar.activation(src, src, ACT.Exp, bias=sneg2[:, s % 2, c:c + 1], scale=SCALE,
                                             accum_out=sden2[:, s % 2, c:c + 1]).then_inc(exp2_done, 1)
                    if s == 1:
                        compressed_copy(g, 0)
                    if s % 4 == 1 and s > 4:
                        compressed_exp(g, s // 4)
                    if s % 4 == 3 and s > 4:
                        compressed_copy(g, s // 4)
                    if s >= 2:
                        copy_turn2(g, s - 2)
                copy_turn2(g, 14)
                copy_turn2(g, 15)
            act.wait_ge(o2_done, 5)
            normed(2, oall, gu, 4)
            prepare(8, lambda m: gains2[:, 2, m:m + 1])
            feed_forward(4)
            for m in range(KT):
                squares(9, m)
            root(9)

        @block.vector
        def _(dve):
            V = nc.vector
            dve.nop().then_inc(t_done, 2)
            dve.nop().then_inc(ml_done, 1)
            dve.nop().then_inc(otok_done, 1)
            dve.nop().then_inc(t2_done, 4)
            dve.nop().then_inc(o2_done, 1)
            dve.wait_ge(x_in, 16)
            dve.nop().then_inc(x_done, KT)

            dve.wait_ge(const_in, 16 * N_CONST)
            dve.wait_ge(pos_in, 16)
            TURN = 6.283185307179586
            C1 = 6.28125
            C2 = 2029 / 2 ** 20
            C3 = TURN - C1 - C2
            MAGIC = 12582912.0
            PI = 3.1415925
            a, k = sin, cos
            V.tensor_copy(a[:, :], posi[:, :]).then_inc(trig, 1)
            dve.wait_ge(trig, 1)
            V.tensor_scalar(a[:, :], a[:, :], ropecol[:, 0:1], None, ALU.mult).then_inc(trig, 1)
            dve.wait_ge(trig, 2)
            V.tensor_scalar(k[:, :], a[:, :], 1.0 / TURN, MAGIC, ALU.mult, ALU.add).then_inc(tables_done, 1)
            dve.wait_ge(tables_done, 1)
            V.tensor_scalar(k[:, :], k[:, :], -MAGIC, None, ALU.add).then_inc(tables_done, 1)
            for n, c in enumerate((C1, C2, C3)):
                dve.wait_ge(tables_done, 2 + n)
                V.scalar_tensor_tensor(a[:, :], k[:, :], -c, a[:, :], ALU.mult, ALU.add).then_inc(tables_done, 1)
            dve.wait_ge(tables_done, 5)
            V.tensor_scalar(a[:, :], a[:, :], PI, -PI, ALU.min, ALU.max).then_inc(trig, 1)
            dve.wait_ge(trig, 3)
            V.tensor_scalar(k[:, :], a[:, :], TURN / 4, None, ALU.add).then_inc(trig, 1)
            dve.wait_ge(trig, 4)
            V.tensor_scalar(cosr[:, :], k[:, :], PI, -TURN, ALU.is_gt, ALU.mult).then_inc(trig, 1)
            dve.wait_ge(trig, 5)
            V.tensor_tensor(k[:, :], k[:, :], cosr[:, :], ALU.add).then_inc(trig, 1)
            dve.wait_ge(trig, 6)
            V.tensor_scalar(k[:, :], k[:, :], PI, -PI, ALU.min, ALU.max).then_inc(trig, 1)
            dve.wait_ge(trig_act, 2)
            V.tensor_scalar(cos[:, :], cos[:, :], ropecol[:, 1:2], ropecol[:, 2:3], ALU.mult, ALU.add)\
                .then_inc(tables_done, 1)
            V.tensor_scalar(sin[:, :], sin[:, :], ropecol[:, 3:4], None, ALU.mult).then_inc(tables_done, 1)
            dve.wait_ge(tables_done, 7)

            def inverse_rms(prep):
                dve.wait_ge(ss_done, prep * 8 + 10)
                V.tensor_scalar(rstd[:, :], B[0][:, :], 1.0 / D, EPS, ALU.mult, ALU.add).then_inc(mean_done, 1)
                dve.wait_ge(root_done, prep + 1)
                V.reciprocal(rstd[:, :], rstd[:, :]).then_inc(rstd_done, 1)
                dve.wait_ge(rstd_done, prep + 1)

            def low_part(ready, m, g):
                dve.wait_ge(xh_done, ready * 8 + (m + 1))
                V.scalar_tensor_tensor(xl[:, m, :], x[:, m, :], g, xh[:, m, :].bitcast(F32), ALU.mult, ALU.subtract)\
                    .then_inc(xl_done, 1)

            def update(m, factor, sem_, value):
                dve.wait_ge(sem_, value)
                V.scalar_tensor_tensor(x[:, m, :], B[m][:, :], factor, x[:, m, :], ALU.mult, ALU.add)\
                    .then_inc(x_done, 1)

            def updates(factor, done, ready=None, g=None):
                for m in range(KT):
                    update(m, factor, *done(m))
                    if g is not None and m >= 1:
                        low_part(ready, m - 1, g(m - 1))
                if g is not None:
                    low_part(ready, KT - 1, g(KT - 1))

            def feed_forward(n):
                def evacuate(f, e):
                    if not isinstance(f, int):
                        dve.wait_ge(act_done, f + (n * FT - 1))
                    for j, dst in ((0, gn), (1, un)):
                        dve.wait_ge(unit_used, f * 2 + (ffn_unit[0] + (j + 3)))
                        V.tensor_tensor(dst[:, e, :], B[4 + 2 * e + j][:, :], rstd[:, :], ALU.mult)\
                            .then_inc(gu_evac, 1)

                def finish(f, e, at):
                    h, lo = acth[:, at, :], actl[:, at, :]
                    if not isinstance(at, int):
                        h, lo = h.rearrange("p a t -> p (a t)"), lo.rearrange("p a t -> p (a t)")
                    dve.wait_ge(gu_evac, f * 2 + (n * 2 * FT + 2))
                    dve.wait_ge(silu_done, f + (n * FT + 1))
                    V.tensor_tensor(h, gn[:, e, :], un[:, e, :], ALU.mult).then_inc(act_part, 1)
                    V.tensor_tensor(un[:, e, :], gn[:, e, :], un[:, e, :], ALU.mult).then_inc(act_part, 1)
                    dve.wait_ge(act_part, f * 2 + (n * 2 * FT + 2))
                    V.tensor_tensor(lo, un[:, e, :], h.bitcast(F32), ALU.subtract).then_inc(act_done, 1)

                evacuate(0, 0)
                evacuate(1, 1)
                finish(0, 0, 0)
                with dve.Fori(1, FT // 2) as i:
                    evacuate(i * 2, 0)
                    finish(i * 2 - 1, 1, bass.ds(i * 2 - 1, 1))
                    evacuate(i * 2 + 1, 1)
                    finish(i * 2, 0, bass.ds(i * 2, 1))
                finish(FT - 1, 1, FT - 1)

            ffn_unit = [0]

            def down_done(n, u0):
                return lambda m: (acc_done, n * 7 + (m + 1)) if m < KT - 1 else (unit_used, u0 + (U_FFN + 2))

            def mixer1(l):
                u0 = l * U_LAYER + U_FFN
                V.tensor_tensor(cosr[:, :], cos[:, :], rstd[:, :], ALU.mult).then_inc(pool_step, 1)
                V.tensor_tensor(sinr[:, :], sin[:, :], rstd[:, :], ALU.mult).then_inc(pool_step, 1)
                ps = l * POOL_OPS
                dve.wait_ge(pool_step, ps + 2)

                def rope(pair, which, u, bank):
                    n = pair * 2 + which
                    dve.wait_ge(unit_used, u + 3)
                    for a in range(4):
                        b = a ^ 1
                        V.tensor_tensor(ropet[32 * b:32 * b + 32, 0, :], bank[32 * a:32 * a + 32, :],
                                        sinr[32 * a:32 * a + 32, :], ALU.mult).then_inc(rope_a, 1)
                    V.tensor_tensor(ropet[:, 1, :], bank[:, :], cosr[:, :], ALU.mult).then_inc(rope_a, 1)
                    dve.wait_ge(rope_a, n * ROPE_READS + ROPE_READS)
                    dve.nop().then_inc(proj_read, 1)
                    V.tensor_tensor(qk[:, which, :], ropet[:, 0, :], ropet[:, 1, :], ALU.add).then_inc(rope_done, 1)
                    dve.wait_ge(rope_done, n + 1)

                def low_q(pair, e):
                    dve.wait_ge(qk_hi, pair * 6 + 2)
                    for a in range(2):
                        r, o = slice(HD * a, HD * (a + 1)), slice(HD * (1 - a), HD * (2 - a))
                        V.tensor_tensor(qs[o, e, a, :], qk[r, 0, :], qs[r, e, a, :].bitcast(F32), ALU.subtract)\
                            .then_inc(qk_lo, 1)
                    dve.wait_ge(qk_lo, pair * 4 + 2)

                def low_k(pair, e):
                    dve.wait_ge(qk_hi, pair * 6 + 6)
                    for a in range(2):
                        r = slice(HD * a, HD * (a + 1))
                        V.tensor_tensor(kl[r, e, :], qk[r, 1, :], ks[r, e, a, :].bitcast(F32), ALU.subtract)\
                            .then_inc(qk_lo, 1)
                    dve.wait_ge(qk_lo, pair * 4 + 4)

                def v_out(pair, u, bank):
                    dve.wait_ge(unit_used, u + 3)
                    V.tensor_tensor(vraw[:, :], bank[:, :], rstd[:, :], ALU.mult).then_inc(v_evac, 1)
                    dve.wait_ge(v_evac, pair + 1)
                    dve.nop().then_inc(proj_read, 1)

                rope(l * PAIRS, 0, u0, B[4])
                rope(l * PAIRS, 1, u0 + 1, B[5])
                V.memset(padded[:, :, :], 0.0).then_inc(pool_step, 1)
                V.memset(win[:, :, :], 0.0).then_inc(pool_step, 1)
                low_q(l * PAIRS, 0)
                low_k(l * PAIRS, 0)
                v_out(l * PAIRS, u0 + 2, B[4])
                dve.wait_ge(pool_step, ps + 4)
                for t in range(2):
                    dve.wait_ge(unit_used, u0 + (t + 6))
                    V.tensor_tensor(padded[:, t, PAD:PAD + T], B[5 - t][:, :], rstd[:, :], ALU.mult)\
                        .then_inc(pool_evac, 1)
                dve.wait_ge(pool_evac, l * 2 + 2)
                dve.nop().then_inc(proj_read, 2)

                E = PAD + T + PAD
                low, high = slice(0, HD), slice(HD, P)
                inner = slice(PAD, PAD + T)
                add, mul, sub = ALU.add, ALU.mult, ALU.subtract
                pool_ops = [
                    (4, win[:, :, 1:E], padded[:, :, 0:E - 1], padded[:, :, 1:E], add),
                    (5, win16[:, PAD - 6:PAD + T + 6], win[:, 1, PAD - 7:PAD + T + 5],
                     win[:, 1, PAD - 5:PAD + T + 7], add),
                    (6, win[high, 1, inner], win[high, 0, PAD - 1:PAD + T - 1], win[high, 0, PAD + 1:PAD + T + 1], add),
                    (7, win[high, 0, inner], win[high, 1, inner], invcount[high, 0, :], mul),
                    (7, win[low, 0, inner], win[low, 0, inner], invcount[low, 0, :], mul),
                    (9, win[:, 1, PAD - 4:PAD + T + 4], win16[:, PAD - 6:PAD + T + 2], win16[:, PAD - 2:PAD + T + 6], add),
                    (10, win16[high, inner], win[high, 1, PAD - 4:PAD + T - 4], win[high, 1, PAD + 4:PAD + T + 4], add),
                    (10, win[low, 1, inner], win[low, 1, inner], invcount[low, 1, :], mul),
                    (12, win[high, 1, inner], win16[high, inner], invcount[high, 1, :], mul),
                    (13, padded[:, :, inner], win[:, :, inner], padded[:, :, inner], sub),
                ]

                def pair_steps(j, e, more, pooled=False):
                    pair = l * PAIRS + j
                    step0 = pair * 8
                    u = u0 + 5 + j * 3
                    slot = (1 + e) % 2

                    for s in range(8):
                        i = s % 4
                        dve.wait_ge(s_done, step0 + (s + 1))
                        dve.wait_ge(tr_done, step0 + (s + 1))
                        dve.nop().then_inc(dve_turn, 1)
                        off = 384 - P * i
                        V.tensor_tensor_reduce(sc[:, s % 4, :], B[1 + s % 2][:, :], band[:, off:off + T], 1.0,
                                               -3.0e38, ALU.add, ALU.max, smax[:, s:s + 1]).then_inc(t_done, 1)
                        dve.wait_ge(t_done, step0 + (s + 3))
                        V.tensor_scalar(sneg[:, s:s + 1], smax[:, s:s + 1], -SCALE, None, ALU.mult)\
                            .then_inc(neg_done, 1)
                        if s == 4 and more:
                            rope(pair + 1, 0, u, B[4 + slot])
                        if s == 5 and more:
                            low_q(pair + 1, 1 - e)
                        for n in range(len(pool_ops) * s // 8, len(pool_ops) * (s + 1) // 8) if pooled else ():
                            after, o, in0, in1, op = pool_ops[n]
                            dve.wait_ge(pool_step, ps + after)
                            V.tensor_tensor(o, in0, in1, op).then_inc(pool_step, 1)
                        if s in (4, 6) and not more:
                            t = s // 2 - 2
                            dve.wait_ge(mh_done, l * 8 + (t + 6))
                            V.scalar_tensor_tensor(ml1[:, t, :], B[4 + t][:, :], poolscale_now[:, t:t + 1],
                                                   mh1[:, t, :].bitcast(F32), ALU.mult, ALU.subtract)\
                                .then_inc(ml_done, 1)
                    if more:
                        rope(pair + 1, 1, u + 1, B[5 - slot])
                        low_k(pair + 1, 1 - e)
                    dve.wait_ge(exp_done, step0 + 8)
                    dve.wait_ge(otok_done, pair + 1)
                    V.reciprocal(srec[:, :], sden[:, :]).then_inc(rec_done, 1)
                    dve.wait_ge(rec_done, pair + 1)
                    dve.wait_ge(pv_done, step0 + 10)
                    V.tensor_tensor(otok[:, :, :], B[7][:, :].rearrange("p (c d) -> p c d", c=8),
                                    srec[:, :].rearrange("p (c a) -> p c a", a=1).to_broadcast([P, 8, HD]), ALU.mult)\
                        .then_inc(otok_done, 1)
                    if more:
                        v_out(pair + 1, u + 2, B[4 + slot])

                def output(done, at):
                    h, lo = mh1[:, at, :], ml1[:, at, :]
                    if not isinstance(at, int):
                        h, lo = h.rearrange("p a t -> p (a t)"), lo.rearrange("p a t -> p (a t)")
                    dve.wait_ge(mh_done, done)
                    V.tensor_tensor(lo, B[6][:, :], h.bitcast(F32), ALU.subtract).then_inc(ml_done, 1)

                with dve.Fori(0, 2) as it:
                    for e in range(2):
                        pair_steps(it * 2 + e, e, True)
                        output(l * 8 + it * 2 + (e + 1), bass.ds(it * 2 + (2 + e), 1))
                pair_steps(4, 0, True, True)
                output(l * 8 + 5, 6)
                pair_steps(5, 1, False)
                output(l * 8 + 8, 7)

            with dve.Fori(0, DEPTH) as l:
                V.tensor_copy(gain[:, :, :], gains[:, bass.ds(l, 1), :, :].rearrange("p a n k -> p (a n) k"))\
                    .then_inc(layer_set, 1)
                V.tensor_copy(poolw_now[:, :, :], poolw[:, bass.ds(l, 1), :, :].rearrange("p a n k -> p (a n) k"))\
                    .then_inc(layer_set, 1)
                V.tensor_copy(poolscale_now[:, :], poolscale[:, bass.ds(l, 1), :].rearrange("p a n -> p (a n)"))\
                    .then_inc(layer_set, 1)
                dve.wait_ge(layer_set, (l + 1) * LAYER_COPIES)
                for m in range(KT):
                    low_part(l * 3, m, gain[:, 0, m:m + 1])
                inverse_rms(l * 3)
                ffn_unit[0] = l * U_LAYER
                feed_forward(l * 2)
                updates(0.5, down_done(l * 2, l * U_LAYER), l * 3 + 1, lambda m: gain[:, 1, m:m + 1])
                inverse_rms(l * 3 + 1)
                mixer1(l)
                uo = l * U_LAYER + (U_FFN + U_PROJ)
                updates(1.0, lambda m: (unit_used, uo + (m + 3)), l * 3 + 2, lambda m: gain[:, 2, m:m + 1])
                inverse_rms(l * 3 + 2)
                ffn_unit[0] = l * U_LAYER + (U_FFN + U_PROJ + U_OUT)
                feed_forward(l * 2 + 1)
                updates(0.5, down_done(l * 2 + 1, l * U_LAYER + (U_FFN + U_PROJ + U_OUT)))

            inverse_rms(6)
            for m in range(KT):
                V.scalar_tensor_tensor(x[:, m, :], x[:, m, :], gains2[:, 0, m:m + 1], rstd[:, :], ALU.mult, ALU.mult)\
                    .then_inc(x_done, 1)
            for m in range(KT):
                dve.wait_ge(x_done, 8 * 7 + m + 1)
                low_part(6, m, gains2[:, 1, m:m + 1])
            inverse_rms(7)
            u0 = U_BLOCK2
            dve.wait_ge(const2_in, 16 * N_CONST2)
            V.tensor_copy(wgh[:, :, :], wg[:, :, :]).then_inc(wg_part, 1)
            dve.wait_ge(wg_part, 1)
            V.tensor_tensor(wgl[:, :, :], wg[:, :, :], wgh[:, :, :].bitcast(F32), ALU.subtract).then_inc(wg_done, 1)
            V.tensor_tensor(wst[:, :, :], wst[:, :, :],
                            causal[:, :].rearrange("p (a n) -> p a n", a=1).to_broadcast([P, 8, P]), ALU.mult)\
                .then_inc(ws_done, 1)

            def bank(n):
                dve.wait_ge(unit_used, u0 + n + 3)
                return B[4 + n % 4]

            def scaled(n, dst, last):
                V.tensor_tensor(dst, bank(n)[:, :], rstd[:, :], ALU.mult).then_inc(last, 1)

            halves = [0]
            for n in range(U_PROJ2):
                if n < 4:
                    scaled(n, gv[:, n, :], gelu_in)
                    dve.wait_ge(gelu_in, n + 1)
                elif n < 6:
                    which = n - 4
                    b = bank(n)
                    if which:
                        dve.wait_ge(blk_done, 4)
                    for kv in range(NKV):
                        r = slice(HD * kv, HD * kv + HD)
                        V.tensor_tensor(shifted[0:HD, kv, :], b[r, :], rstd[0:HD, :], ALU.mult).then_inc(shift_done, 1)
                        V.tensor_tensor(shifted[HD:P, kv, 0:T - 1], b[r, 1:T], rstd[HD:P, 1:T], ALU.mult)\
                            .then_inc(shift_done, 1)
                    dve.wait_ge(shift_done, 4 * which + 4)
                    for kv in range(NKV):
                        v = shifted[:, kv, :].rearrange("p (n s two) -> p s n two", s=8, two=2)
                        for half in range(2):
                            V.tensor_tensor(blk[:, which, 8 * half:8 * half + 8, NCMP * kv:NCMP * (kv + 1)],
                                            v[:, :, half:half + NCMP, 0],
                                            poscol[:, which, 8 * half:8 * half + 8]
                                            .rearrange("p (s a) -> p s a", a=1).to_broadcast([P, 8, NCMP]), ALU.add)\
                                .then_inc(blk_done, 1)
                elif n < 8:
                    b = bank(n)
                    for kv in range(NKV):
                        for half in range(2):
                            V.tensor_tensor(kdup[HD * half:HD * half + HD, n - 6, kv, :],
                                            b[HD * kv:HD * kv + HD, :], rstd[HD * half:HD * half + HD, :], ALU.mult)\
                                .then_inc(half2, 1)
                            halves[0] += 1
                    dve.wait_ge(half2, halves[0])
                elif n < 10:
                    scaled(n, vs2[:, n - 8, :], half2)
                    halves[0] += 1
                    dve.wait_ge(half2, halves[0])
                elif n < 14:
                    scaled(n, qall[:, n - 10, :], half2)
                    halves[0] += 1
                    dve.wait_ge(half2, halves[0])
                else:
                    scaled(n, gu[:, n - 14, :], gelu_in)
                    dve.wait_ge(gelu_in, 4 + n - 14 + 1)
                dve.nop().then_inc(evac2, 1)

            def inverse_rms2(n, b, width):
                dve.wait_ge(ss2_done, n + 1)
                V.tensor_scalar(rstd2[:, :], b[:, :], 1.0 / width, EPS, ALU.mult, ALU.add).then_inc(mean2, 1)
                dve.wait_ge(root2, n + 1)
                V.reciprocal(rstd2[:, :], rstd2[:, :]).then_inc(rstd2_done, 1)
                dve.wait_ge(rstd2_done, n + 1)

            inverse_rms2(0, B[1], 512)
            for t in range(4):
                V.scalar_tensor_tensor(gv[:, t, :], gv[:, t, :], vec2[:, 0, t:t + 1], rstd2[:, :], ALU.mult, ALU.mult)\
                    .then_inc(vn_done, 1)
            dve.wait_ge(rc_mm, 1)
            V.tensor_copy(rcol[:, :], B[2][:, :].rearrange("p (i n) -> p i n", i=NQ)[:, :, 0]).then_inc(rcol_done, 1)
            dve.wait_ge(rcol_done, 1)
            dve.wait_ge(gate_mm, 1)
            V.tensor_tensor(gates[:, :, :], B[0][:, 0:NQ * NGATE].rearrange("p (i n) -> p i n", i=NQ),
                            rcol[:, :].rearrange("p (i a) -> p i a", a=1).to_broadcast([P, NQ, NGATE]), ALU.mult)\
                .then_inc(gate_a, 1)
            dve.wait_ge(gate_a, 1)
            V.tensor_tensor(gates[:, :, :], gates[:, :, :],
                            gateb[:, :].rearrange("p (a n) -> p a n", a=1).to_broadcast([P, NQ, NGATE]), ALU.add)\
                .then_inc(gate_b, 1)
            dve.wait_ge(cmp_mm, 1)
            V.tensor_copy(kcall[:, :, :], B[2][:, 0:NKV * NCMP].rearrange("p (a n) -> p a n", a=NKV))\
                .then_inc(cmp_done, 1)
            dve.wait_ge(cmp_mm, 2)
            V.tensor_copy(vcall[0:NCMP, :, :], B[0][0:NCMP, 0:NKV * HD].rearrange("p (a n) -> p a n", a=NKV))\
                .then_inc(cmp_done, 1)
            dve.wait_ge(gelu_done, 8)
            for t in range(4):
                dve.wait_ge(sv_mm, t + 1)
                b = B[4 + t % 2]
                if t >= 2:
                    dve.wait_ge(a_done, t - 1)
                V.tensor_tensor(svt(t), b[:, :].rearrange("p (c n) -> p c n", c=NQ),
                                bsb[:, t:t + 1, :].to_broadcast([P, NQ, P]), ALU.add).then_inc(sv_add, 1)
                dve.wait_ge(sv_add, t + 1)
                V.tensor_tensor(gu[:, t, :], gu[:, t, :], vs2[:, t % 2, :], ALU.mult)\
                    .then_inc(a_done, 1)

            def normed(n, src, base):
                for t in range(4):
                    V.scalar_tensor_tensor(src[:, t, :], src[:, t, :], vec2[:, n, t:t + 1], rstd2[:, :],
                                           ALU.mult, ALU.mult).then_inc(norm_mul, 1)
                for t in range(4):
                    dve.wait_ge(norm_mul, 4 * (n - 1) + t + 1)
                    dve.wait_ge(mh2_done, 4 * (n - 1) + t + 1)
                    V.tensor_tensor(ml2[:, base + t, :], src[:, t, :], mh2[:, base + t, :].bitcast(F32), ALU.subtract)\
                        .then_inc(ml2_done, 1)

            inverse_rms2(1, B[6], 512)
            normed(1, gu, 0)

            dve.wait_ge(gates_done, 1)
            dve.wait_ge(cmp_done, 2)
            dve.wait_ge(v2_done, 2)
            def wide(v):
                return v.rearrange("p (i a) -> p i a", a=1).to_broadcast([P, NQ, NCMP])

            def compressed_max(g, hh):
                H = g * 4 + hh
                dve.wait_ge(cs_done, H + 1)
                dve.wait_ge(ctr_done, H + 1)
                V.tensor_tensor(scc[:, :, :], B[5][:, 0:NQ * NCMP].rearrange("p (i n) -> p i n", i=NQ),
                                cmpbias[:, :, :], ALU.add).then_inc(ct_step, 1)
                dve.wait_ge(ct_step, H * 2 + 1)
                V.reduce_max(cmax[:, :], scc[:, :, :], mybir.AxisListType.X).then_inc(ct_step, 1)
                dve.wait_ge(ct_step, H * 2 + 2)
                V.tensor_tensor(scc[:, :, :], scc[:, :, :], wide(cmax[:, :]), ALU.subtract).then_inc(ct_done, 1)

            def compressed_normalise(g, hh):
                H = g * 4 + hh
                dve.wait_ge(ce_done, H + 1)
                V.reduce_sum(cden[:, :], scc[:, :, :], mybir.AxisListType.X).then_inc(cn_step, 1)
                dve.wait_ge(cn_step, H * 4 + 1)
                V.reciprocal(cden[:, :], cden[:, :]).then_inc(cn_step, 1)
                dve.wait_ge(cn_step, H * 4 + 2)
                V.tensor_tensor(cden[:, :], cden[:, :], gst[:, :, 0, hh], ALU.mult).then_inc(cn_step, 1)
                dve.wait_ge(cn_step, H * 4 + 3)
                V.tensor_tensor(scc[:, :, :], scc[:, :, :], wide(cden[:, :]), ALU.mult).then_inc(cn_step, 1)
                dve.wait_ge(cn_step, H * 4 + 4)
                V.tensor_tensor(scc[:, :, :], scc[:, :, :], cmpseen[:, :, :], ALU.mult).then_inc(cp_done, 1)

            with dve.Fori(0, NKV) as g:
                dve.wait_ge(pv2_done, g * 16 + 2)
                dve.nop().then_inc(stage_open, 1)
                for n in range(2):
                    V.tensor_copy(kst[:, n, :], kdup[:, n, bass.ds(g, 1), :].rearrange("p a t -> p (a t)"))\
                        .then_inc(staged, 1)
                    V.tensor_copy(vst[:, n, :, :], vall[:, n, :, bass.ds(g * HD, HD)]).then_inc(staged, 1)
                    V.tensor_copy(qst[:, n, :], qall[:, bass.ds(g * 2 + n, 1), :].rearrange("p a t -> p (a t)"))\
                        .then_inc(staged, 1)
                V.tensor_copy(kcst[:, :], kcall[:, bass.ds(g, 1), :].rearrange("p a t -> p (a t)")).then_inc(staged, 1)
                V.tensor_copy(vcst[0:NCMP, :], vcall[0:NCMP, bass.ds(g, 1), :].rearrange("p a t -> p (a t)"))\
                    .then_inc(staged, 1)
                V.tensor_copy(gst[:, :, :, :], gates[:, :, :].rearrange("p i (n h) -> p i n h", n=3)
                              [:, :, :, bass.ds(g * 4, 4)]).then_inc(staged, 1)
                dve.wait_ge(staged, (g + 1) * STAGED)
                compressed_max(g, 0)
                for n in range(2):
                    dve.wait_ge(hi2_done, g * 6 + (n + 1))
                    V.tensor_tensor(kl2[:, n, :], kst[:, n, :], kh2[:, n, :].bitcast(F32), ALU.subtract)\
                        .then_inc(lo2_done, 1)
                for hd in range(4):
                    a = hd % 2
                    r, o = slice(HD * a, HD * (a + 1)), slice(HD * (1 - a), HD * (2 - a))
                    dve.wait_ge(hi2_done, g * 6 + (hd + 3))
                    V.tensor_tensor(qs2[o, hd, :], qst[r, hd // 2, :], qs2[r, hd, :].bitcast(F32), ALU.subtract)\
                        .then_inc(lo2_done, 1)

                def normalise2(s):
                    i, par, hh = TILES2[s % 4], s % 2, s // 4
                    n = P * (i + 1)
                    G = g * 16 + s
                    dve.wait_ge(exp2_done, G * 2 + 2)
                    V.reciprocal(srec2[:, par, :], sden2[:, par, :]).then_inc(rec2_done, 1)
                    dve.wait_ge(rec2_done, G + 1)
                    V.tensor_tensor(coef2[:, par, :], srec2[:, par, :], gst[:, i, 1:3, hh], ALU.mult)\
                        .then_inc(coef2_done, 1)
                    dve.wait_ge(coef2_done, G + 1)
                    for c in range(2):
                        V.tensor_scalar(sc2[:, s % 4, c, 0:n], sc2[:, s % 4, c, 0:n], coef2[:, par, c:c + 1], None,
                                        ALU.mult).then_inc(p2_done, 1)

                def output2(t2, done):
                    dve.wait_ge(pv2_done, done)
                    V.tensor_scalar(oall[:, bass.ds(g * 2 + t2, 1), :].rearrange("p a t -> p (a t)"), B[7][:, :],
                                    1.0, None, ALU.mult).then_inc(o2_done, 1)

                for s in range(16):
                    i, par = TILES2[s % 4], s % 2
                    n = P * (i + 1)
                    off = 384 - P * i
                    G = g * 16 + s
                    dve.wait_ge(s2_done, G + 1)
                    dve.wait_ge(tr2_done, G + 1)
                    dve.nop().then_inc(turn2, 1)
                    for c in range(2):
                        V.tensor_tensor_reduce(sc2[:, s % 4, c, 0:n], B[1 + 2 * c + par][:, 0:n], tri[:, off:off + n],
                                               1.0, -3.0e38, ALU.add, ALU.max, smax2[:, par, c:c + 1])\
                            .then_inc(t2_done, 1)
                    dve.wait_ge(t2_done, G * 2 + 6)
                    V.tensor_scalar(sneg2[:, par, :], smax2[:, par, :], -SCALE, None, ALU.mult).then_inc(neg2_done, 1)
                    if s == 0:
                        compressed_normalise(g, 0)
                    if s >= 1:
                        normalise2(s - 1)
                    if s % 4 == 0 and s > 0:
                        compressed_max(g, s // 4)
                    if s % 4 == 1 and s > 4:
                        compressed_normalise(g, s // 4)
                    if s == 10:
                        output2(0, g * 16 + 10)
                normalise2(15)
                output2(1, g * 16 + 18)
            inverse_rms2(2, B[1], 512)
            normed(2, oall, 4)
            uo = U_BLOCK2 + U_PROJ2
            updates(1.0, lambda m: (unit_used, uo + m + 3), 7, lambda m: gains2[:, 2, m:m + 1])
            inverse_rms(8)
            ffn_unit[0] = uo + U_OUT
            feed_forward(4)
            updates(1.0, down_done(4, uo + U_OUT))
            inverse_rms(9)
            for m in range(KT):
                V.scalar_tensor_tensor(x[:, m, :], x[:, m, :], gains2[:, 3, m:m + 1], rstd[:, :], ALU.mult, ALU.mult)\
                    .then_inc(fin_done, 1)


def lay_out(inputs):
    a = {k: np.asarray(v) for k, v in inputs.items()}

    def cols(w, c):
        return w[:, c:c + P].reshape(8, P, P).transpose(1, 0, 2)

    units = []

    def ffn(g, u, dn):
        for f in range(FT):
            units.append(cols(g, f * P))
            units.append(cols(u, f * P))
        for f in range(FT):
            units.append(dn[f * P:(f + 1) * P].reshape(P, 8, P))

    turned = np.r_[HEAD_ORDER, HD + HEAD_ORDER]

    for l in range(DEPTH):
        ffn(a["ffn1_w_gate"][l], a["ffn1_w_up"][l], a["ffn1_w_down"][l])
        w = a["w_in"][l]
        pooled = [cols(w, 0), cols(w, P)]
        for j in range(PAIRS):
            q, k, v = [cols(w, POOL_W + n * PAIRS * P + j * P) for n in range(3)]
            units += [q[..., turned], k[..., turned], v] + (pooled if j == 0 else [])
        units += [cols(a["w_out"][l], m * P) for m in range(KT)]
        ffn(a["ffn2_w_gate"][l], a["ffn2_w_up"][l], a["ffn2_w_down"][l])
    w = a["w_in_2"][0]
    units += [cols(w, c * P) for c in ORDER2]
    units += [cols(a["w_o_2"][0], m * P) for m in range(KT)]
    ffn(a["w_gate_2"][0], a["w_up_2"][0], a["w_down_2"][0])
    assert len(units) == U_ALL
    stream = np.empty((U_ALL // 2, P, 2, 8 * P), np.float32)
    for u, unit in enumerate(units):
        stream[u // 2, :, u % 2] = unit.reshape(P, 8 * P)

    def tiles(v):
        v = v.reshape(*v.shape[:-1], -1, P)
        return np.moveaxis(v, -1, 0)

    out = {
        "x": a["x"][0].T.reshape(KT, P, T).transpose(1, 0, 2),
        "positions": a["positions"].reshape(1, T),
        "stream": stream,
        "gains": tiles(np.stack([a["ffn1_norm"], a["mix_norm"], a["ffn2_norm"]], 1)),
        "gains2": tiles(np.stack([a["final_norm"], a["norm_mix_w_2"][0], a["norm_ffn_w_2"][0], a["final_norm_w_2"]])),
        "poolw": a["pool_w"].reshape(DEPTH, 2, P, HD).transpose(2, 0, 1, 3),
        "poolscale": tiles(a["pool_scale"]),
        "ws_2": a["gmlp_ws_2"][0].transpose(2, 0, 1),
        "bs_2": a["gmlp_bs_2"][0].reshape(4, 2, P).transpose(1, 0, 2),
        "wg_2": w[:, U_PROJ2 * P:].reshape(8, P, NGATE).transpose(1, 0, 2),
        "gate_b_2": np.broadcast_to(a["gate_b_2"], (P, NGATE)),
        "vec_2": tiles(np.concatenate([a["gmlp_norm_w_2"], a["out_norm_a_w_2"], a["out_norm_b_w_2"]])),
        "pos_2": np.stack([a["cmp_pos_k_2"][0], a["cmp_pos_v_2"][0]]).reshape(2, SLABS, P).transpose(2, 0, 1),
        "w1k_2": a["cmp_k_w1_2"][0].reshape(SLABS, P, CH).transpose(1, 0, 2),
        "w1v_2": a["cmp_v_w1_2"][0].reshape(SLABS, P, CH).transpose(1, 0, 2),
        "w2k_2": a["cmp_k_w2_2"][0].reshape(2, P, HD).transpose(1, 0, 2),
        "w2v_2": a["cmp_v_w2_2"][0].reshape(2, P, HD).transpose(1, 0, 2),
    }
    out.update(shape_constants())
    return {k: np.ascontiguousarray(v) for k, v in out.items()}


def kernel(**inputs):
    import concourse.bacc as bacc
    from concourse.bass_utils import run_bass_kernel_spmd as run

    nc = bacc.Bacc("TRN2", target_bir_lowering=False, num_devices=1)
    arrays = {"in_" + k: v for k, v in lay_out(inputs).items()}
    d = {k[3:]: nc.dram_tensor(k, v.shape, mybir.dt.from_np(v.dtype), kind="ExternalInput").ap()
         for k, v in arrays.items()}
    d["out"] = nc.dram_tensor("out_dram", (P, KT, T), F32, kind="ExternalOutput").ap()
    build(nc, d)
    r = run(nc, [arrays], core_ids=[0])
    y = r.results[0]["out_dram"]
    return np.ascontiguousarray(y.transpose(1, 0, 2).reshape(D, T).T).reshape(1, T, D)
```

```python
from contextlib import ExitStack

import numpy as np

import concourse.bass as bass
from concourse import mybir

F32 = mybir.dt.float32
F32R = mybir.dt.float32r
I32 = mybir.dt.int32
ALU = mybir.AluOpType
ACT = mybir.ActivationFunctionType

P = 128
T = 512
D = 1024
KT = D // P
DEPTH = 2
DFF = 2816
FT = DFF // P
NQ = T // P
HD = 64
EPS = 1e-6
SCALE = HD ** -0.5
NEG = -1e30

POOL_W = 256
PAIRS = 6
WINDOWS = (2, 4, 8, 16)
PAD = 8
POOL_OPS = 4 + 10
NKV = 2
NCMP = (T - 32) // 16 + 1
CH = 256
NGATE = 24
SLABS = 16

U_FFN = 3 * FT
U_PROJ = 2 + 3 * PAIRS
U_OUT = KT
U_LAYER = 2 * U_FFN + U_PROJ + U_OUT
U_PROJ2 = 18
U_BLOCK2 = DEPTH * U_LAYER
U_ALL = U_BLOCK2 + U_PROJ2 + U_OUT + U_FFN
ORDER2 = [12, 13, 4, 5, 6, 7, 0, 1, 2, 3, 14, 16, 15, 17, 8, 9, 10, 11]

HEAD_ORDER = np.r_[0:8, 16:40, 8:16, 40:64]
ROPE_READS = 5
LAG2 = 3
TILES2 = (3, 0, 2, 1)


def shape_constants():
    p = np.arange(P)[:, None]
    c = np.arange(T + 384)[None, :]
    d = c - 384 - p
    count = (np.abs(d) <= 64) * 1 + ((d % 4 == 0) & (np.abs(d) <= 256)) + (d % 16 == 0)
    band = np.where(count > 0, np.log(np.maximum(count, 1)) / SCALE, NEG)
    tri = np.where(c[:, :T] - 384 <= p, 0.0, NEG)
    tq = (np.arange(NQ)[None, :, None] * P + np.arange(P)[:, None, None])
    seen = (16 * np.arange(NCMP)[None, None, :] + 31) <= tq
    pos = np.arange(T)
    inv = np.zeros((P, 2, T))
    for g, w in enumerate(WINDOWS):
        lo = np.maximum(pos - w // 2, 0)
        hi = np.minimum(pos + w - 1 - w // 2, T - 1)
        inv[64 * (g % 2):64 * (g % 2) + 64, g // 2, :] = 1.0 / (hi - lo + 1)
    dim = np.tile(HEAD_ORDER, 2)
    freq = np.where(dim < 16, np.float32(500000.0) ** (-(2 * (dim % 8)).astype(np.float32) / np.float32(16)), 0.0)
    cols = np.stack([freq, dim < 16, dim >= 16, (dim < 8) * 1.0 - ((dim >= 8) & (dim < 16))], 1)
    out = {
        "c_band": band, "c_tri": tri, "c_cmpbias": np.where(seen, 0.0, NEG), "c_cmpseen": seen,
        "c_ident": np.eye(P), "c_ones": np.ones((P, P)), "c_invcount": inv,
        "c_causal": p <= np.arange(P)[None, :], "c_rope": cols,
    }
    return {k: np.ascontiguousarray(v.astype(np.float32)) for k, v in out.items()}


def build(nc, d):
    ctx = ExitStack()
    with ctx:
        def sem(name):
            return ctx.enter_context(nc.semaphore(name))

        def sb(name, shape, dt=F32, at=ctx):
            return at.enter_context(nc.sbuf_tensor(name, shape, dt))

        parts = ExitStack()
        xh = sb("xh", [P, KT, T], F32R, at=parts)
        xl = sb("xl", [P, KT, T], F32R, at=parts)
        parts.close()
        sc2 = sb("sc2", [P, 4, 2, T])
        pt2 = sb("pt2", [P, 2, 2, T])
        vst = sb("vst", [P, 2, NQ, HD])
        parts_rest = sb("parts_rest", [P, 3, T])
        x = sb("x", [P, KT, T])
        raw = sb("raw", [P, 2, 2, 8 * P])
        wh = sb("wh", [P, 2, 8, P], F32R)
        wl = sb("wl", [P, 2, 8, P], F32R)
        sq = sb("sq", [P, 4, T])
        rstd = sb("rstd", [P, T])
        ident = sb("ident", [P, P])
        ones = sb("ones", [P, P])
        gains = sb("gains", [P, DEPTH, 3, KT])
        gains2 = sb("gains2", [P, 4, KT])
        gain = sb("gain", [P, 3, KT])

        block1 = ExitStack()
        cos = sb("cos", [P, T], at=block1)
        sin = sb("sin", [P, T], at=block1)
        band = sb("band", [P, T + 384], at=block1)
        invcount = sb("invcount", [P, 2, T], at=block1)
        ropecol = sb("ropecol", [P, 4], at=block1)
        poolw = sb("poolw", [P, DEPTH, 2, HD], at=block1)
        poolscale = sb("poolscale", [P, DEPTH, 2], at=block1)
        poolw_now = sb("poolw_now", [P, 2, HD], at=block1)
        poolscale_now = sb("poolscale_now", [P, 2], at=block1)

        mix1 = ExitStack()
        posi = sb("posi", [P, T], I32, at=mix1)
        cosr = sb("cosr", [P, T], at=mix1)
        sinr = sb("sinr", [P, T], at=mix1)
        mh1 = sb("mh1", [P, KT, T], F32R, at=mix1)
        ml1 = sb("ml1", [P, KT, T], F32R, at=mix1)
        vraw = sb("vraw", [P, T], at=mix1)
        qk = sb("qk", [P, 2, T], at=mix1)
        qs = sb("qs", [P, 2, 2, T], F32R, at=mix1)
        ks = sb("ks", [P, 2, 2, T], F32R, at=mix1)
        kl = sb("kl", [P, 2, T], F32R, at=mix1)
        vtok = sb("vtok", [P, 2, NQ, P], at=mix1)
        sc = sb("sc", [P, 4, T], at=mix1)
        pt = sb("pt", [P, 2, T], at=mix1)
        otok = sb("otok", [P, 8, HD], at=mix1)
        ropet = sb("ropet", [P, 2, T], at=mix1)
        padded = sb("padded", [P, 2, PAD + T + PAD], at=mix1)
        win = sb("win", [P, 2, PAD + T + PAD], at=mix1)
        win16 = sb("win16", [P, PAD + T + PAD], at=mix1)
        smax = sb("smax", [P, 8], at=mix1)
        sneg = sb("sneg", [P, 8], at=mix1)
        sden = sb("sden", [P, 8], at=mix1)
        srec = sb("srec", [P, 8], at=mix1)
        mix1.close()

        ffn = ExitStack()
        acth = sb("acth", [P, FT, T], F32R, at=ffn)
        actl = sb("actl", [P, FT, T], F32R, at=ffn)
        gn = sb("gn", [P, 2, T], at=ffn)
        un = sb("un", [P, 2, T], at=ffn)
        ffn.close()
        block1.close()

        mix2 = ExitStack()
        gu = sb("gu", [P, 4, T], at=mix2)
        bsb = sb("bsb", [P, 4, P], at=mix2)
        causal = sb("causal", [P, P], at=mix2)
        tri = sb("tri", [P, T], at=mix2)
        cmpbias = sb("cmpbias", [P, NQ, NCMP], at=mix2)
        cmpseen = sb("cmpseen", [P, NQ, NCMP], at=mix2)
        wg = sb("wg", [P, KT, NGATE], at=mix2)
        wgh = sb("wgh", [P, KT, NGATE], F32R, at=mix2)
        wgl = sb("wgl", [P, KT, NGATE], F32R, at=mix2)
        gateb = sb("gateb", [NGATE, 1], at=mix2)
        gates = sb("gates", [P, NQ, NGATE], at=mix2)
        vec2 = sb("vec2", [P, 3, 4], at=mix2)
        poscol = sb("poscol", [P, 2, SLABS], at=mix2)
        w2k = sb("w2k", [P, 2, P], at=mix2)
        w2v = sb("w2v", [P, 2, HD], at=mix2)
        kdup = sb("kdup", [P, 2, NKV, T], at=mix2)
        vall = sb("vall", [P, 2, NQ, P], at=mix2)
        qall = sb("qall", [P, 4, T], at=mix2)
        oall = sb("oall", [P, 4, T], at=mix2)
        kcall = sb("kcall", [P, NKV, NCMP + 1], at=mix2)
        vcall = sb("vcall", [P, NKV, HD], at=mix2)
        rstd2 = sb("rstd2", [P, T], at=mix2)

        comp = ExitStack()
        gv = sb("gv", [P, 4, T], at=comp)
        gvtok = sb("gvtok", [P, 4, NQ, P], at=comp)
        wst = sb("wst", [P, 8, P], at=comp)
        vs2 = sb("vs2", [P, 2, T], at=comp)

        def svt(t):
            return shifted[:, t % 2, :].rearrange("p (c n) -> p c n", c=NQ)
        w1 = sb("w1", [P, SLABS, CH], at=comp)
        shifted = sb("shifted", [P, NKV, T], at=comp)
        blk = sb("blk", [P, 2, SLABS, NKV * NCMP], at=comp)
        hidt = sb("hidt", [P, 2, CH], at=comp)
        hid = sb("hid", [P, 2, 2, NKV * NCMP], at=comp)
        comp.close()
        attn2 = ExitStack()
        mh2 = sb("mh2", [P, KT, T], F32R, at=attn2)
        ml2 = sb("ml2", [P, KT, T], F32R, at=attn2)
        qs2 = sb("qs2", [P, 4, T], F32R, at=attn2)
        kh2 = sb("kh2", [P, 2, T], F32R, at=attn2)
        kl2 = sb("kl2", [P, 2, T], F32R, at=attn2)
        kch = sb("kch", [P, NCMP + 1], F32R, at=attn2)
        kcl = sb("kcl", [P, NCMP + 1], F32R, at=attn2)
        vcst = sb("vcst", [P, HD], at=attn2)
        gst = sb("gst", [P, NQ, 3, 4], at=attn2)
        scc = sb("scc", [P, NQ, NCMP], at=attn2)
        ptc = sb("ptc", [P, 2, T], at=attn2)
        smax2 = sb("smax2", [P, 2, 2], at=attn2)
        sneg2 = sb("sneg2", [P, 2, 2], at=attn2)
        sden2 = sb("sden2", [P, 2, 2], at=attn2)
        srec2 = sb("srec2", [P, 2, 2], at=attn2)
        coef2 = sb("coef2", [P, 2, 2], at=attn2)
        cmax = sb("cmax", [P, NQ], at=attn2)
        cden = sb("cden", [P, NQ], at=attn2)
        attn2.close()
        mix2.close()

        B = [ctx.enter_context(nc.psum_tensor(f"bank{i}", [P, T], F32)) for i in range(8)]

        raw_in = [sem("raw_in0"), sem("raw_in1")]
        x_in = [sem("x_in0"), sem("x_in1")]
        gains_in = sem("gains_in")
        const_in = sem("const_in")
        const2_in = sem("const2_in")
        pos_in = sem("pos_in")
        w1k_in = sem("w1k_in")
        w1v_in = sem("w1v_in")
        out_done = [sem(f"out_done{part}") for part in range(4)]
        split_begun = sem("split_begun")
        hi_split = sem("hi_split")
        split_done = sem("split_done")
        unit_used = sem("unit_used")
        x_done = sem("x_done")
        sq_done = sem("sq_done")
        sq_used = sem("sq_used")
        ss_done = sem("ss_done")
        xh_done = sem("xh_done")
        xl_done = sem("xl_done")
        mean_done = sem("mean_done")
        root_done = sem("root_done")
        rstd_done = sem("rstd_done")
        layer_set = sem("layer_set")
        gu_evac = sem("gu_evac")
        silu_done = sem("silu_done")
        act_part = sem("act_part")
        act_done = sem("act_done")
        acc_done = sem("acc_done")
        trig = sem("trig")
        trig_act = sem("trig_act")
        tables_done = sem("tables_done")
        pool_step = sem("pool_step")
        pool_evac = sem("pool_evac")
        proj_read = sem("proj_read")
        qk_hi = sem("qk_hi")
        qk_lo = sem("qk_lo")
        v_evac = sem("v_evac")
        rope_a = sem("rope_a")
        rope_done = sem("rope_done")
        vt_done = sem("vt_done")
        vtok_done = sem("vtok_done")
        s_done = sem("s_done")
        dve_turn = sem("dve_turn")
        t_done = sem("t_done")
        neg_done = sem("neg_done")
        exp_done = sem("exp_done")
        rec_done = sem("rec_done")
        otok_done = sem("otok_done")
        ot_done = sem("ot_done")
        tr_done = sem("tr_done")
        pte_done = sem("pte_done")
        pv_done = sem("pv_done")
        poolmm_done = sem("poolmm_done")
        out_turn = sem("out_turn")
        pe_turn = sem("pe_turn")
        mh_done = sem("mh_done")
        ml_done = sem("ml_done")
        evac2 = sem("evac2")
        half2 = sem("half2")
        gelu_in = sem("gelu_in")
        gelu_done = sem("gelu_done")
        sq2_done = sem("sq2_done")
        ss2_done = sem("ss2_done")
        mean2 = sem("mean2")
        root2 = sem("root2")
        rstd2_done = sem("rstd2_done")
        wg_part = sem("wg_part")
        wg_done = sem("wg_done")
        gate_mm = sem("gate_mm")
        gate_a = sem("gate_a")
        gate_b = sem("gate_b")
        gate_tr = sem("gate_tr")
        gates_done = sem("gates_done")
        shift_done = sem("shift_done")
        blk_done = sem("blk_done")
        hid_mm = sem("hid_mm")
        hid_gelu = sem("hid_gelu")
        hid_tr = sem("hid_tr")
        hid_done = sem("hid_done")
        cmp_mm = sem("cmp_mm")
        cmp_done = sem("cmp_done")
        v2_mm = sem("v2_mm")
        v2_done = sem("v2_done")
        vn_done = sem("vn_done")
        gt_mm = sem("gt_mm")
        gt_done = sem("gt_done")
        ws_done = sem("ws_done")
        sv_mm = sem("sv_mm")
        sv_add = sem("sv_add")
        a_done = sem("a_done")
        norm_mul = sem("norm_mul")
        mh2_done = sem("mh2_done")
        ml2_done = sem("ml2_done")
        stage_open = sem("stage_open")
        staged = sem("staged")
        s2_done = sem("s2_done")
        turn2 = sem("turn2")
        t2_done = sem("t2_done")
        neg2_done = sem("neg2_done")
        exp2_done = sem("exp2_done")
        rec2_done = sem("rec2_done")
        coef2_done = sem("coef2_done")
        p2_done = sem("p2_done")
        cs_done = sem("cs_done")
        ct_step = sem("ct_step")
        ct_done = sem("ct_done")
        ce_done = sem("ce_done")
        cn_step = sem("cn_step")
        cp_done = sem("cp_done")
        ctr_done = sem("ctr_done")
        cpt_done = sem("cpt_done")
        tr2_done = sem("tr2_done")
        pte2_done = sem("pte2_done")
        pv2_done = sem("pv2_done")
        hi2_done = sem("hi2_done")
        lo2_done = sem("lo2_done")
        o2_done = sem("o2_done")
        fin_done = sem("fin_done")

        N_CONST = 5
        N_CONST2 = 14
        STAGED = 4
        LOW_PARTS = 7
        LAYER_COPIES = 3

        block = ctx.enter_context(nc.Block())

        @block.sync
        def _(sp):
            sp.dma_start(posi[:, :], d["positions"].to_broadcast([P, T])).then_inc(pos_in, 16)
            sp.dma_start(ropecol[:, :], d["c_rope"]).then_inc(pos_in, 16)
            sp.dma_start(x[:, 0:4, :], d["x"][:, 0:4, :]).then_inc(x_in[0], 16)

            def load_pair(pair, e, first):
                if not first:
                    sp.wait_ge(split_done, pair * 2 - 2)
                sp.dma_start(raw[:, e, :, :], d["stream"][pair]).then_inc(raw_in[e], 16)

            load_pair(0, 0, True)
            sp.dma_start(x[:, 4:8, :], d["x"][:, 4:8, :]).then_inc(x_in[1], 16)
            load_pair(1, 1, True)
            with sp.Fori(1, U_BLOCK2 // 4 + 1) as i:
                for e in range(2):
                    load_pair(i * 2 + e, e, False)

            sp.wait_ge(x_done, 8 * 8)
            for dst, name in ((wst, "ws_2"), (causal, "c_causal"), (tri, "c_tri"), (cmpbias, "c_cmpbias"),
                              (cmpseen, "c_cmpseen"), (wg, "wg_2"), (gateb, "gate_b_2"), (vec2, "vec_2"),
                              (poscol, "pos_2"), (w2v, "w2v_2")):
                sp.dma_start(dst[tuple([slice(None)] * len(dst.shape))], d[name]).then_inc(const2_in, 16)
            for half in range(2):
                sp.dma_start(w2k[:, :, HD * half:HD * half + HD], d["w2k_2"]).then_inc(const2_in, 16)
                sp.dma_start(bsb[HD * half:HD * half + HD, :, :],
                             d["bs_2"][half:half + 1].to_broadcast([HD, 4, P])).then_inc(const2_in, 16)
            sp.dma_start(w1[:, :, :], d["w1k_2"]).then_inc(w1k_in, 16)

            for e in range(2):
                load_pair((U_BLOCK2 // 4 + 1) * 2 + e, e, False)
            sp.wait_ge(hid_mm, 1)
            sp.dma_start(w1[:, :, :], d["w1v_2"]).then_inc(w1v_in, 16)
            with sp.Fori(U_BLOCK2 // 4 + 2, U_ALL // 4) as i:
                for e in range(2):
                    load_pair(i * 2 + e, e, False)
            for part in range(4):
                sp.wait_ge(fin_done, 2 * part + 2)
                sp.dma_start(d["out"][:, 2 * part:2 * part + 2, :], x[:, 2 * part:2 * part + 2, :])\
                    .then_inc(out_done[part], 16)
            for part in range(4):
                sp.wait_ge(out_done[part], 16)

        @block.gpsimd
        def _(pool):
            with pool.Fori(0, U_ALL // 4) as i:
                for e in range(2):
                    for h in range(2):
                        u = i * 4 + (2 * e + h)
                        if h == 0:
                            pool.wait_ge(raw_in[e], i * 16 + 16)
                        pool.wait_ge(unit_used, u + 1)
                        nc.gpsimd.nop().then_inc(split_begun, 1)
                        src = raw[:, e, h, :].rearrange("p (k n) -> p k n", k=8)
                        nc.gpsimd.tensor_scalar(wh[:, h, :, :], src, 1.0, 1.0, ALU.mult, ALU.mult)\
                            .then_inc(hi_split, 1)
                        pool.wait_ge(hi_split, u + 1)
                        nc.gpsimd.tensor_tensor(wl[:, h, :, :], src, wh[:, h, :, :].bitcast(F32),
                                                ALU.subtract).then_inc(split_done, 1)

        @block.tensor
        def _(pe):
            pe.nop().then_inc(unit_used, 2)
            pe.nop().then_inc(tr_done, 4)
            pe.nop().then_inc(pv_done, 2)
            pe.nop().then_inc(tr2_done, 4)
            pe.nop().then_inc(pv2_done, 2)
            pe.nop().then_inc(ctr_done, 1)
            def split_product(bank, slot, k, rh, rl, start, stop):
                mm = nc.tensor.matmul(bank, wh[:, slot, k, :], rh, start=start, stop=False)
                mm = nc.tensor.matmul(bank, wh[:, slot, k, :], rl, start=False, stop=False)
                return nc.tensor.matmul(bank, wl[:, slot, k, :], rh, start=False, stop=stop)

            def square_sum(prep, m, bank):
                pe.wait_ge(sq_done, prep * 8 + (m + 1))
                nc.tensor.matmul(bank[:, :], ones[:, :], sq[:, m % 4, :], start=(m == 0), stop=(m == KT - 1))\
                    .then_inc(sq_used, 1)

            def sum_of_sums(prep, bank):
                pe.wait_ge(const_in, 16 * N_CONST)
                pe.wait_ge(sq_used, prep * 8 + 12)
                nc.tensor.matmul(bank[:, :], ones[:, :], rstd[:, :], start=True, stop=True).then_inc(ss_done, 1)

            def first_units(ready, u, banks):
                def high(e, k):
                    nc.tensor.matmul(banks[e][:, :], wh[:, e, k, :], xh[:, k, :], start=(k == 0), stop=False)
                    nc.tensor.matmul(banks[e][:, :], wl[:, e, k, :], xh[:, k, :], start=False, stop=False)

                def low(e):
                    for k in range(KT):
                        pe.wait_ge(xl_done, ready * 8 + (k + 1))
                        mm = nc.tensor.matmul(banks[e][:, :], wh[:, e, k, :], xl[:, k, :], start=False,
                                              stop=(k == KT - 1))
                    mm.then_inc(unit_used, 1)

                pe.wait_ge(split_done, u + 1)
                for k in range(KT):
                    pe.wait_ge(xh_done, ready * 8 + (k + 1))
                    high(0, k)
                pe.wait_ge(split_done, u + 2)
                for k in range(4):
                    high(1, k)
                low(0)
                for k in range(4, KT):
                    high(1, k)
                low(1)

            def unit_blocks(u, slot, bank, ks, hi=xh, lo=xl):
                for k in ks:
                    if k == 0:
                        pe.wait_ge(split_done, u + 1)
                    mm = split_product(bank[:, :], slot, k, hi[:, k, :], lo[:, k, :], k == 0, k == KT - 1)
                if ks[-1] == KT - 1:
                    mm.then_inc(unit_used, 1)

            def feed_forward(n, prep, ready, u0):
                first_units(ready, u0, B[0:2])
                unit_blocks(u0 + 2, 0, B[2], range(4))
                sum_of_sums(prep, B[7])
                unit_blocks(u0 + 2, 0, B[2], range(4, KT))
                unit_blocks(u0 + 3, 1, B[3], range(KT))
                with pe.Fori(1, FT // 2) as i:
                    for j in range(4):
                        pe.wait_ge(gu_evac, i * 4 + (n * 2 * FT + (j - 3)))
                        unit_blocks(i * 4 + (u0 + j), j % 2, B[j], range(KT))

                def down(f, f0, at, first, last):
                    h, lo = acth[:, at, :], actl[:, at, :]
                    if not isinstance(at, int):
                        h, lo = h.rearrange("p a t -> p (a t)"), lo.rearrange("p a t -> p (a t)")
                    pe.wait_ge(act_done, f + 1 + n * FT)
                    pe.wait_ge(split_done, f + 1 + (u0 + 2 * FT))
                    for m in ((4, 5, 6, 7, 0, 1, 2, 3) if first else range(KT)):
                        if first and m == 0:
                            pe.wait_ge(gu_evac, (n + 1) * (2 * FT))
                        mm = split_product(B[m][:, :], f0 % 2, m, h, lo, first, last)
                        if last and m < KT - 1:
                            mm.then_inc(acc_done, 1)
                    mm.then_inc(unit_used, 1)

                down(0, 0, 0, True, False)
                down(1, 1, 1, False, False)
                with pe.Fori(1, FT // 2 - 1) as i:
                    for e in range(2):
                        down(i * 2 + e, e, bass.ds(i * 2 + e, 1), False, False)
                down(FT - 2, 0, FT - 2, False, False)
                down(FT - 1, 1, FT - 1, False, True)

            def mixer1(l):
                u0 = l * U_LAYER + U_FFN
                first_units(l * 3 + 1, u0, B[0:2])

                unit_blocks(u0 + 2, 0, B[6], range(4))
                sum_of_sums(l * 3 + 1, B[7])
                unit_blocks(u0 + 2, 0, B[6], range(4, KT))
                for n, bank in ((3, B[3]), (4, B[4])):
                    unit_blocks(u0 + n, n % 2, bank, range(KT))

                def turn_back(pair):
                    pe.wait_ge(otok_done, pair + 2)
                    for i in range(NQ):
                        tr = nc.tensor.transpose(B[6][:, i * P:(i + 1) * P],
                                                 otok[:, 2 * i:2 * i + 2, :].rearrange("p h d -> p (h d)"), ident[:, :])
                    tr.then_inc(ot_done, 1)

                def pair_steps(j, e, more):
                    pair = l * PAIRS + j
                    step0 = pair * 8
                    u = u0 + 5 + j * 3
                    slot = (1 + e) % 2
                    work = [(n, k) for n in range(3) for k in range(KT)] if more else []

                    def fill(count):
                        for n, k in [work.pop(0) for _ in range(count if more else 0)]:
                            if k == 0:
                                pe.wait_ge(proj_read, l * U_PROJ + j * 3 + (4 + n))
                            unit_blocks(u + n, (slot + n) % 2, B[(slot + n) % 2], [k])

                    def scores(s):
                        a, i = s // 4, P * (s % 4)
                        h = HD * a
                        if s == 0:
                            pe.wait_ge(qk_lo, pair * 4 + 4)
                        pe.wait_ge(t_done, step0 + (s + 1))
                        nc.tensor.matmul(B[(5, 2)[s % 2]][:, :], qs[:, e, a, i:i + P], ks[:, e, a, :],
                                         start=True, stop=False)
                        nc.tensor.matmul(B[(5, 2)[s % 2]][:, :], qs[h:h + HD, e, a, i:i + P], kl[h:h + HD, e, :],
                                         start=False, stop=True).then_inc(s_done, 1)

                    def turn(s):
                        pe.wait_ge(exp_done, step0 + (s + 1))
                        pe.wait_ge(pte_done, step0 + (s + 1))
                        for kt in range(NQ):
                            tr = nc.tensor.transpose(B[(3, 4)[s % 2]][:, kt * P:(kt + 1) * P],
                                                     sc[:, s % 4, kt * P:(kt + 1) * P], ident[:, :])
                        tr.then_inc(tr_done, 1)

                    def values(s):
                        a, i = s // 4, s % 4
                        if s == 0:
                            pe.wait_ge(vtok_done, pair + 1)
                            pe.wait_ge(otok_done, pair + 1)
                        pe.wait_ge(pte_done, step0 + (s + 3))
                        c = HD * (2 * i + a)
                        for kt in range(NQ):
                            mm = nc.tensor.matmul(B[7][:, c:c + HD], pt[:, s % 2, kt * P:(kt + 1) * P],
                                                  vtok[:, e, kt, HD * a:HD * (a + 1)],
                                                  start=(kt == 0), stop=(kt == NQ - 1))
                        mm.then_inc(pv_done, 1)

                    for s in range(8):
                        if s == 0:
                            fill(3)
                        scores(s)
                        if s > 0:
                            fill((3, 3, 3, 2, 2, 2, 1, 1)[s])
                        if s == 1:
                            pe.wait_ge(v_evac, pair + 1)
                            pe.wait_ge(ml_done, l * 8 + j + 1)
                            for kt in range(NQ):
                                tr = nc.tensor.transpose(B[6][:, kt * P:(kt + 1) * P],
                                                         vraw[:, kt * P:(kt + 1) * P], ident[:, :])
                            tr.then_inc(vt_done, 1)
                        if s in (2, 4) and not more:
                            t = s // 2 - 1
                            pe.wait_ge(pool_step, (l + 1) * POOL_OPS)
                            pe.wait_ge(proj_read, (l + 1) * U_PROJ)
                            pe.nop().then_inc(pe_turn, 1)
                            for h in (0, HD):
                                mm = nc.tensor.matmul(B[t][h:h + HD, :], poolw_now[h:h + HD, t, :],
                                                      padded[h:h + HD, t, PAD:PAD + T], start=True, stop=True)
                            mm.then_inc(poolmm_done, 1)
                        if s >= 2:
                            turn(s - 2)
                        if s >= 3:
                            values(s - 3)
                    fill(2)
                    turn(6)
                    values(5)
                    fill(2)
                    turn(7)
                    values(6)
                    fill(1)
                    values(7)
                    fill(2)
                    if more:
                        turn_back(pair)

                with pe.Fori(0, 2) as it:
                    for e in range(2):
                        pair_steps(it * 2 + e, e, True)
                pair_steps(4, 0, True)
                pair_steps(5, 1, False)

                def out_blocks(m, ks_):
                    unit_blocks(u0 + (U_PROJ + m), m % 2, B[m], ks_, mh1, ml1)

                pe.wait_ge(ml_done, l * 8 + 8)
                out_blocks(0, range(KT - 1))
                turn_back(l * PAIRS + 5)
                out_blocks(1, range(4))
                pe.wait_ge(ml_done, l * 8 + 9)
                out_blocks(0, [KT - 1])
                out_blocks(1, range(4, KT))
                for m in range(2, KT):
                    out_blocks(m, range(KT))

            with pe.Fori(0, DEPTH) as l:
                feed_forward(l * 2, l * 3, l * 3, l * U_LAYER)
                mixer1(l)
                feed_forward(l * 2 + 1, l * 3 + 2, l * 3 + 2, l * U_LAYER + (U_FFN + U_PROJ + U_OUT))

            for m in range(KT):
                square_sum(6, m, B[0])
            u0 = U_BLOCK2
            first_units(6, u0, B[4:6])

            def gate_products():
                pe.wait_ge(wg_done, 1)
                for k in range(KT):
                    o = B[0][0:NGATE, :]
                    nc.tensor.matmul(o, wgh[:, k, :], xh[:, k, :], start=(k == 0), stop=False)
                    nc.tensor.matmul(o, wgh[:, k, :], xl[:, k, :], start=False, stop=False)
                    mm = nc.tensor.matmul(o, wgl[:, k, :], xh[:, k, :], start=False, stop=(k == KT - 1))
                mm.then_inc(gate_mm, 1)

            def gate_turn():
                pe.wait_ge(gate_b, 1)
                pe.wait_ge(cmp_done, 3)
                for i in range(NQ):
                    tr = nc.tensor.transpose(B[0][:, NGATE * i:NGATE * (i + 1)], qall[0:NGATE, 0, i * P:(i + 1) * P],
                                             ident[0:NGATE, 0:NGATE])
                tr.then_inc(gate_tr, 1)

            def sum_squares2(n, src, bank):
                for t in range(4):
                    pe.wait_ge(sq2_done, 4 * n + t + 1)
                    mm = nc.tensor.matmul(bank[:, :], ones[:, :], src[:, t, :], start=(t == 0), stop=(t == 3))
                mm.then_inc(ss2_done, 1)

            def hidden(which, bank):
                pe.wait_ge(blk_done, 4 * which + 4)
                pe.wait_ge((w1k_in, w1v_in)[which], 16)
                for s in range(SLABS):
                    mm = nc.tensor.matmul(bank[0:NKV * NCMP, 0:CH], blk[:, which, s, :], w1[:, s, :],
                                          start=(s == 0), stop=(s == SLABS - 1))
                mm.then_inc(hid_mm, 1)

            def hidden_turn(which, bank):
                pe.wait_ge(hid_gelu, which + 1)
                for m in range(2):
                    tr = nc.tensor.transpose(bank[:, CH + HD * m:CH + HD * m + NKV * NCMP],
                                             hidt[0:NKV * NCMP, which, P * m:P * (m + 1)],
                                             ident[0:NKV * NCMP, 0:NKV * NCMP])
                tr.then_inc(hid_tr, 1)

            def compressed_keys():
                pe.wait_ge(hid_done, 1)
                for m in range(2):
                    mm = nc.tensor.matmul(B[2][:, 0:NKV * NCMP], w2k[:, m, :], hid[:, 0, m, :],
                                          start=(m == 0), stop=(m == 1))
                mm.then_inc(cmp_mm, 1)

            def compressed_values():
                pe.wait_ge(hid_done, 2)
                pe.wait_ge(gate_a, 1)
                for kv in range(NKV):
                    for m in range(2):
                        mm = nc.tensor.matmul(B[0][0:NCMP, HD * kv:HD * (kv + 1)],
                                              hid[:, 1, m, NCMP * kv:NCMP * (kv + 1)], w2v[:, m, :],
                                              start=(m == 0), stop=(m == 1))
                mm.then_inc(cmp_mm, 1)

            def gated_turn(t):
                pe.wait_ge(vn_done, t + 1)
                pe.wait_ge(hid_done, 2)
                if t >= 2:
                    pe.wait_ge(gt_done, t - 1)
                for c in range(NQ):
                    tr = nc.tensor.transpose(B[1 + 2 * (t % 2)][:, c * P:(c + 1) * P], gv[:, t, c * P:(c + 1) * P],
                                             ident[:, :])
                tr.then_inc(gt_mm, 1)

            def spatial(t):
                pe.wait_ge(gt_done, t + 1)
                pe.wait_ge(ws_done, 1)
                pe.wait_ge(gates_done, 1)
                if t >= 2:
                    pe.wait_ge(sv_add, t - 1)
                for h in range(2):
                    for c in range(NQ):
                        mm = nc.tensor.matmul(B[2 * (t % 2)][HD * h:HD * (h + 1), c * P:(c + 1) * P],
                                              gvtok[:, t, c, HD * h:HD * (h + 1)], wst[:, 2 * t + h, :],
                                              start=True, stop=True)
                mm.then_inc(sv_mm, 1)

            def token_values(n):
                pe.wait_ge(evac2, 13 + n)
                pe.wait_ge(gt_done, 3 + n)
                for kt in range(NQ):
                    tr = nc.tensor.transpose(B[1 + 2 * n][:, kt * P:(kt + 1) * P], vs2[:, n, kt * P:(kt + 1) * P],
                                             ident[:, :])
                tr.then_inc(v2_mm, 1)

            between = {
                3: [lambda: hidden(0, B[3])],
                5: [gate_products, lambda: hidden_turn(0, B[3])],
                7: [lambda: hidden(1, B[1]), lambda: pe.wait_ge(hid_done, 1), lambda: sum_squares2(0, oall, B[3])],
                8: [compressed_keys, lambda: hidden_turn(1, B[1])],
                9: [compressed_values, lambda: gated_turn(0), lambda: gated_turn(1)],
                10: [lambda: gated_turn(2), lambda: gated_turn(3), gate_turn],
                11: [lambda: spatial(0), lambda: spatial(1)],
                12: [lambda: spatial(2), lambda: spatial(3)],
                14: [lambda: pe.wait_ge(sv_add, 3), lambda: sum_squares2(1, oall, B[0]),
                     lambda: token_values(0), lambda: token_values(1)],
            }
            for n in range(2, U_PROJ2):
                if n >= 4:
                    pe.wait_ge(evac2, n - 3)
                unit_blocks(u0 + n, n % 2, B[4 + n % 4], range(4))
                if n == 2:
                    sum_of_sums(7, B[0])
                unit_blocks(u0 + n, n % 2, B[4 + n % 4], range(4, KT))
                for product in between.get(n, ()):
                    product()

            def turn2_(g, s):
                i = TILES2[s % 4]
                G = g * 16 + s
                pe.wait_ge(p2_done, G * 2 + 2)
                pe.wait_ge(pte2_done, G * 2 + 2)
                for c, bank in ((0, B[6]), (1, B[0])):
                    for kt in range(i + 1):
                        tr = nc.tensor.transpose(bank[:, kt * P:(kt + 1) * P], sc2[:, s % 4, c, kt * P:(kt + 1) * P],
                                                 ident[:, :])
                tr.then_inc(tr2_done, 1)

            def compressed_scores(g, hh):
                pe.wait_ge(cpt_done, g * 4 + (hh + 1))
                for i in range(NQ):
                    o = B[5][:, (NCMP + 1) * i:(NCMP + 1) * (i + 1)]
                    nc.tensor.matmul(o, qs2[:, hh, i * P:(i + 1) * P], kch[:, :], start=True, stop=False)
                    mm = nc.tensor.matmul(o, qs2[:, hh, i * P:(i + 1) * P], kcl[:, :], start=False, stop=True)
                mm.then_inc(cs_done, 1)

            def compressed_turn(g, hh):
                pe.wait_ge(cp_done, g * 4 + (hh + 1))
                for i in range(NQ):
                    tr = nc.tensor.transpose(B[5][0:NCMP, i * P:(i + 1) * P], scc[:, i, :], ident[:, :])
                tr.then_inc(ctr_done, 1)

            def values2(g, s):
                hh, i = s // 4, TILES2[s % 4]
                h = HD * (hh % 2)
                G = g * 16 + s
                if s % 8 == 0:
                    pe.wait_ge(o2_done, g * 2 + (s // 8 + 1))
                if s == 0:
                    pe.wait_ge(staged, (g + 1) * STAGED)
                if s % 4 == 0:
                    pe.wait_ge(cpt_done, g * 4 + (hh + 2))
                pe.wait_ge(pte2_done, G * 2 + 4)
                o = B[7][h:h + HD, i * P:(i + 1) * P]
                for c in range(2):
                    for kt in range(i + 1):
                        nc.tensor.matmul(o, vst[:, c, kt, :], pt2[:, s % 2, c, kt * P:(kt + 1) * P],
                                         start=(c == 0 and kt == 0), stop=False)
                nc.tensor.matmul(o, vcst[0:NCMP, :], ptc[0:NCMP, hh % 2, i * P:(i + 1) * P],
                                 start=False, stop=True).then_inc(pv2_done, 1)

            pe.wait_ge(mean2, 2)
            with pe.Fori(0, NKV) as g:
                pe.wait_ge(lo2_done, g * LOW_PARTS + 4)
                for s in range(16):
                    hh, i, par = s // 4, TILES2[s % 4], s % 2
                    n = P * (i + 1)
                    if s % 4 == 0 and s > 0:
                        pe.wait_ge(lo2_done, g * LOW_PARTS + (4 + hh))
                    pe.wait_ge(t2_done, g * 32 + (2 * s + 2))
                    for c in range(2):
                        o = B[1 + 2 * c + par][:, 0:n]
                        nc.tensor.matmul(o, qs2[:, hh, i * P:(i + 1) * P], kh2[:, c, 0:n], start=True, stop=False)
                        mm = nc.tensor.matmul(o, qs2[:, hh, i * P:(i + 1) * P], kl2[:, c, 0:n], start=False, stop=True)
                    mm.then_inc(s2_done, 1)
                    if s == 2:
                        compressed_turn(g, 0)
                    if s % 4 == 0:
                        compressed_scores(g, s // 4)
                    if s >= LAG2:
                        turn2_(g, s - LAG2)
                    if s >= LAG2 + 1:
                        values2(g, s - LAG2 - 1)
                    if s % 4 == 2 and s > 4:
                        compressed_turn(g, s // 4)
                for s in range(16, 17 + LAG2):
                    if s - LAG2 < 16:
                        turn2_(g, s - LAG2)
                    values2(g, s - LAG2 - 1)
            sum_squares2(2, gu, B[5])
            for m in range(2):
                unit_blocks(u0 + (U_PROJ2 + m), m % 2, B[m], range(4), mh2, ml2)
            for k in range(4, KT):
                pe.wait_ge(ml2_done, k + 1)
                unit_blocks(u0 + U_PROJ2, 0, B[0], [k], mh2, ml2)
            unit_blocks(u0 + (U_PROJ2 + 1), 1, B[1], range(4, KT), mh2, ml2)
            for m in range(2, KT):
                unit_blocks(u0 + (U_PROJ2 + m), m % 2, B[m], range(KT), mh2, ml2)
            feed_forward(4, 8, 7, u0 + (U_PROJ2 + U_OUT))
            for m in range(KT):
                square_sum(9, m, B[0])

        @block.scalar
        def _(act):
            for dst, name in ((gains, "gains"), (poolw, "poolw"), (poolscale, "poolscale")):
                act.dma_start(dst[tuple([slice(None)] * len(dst.shape))], d[name]).then_inc(gains_in, 16)
            for dst, name in ((ones, "c_ones"), (ident, "c_ident"), (gains2, "gains2"), (band, "c_band"),
                              (invcount, "c_invcount")):
                act.dma_start(dst[tuple([slice(None)] * len(dst.shape))], d[name]).then_inc(const_in, 16)
            act.nop().then_inc(pte_done, 2)
            act.nop().then_inc(pte2_done, 2)
            act.nop().then_inc(cpt_done, 1)

            def squares(prep, m):
                act.wait_ge(x_done, prep * 8 + (m + 1))
                act.wait_ge(sq_used, prep * 8 + (m + 1))
                nc.scalar.activation(sq[:, m % 4, :], x[:, m, :], ACT.Square).then_inc(sq_done, 1)

            def root(prep):
                act.wait_ge(mean_done, prep + 1)
                nc.scalar.activation(rstd[:, :], rstd[:, :], ACT.Sqrt).then_inc(root_done, 1)

            def prepare(prep, gains_of):
                for m in range(KT):
                    act.wait_ge(x_done, prep * 8 + (m + 1))
                    nc.scalar.activation(xh[:, m, :], x[:, m, :], ACT.Identity, scale=gains_of(m))\
                        .then_inc(xh_done, 1)
                for m in range(KT):
                    squares(prep, m)
                root(prep)

            def feed_forward(n):
                with act.Fori(0, FT // 2) as i:
                    for e in range(2):
                        act.wait_ge(gu_evac, i * 4 + (n * 2 * FT + (2 * e + 1)))
                        nc.scalar.activation(gn[:, e, :], gn[:, e, :], ACT.Silu).then_inc(silu_done, 1)

            def high_q(pair, e):
                act.wait_ge(rope_done, pair * 2 + 1)
                for a in range(2):
                    r = slice(HD * a, HD * (a + 1))
                    nc.scalar.activation(qs[r, e, a, :], qk[r, 0, :], ACT.Copy).then_inc(qk_hi, 1)

            def high_k(pair, e):
                act.wait_ge(rope_done, pair * 2 + 2)
                for a in range(2):
                    for b in (a, 1 - a):
                        nc.scalar.activation(ks[HD * b:HD * (b + 1), e, a, :], qk[HD * a:HD * (a + 1), 1, :], ACT.Copy)\
                            .then_inc(qk_hi, 1)

            def mixer1(l):
                high_q(l * PAIRS, 0)
                high_k(l * PAIRS, 0)

                def pair_steps(j, e, more):
                    pair = l * PAIRS + j
                    step0 = pair * 8

                    def copy_turn(s):
                        act.wait_ge(tr_done, step0 + (s + 5))
                        act.wait_ge(pv_done, step0 + (s + 1))
                        nc.scalar.activation(pt[:, s % 2, :], B[(3, 4)[s % 2]][:, :], ACT.Copy).then_inc(pte_done, 1)

                    for s in range(8):
                        if s >= 2:
                            copy_turn(s - 2)
                        act.wait_ge(neg_done, step0 + (s + 1))
                        c = 2 * (s % 4) + s // 4
                        nc.scalar.activation(sc[:, s % 4, :], sc[:, s % 4, :], ACT.Exp, bias=sneg[:, s:s + 1],
                                             scale=SCALE, accum_out=sden[:, c:c + 1]).then_inc(exp_done, 1)
                        if s == 2:
                            act.wait_ge(vt_done, pair + 1)
                            nc.scalar.activation(vtok[:, e, :, :], B[6][:, :].rearrange("p (k n) -> p k n", k=NQ),
                                                 ACT.Copy).then_inc(vtok_done, 1)
                        if s == 5 and more:
                            high_q(pair + 1, 1 - e)
                        if s in (3, 5) and not more:
                            t = (s - 3) // 2
                            act.wait_ge(poolmm_done, l * 2 + (t + 1))
                            nc.scalar.activation(mh1[:, t, :], B[t][:, :], ACT.Identity,
                                                 scale=poolscale_now[:, t:t + 1]).then_inc(mh_done, 1)
                    copy_turn(6)
                    if more:
                        high_k(pair + 1, 1 - e)
                    copy_turn(7)
                    act.wait_ge(ot_done, pair + 1)

                with act.Fori(0, 2) as it:
                    for e in range(2):
                        pair_steps(it * 2 + e, e, True)
                        act.nop().then_inc(out_turn, 1)
                        nc.scalar.activation(mh1[:, bass.ds(it * 2 + (2 + e), 1), :].rearrange("p a t -> p (a t)"),
                                             B[6][:, :], ACT.Copy).then_inc(mh_done, 1)
                for j in (4, 5):
                    pair_steps(j, j % 2, j == 4)
                    nc.scalar.activation(mh1[:, 2 + j, :], B[6][:, :], ACT.Copy).then_inc(mh_done, 1)

            act.wait_ge(trig, 4)
            nc.scalar.activation(sin[:, :], sin[:, :], ACT.Sin).then_inc(trig_act, 1)
            act.wait_ge(trig, 7)
            nc.scalar.activation(cos[:, :], cos[:, :], ACT.Sin).then_inc(trig_act, 1)

            with act.Fori(0, DEPTH) as l:
                act.wait_ge(layer_set, (l + 1) * LAYER_COPIES)
                prepare(l * 3, lambda m: gain[:, 0, m:m + 1])
                feed_forward(l * 2)
                prepare(l * 3 + 1, lambda m: gain[:, 1, m:m + 1])
                mixer1(l)
                prepare(l * 3 + 2, lambda m: gain[:, 2, m:m + 1])
                feed_forward(l * 2 + 1)

            for m in range(KT):
                squares(6, m)
            root(6)
            prepare(7, lambda m: gains2[:, 1, m:m + 1])

            def gelu(n, buf):
                act.wait_ge(gelu_in, n + 1)
                nc.scalar.activation(buf, buf, ACT.Gelu_apprx_tanh).then_inc(gelu_done, 1)

            def root_of(n):
                act.wait_ge(mean2, n + 1)
                nc.scalar.activation(rstd2[:, :], rstd2[:, :], ACT.Sqrt).then_inc(root2, 1)

            def hidden(which, bank):
                act.wait_ge(hid_mm, which + 1)
                nc.scalar.activation(hidt[0:NKV * NCMP, which, :], bank[0:NKV * NCMP, 0:CH], ACT.Gelu_apprx_tanh)\
                    .then_inc(hid_gelu, 1)

            def hidden_copy(which, bank):
                act.wait_ge(hid_tr, which + 1)
                nc.scalar.activation(hid[:, which, :, :],
                                     bank[:, CH:CH + 2 * HD].rearrange("p (m n) -> p m n", m=2)[:, :, 0:NKV * NCMP],
                                     ACT.Copy).then_inc(hid_done, 1)

            gelu(0, gv[:, 0, :])
            hidden(0, B[3])
            for t in range(1, 4):
                gelu(t, gv[:, t, :])
            for t in range(4):
                act.wait_ge(gelu_done, t + 1)
                nc.scalar.activation(oall[:, t, :], gv[:, t, :], ACT.Square).then_inc(sq2_done, 1)
            hidden_copy(0, B[3])
            gelu(4, gu[:, 0, :])
            gelu(5, gu[:, 1, :])
            hidden(1, B[1])
            root_of(0)
            gelu(6, gu[:, 2, :])
            hidden_copy(1, B[1])
            gelu(7, gu[:, 3, :])
            act.wait_ge(gate_a, 1)
            nc.scalar.activation(qall[0:NGATE, 0, :], qall[0:NGATE, 0, :], ACT.Sigmoid, bias=gateb[:, 0:1])\
                .then_inc(gate_b, 1)
            for t in range(4):
                act.wait_ge(gt_mm, t + 1)
                nc.scalar.activation(gvtok[:, t, :, :], B[1 + 2 * (t % 2)][:, :].rearrange("p (c n) -> p c n", c=NQ),
                                     ACT.Copy).then_inc(gt_done, 1)
            def normed(n, src, scratch, base):
                for t in range(4):
                    if n == 1:
                        act.wait_ge(a_done, t + 1)
                    nc.scalar.activation(scratch[:, t, :], src[:, t, :], ACT.Square).then_inc(sq2_done, 1)
                if n == 1:
                    for c in range(2):
                        act.wait_ge(v2_mm, c + 1)
                        nc.scalar.activation(vall[:, c, :, :], B[1 + 2 * c][:, :].rearrange("p (k n) -> p k n", k=NQ),
                                             ACT.Copy).then_inc(v2_done, 1)
                root_of(n)
                for t in range(4):
                    act.wait_ge(norm_mul, 4 * (n - 1) + t + 1)
                    nc.scalar.activation(mh2[:, base + t, :], src[:, t, :], ACT.Copy).then_inc(mh2_done, 1)

            normed(1, gu, oall, 0)

            def copy_turn2(g, s):
                G = g * 16 + s
                n = P * (TILES2[s % 4] + 1)
                act.wait_ge(tr2_done, G + 5)
                act.wait_ge(pv2_done, G + 1)
                for c, bank in ((0, B[6]), (1, B[0])):
                    nc.scalar.activation(pt2[:, s % 2, c, 0:n], bank[:, 0:n], ACT.Copy).then_inc(pte2_done, 1)

            def compressed_exp(g, hh):
                act.wait_ge(ct_done, g * 4 + (hh + 1))
                nc.scalar.activation(scc[:, :, :], scc[:, :, :], ACT.Exp, scale=SCALE).then_inc(ce_done, 1)

            def compressed_copy(g, hh):
                act.wait_ge(ctr_done, g * 4 + (hh + 2))
                if hh >= 2:
                    act.wait_ge(pv2_done, g * 16 + (4 * (hh - 1) + 2))
                nc.scalar.activation(ptc[0:NCMP, hh % 2, :], B[5][0:NCMP, :], ACT.Copy).then_inc(cpt_done, 1)

            with act.Fori(0, NKV) as g:
                act.wait_ge(evac2, 12)
                act.wait_ge(cmp_done, 3)
                act.wait_ge(t2_done, g * 32 + 4)
                act.nop().then_inc(stage_open, 1)
                nc.scalar.activation(kch[:, :], kcall[:, bass.ds(g, 1), :].rearrange("p a t -> p (a t)"), ACT.Copy)\
                    .then_inc(hi2_done, 1)
                for n in range(2):
                    nc.scalar.activation(kh2[:, n, :], kdup[:, n, bass.ds(g, 1), :].rearrange("p a t -> p (a t)"),
                                         ACT.Copy).then_inc(hi2_done, 1)
                for hd in range(4):
                    r = slice(HD * (hd % 2), HD * (hd % 2 + 1))
                    if hd % 2 == 0:
                        act.wait_ge(evac2, 15 + hd // 2)
                    nc.scalar.activation(qs2[r, hd, :], qall[r, bass.ds(g * 2 + hd // 2, 1), :]
                                         .rearrange("p a t -> p (a t)"), ACT.Copy).then_inc(hi2_done, 1)
                for s in range(16):
                    n = P * (TILES2[s % 4] + 1)
                    if s >= LAG2:
                        copy_turn2(g, s - LAG2)
                    act.wait_ge(neg2_done, g * 16 + (s + 1))
                    for c in range(2):
                        src = sc2[:, s % 4, c, 0:n]
                        nc.scalar.activation(src, src, ACT.Exp, bias=sneg2[:, s % 2, c:c + 1], scale=SCALE,
                                             accum_out=sden2[:, s % 2, c:c + 1]).then_inc(exp2_done, 1)
                    if s == 0:
                        compressed_exp(g, 0)
                    if s == 2:
                        compressed_copy(g, 0)
                    if s % 4 == 1 and s > 4:
                        compressed_exp(g, s // 4)
                    if s % 4 == 3 and s > 4:
                        compressed_copy(g, s // 4)
                for s in range(16 - LAG2, 16):
                    copy_turn2(g, s)
            act.wait_ge(o2_done, 5)
            normed(2, oall, gu, 4)
            prepare(8, lambda m: gains2[:, 2, m:m + 1])
            feed_forward(4)
            for m in range(KT):
                squares(9, m)
            root(9)

        @block.vector
        def _(dve):
            V = nc.vector
            dve.nop().then_inc(t_done, 2)
            dve.nop().then_inc(ml_done, 1)
            dve.nop().then_inc(otok_done, 1)
            dve.nop().then_inc(sq_used, 4)
            dve.nop().then_inc(t2_done, 4)
            dve.nop().then_inc(o2_done, 1)

            dve.wait_ge(pos_in, 32)
            TURN = 6.283185307179586
            C1 = 6.28125
            C2 = 2029 / 2 ** 20
            C3 = TURN - C1 - C2
            MAGIC = 12582912.0
            PI = 3.1415925
            a, k = sin, cos
            V.tensor_copy(a[:, :], posi[:, :]).then_inc(trig, 1)
            dve.wait_ge(trig, 1)
            V.tensor_scalar(a[:, :], a[:, :], ropecol[:, 0:1], None, ALU.mult).then_inc(trig, 1)
            dve.wait_ge(trig, 2)
            V.tensor_scalar(k[:, :], a[:, :], 1.0 / TURN, MAGIC, ALU.mult, ALU.add).then_inc(tables_done, 1)
            dve.wait_ge(tables_done, 1)
            V.tensor_scalar(k[:, :], k[:, :], -MAGIC, None, ALU.add).then_inc(tables_done, 1)
            for n, c in enumerate((C1, C2, C3)):
                dve.wait_ge(tables_done, 2 + n)
                V.scalar_tensor_tensor(a[:, :], k[:, :], -c, a[:, :], ALU.mult, ALU.add).then_inc(tables_done, 1)
            dve.wait_ge(tables_done, 5)
            V.tensor_scalar(a[:, :], a[:, :], PI, -PI, ALU.min, ALU.max).then_inc(trig, 1)
            dve.wait_ge(trig, 3)
            V.tensor_scalar(k[:, :], a[:, :], TURN / 4, None, ALU.add).then_inc(trig, 1)
            dve.wait_ge(trig, 4)
            V.tensor_scalar(cosr[:, :], k[:, :], PI, -TURN, ALU.is_gt, ALU.mult).then_inc(trig, 1)
            dve.wait_ge(trig, 5)
            V.tensor_tensor(k[:, :], k[:, :], cosr[:, :], ALU.add).then_inc(trig, 1)
            dve.wait_ge(trig, 6)
            V.tensor_scalar(k[:, :], k[:, :], PI, -PI, ALU.min, ALU.max).then_inc(trig, 1)
            for half in range(2):
                dve.wait_ge(x_in[half], 16)
                dve.nop().then_inc(x_done, KT // 2)
            dve.wait_ge(gains_in, 16 * 3)
            dve.wait_ge(trig_act, 2)
            V.tensor_scalar(cos[:, :], cos[:, :], ropecol[:, 1:2], ropecol[:, 2:3], ALU.mult, ALU.add)\
                .then_inc(tables_done, 1)
            V.tensor_scalar(sin[:, :], sin[:, :], ropecol[:, 3:4], None, ALU.mult).then_inc(tables_done, 1)
            dve.wait_ge(tables_done, 7)

            def inverse_rms(prep, bank):
                V.tensor_scalar(rstd[:, :], bank[:, :], 1.0 / D, EPS, ALU.mult, ALU.add).then_inc(mean_done, 1)
                dve.wait_ge(root_done, prep + 1)
                V.reciprocal(rstd[:, :], rstd[:, :]).then_inc(rstd_done, 1)
                dve.wait_ge(rstd_done, prep + 1)

            def norm(prep, number, bank):
                dve.wait_ge(sq_done, prep * 8 + 2)
                V.tensor_tensor(rstd[:, :], sq[:, 0, :], sq[:, 1, :], ALU.add).then_inc(sq_used, 2)
                for m in range(2, KT):
                    dve.wait_ge(sq_done, prep * 8 + (m + 1))
                    dve.wait_ge(sq_used, prep * 8 + (m + 4))
                    V.tensor_tensor(rstd[:, :], rstd[:, :], sq[:, m % 4, :], ALU.add).then_inc(sq_used, 1)
                dve.wait_ge(ss_done, number + 1)
                inverse_rms(prep, bank)

            def low_part(ready, m, g):
                dve.wait_ge(xh_done, ready * 8 + (m + 1))
                V.scalar_tensor_tensor(xl[:, m, :], x[:, m, :], g, xh[:, m, :].bitcast(F32), ALU.mult, ALU.subtract)\
                    .then_inc(xl_done, 1)

            def update(m, factor, sem_, value):
                dve.wait_ge(sem_, value)
                V.scalar_tensor_tensor(x[:, m, :], B[m][:, :], factor, x[:, m, :], ALU.mult, ALU.add)\
                    .then_inc(x_done, 1)

            def updates(factor, done, ready=None, g=None, behind=KT):
                for m in range(KT + behind):
                    if m < KT:
                        update(m, factor, *done(m))
                    if g is not None and m >= behind:
                        low_part(ready, m - behind, g(m - behind))

            def feed_forward(n):
                def evacuate(f, e):
                    if not isinstance(f, int):
                        dve.wait_ge(act_done, f + (n * FT - 1))
                    for j, dst in ((0, gn), (1, un)):
                        dve.wait_ge(unit_used, f * 2 + (ffn_unit[0] + (j + 3)))
                        V.tensor_tensor(dst[:, e, :], B[2 * e + j][:, :], rstd[:, :], ALU.mult)\
                            .then_inc(gu_evac, 1)

                def finish(f, e, at):
                    h, lo = acth[:, at, :], actl[:, at, :]
                    if not isinstance(at, int):
                        h, lo = h.rearrange("p a t -> p (a t)"), lo.rearrange("p a t -> p (a t)")
                    dve.wait_ge(gu_evac, f * 2 + (n * 2 * FT + 2))
                    dve.wait_ge(silu_done, f + (n * FT + 1))
                    V.tensor_tensor(h, gn[:, e, :], un[:, e, :], ALU.mult).then_inc(act_part, 1)
                    V.tensor_tensor(un[:, e, :], gn[:, e, :], un[:, e, :], ALU.mult).then_inc(act_part, 1)
                    dve.wait_ge(act_part, f * 2 + (n * 2 * FT + 2))
                    V.tensor_tensor(lo, un[:, e, :], h.bitcast(F32), ALU.subtract).then_inc(act_done, 1)

                evacuate(0, 0)
                evacuate(1, 1)
                finish(0, 0, 0)
                with dve.Fori(1, FT // 2) as i:
                    evacuate(i * 2, 0)
                    finish(i * 2 - 1, 1, bass.ds(i * 2 - 1, 1))
                    evacuate(i * 2 + 1, 1)
                    finish(i * 2, 0, bass.ds(i * 2, 1))
                finish(FT - 1, 1, FT - 1)

            ffn_unit = [0]

            def down_done(n, u0):
                return lambda m: (acc_done, n * 7 + (m + 1)) if m < KT - 1 else (unit_used, u0 + (U_FFN + 2))

            def mixer1(l):
                u0 = l * U_LAYER + U_FFN
                dve.wait_ge(const_in, 16 * N_CONST)
                V.tensor_tensor(cosr[:, :], cos[:, :], rstd[:, :], ALU.mult).then_inc(pool_step, 1)
                V.tensor_tensor(sinr[:, :], sin[:, :], rstd[:, :], ALU.mult).then_inc(pool_step, 1)
                ps = l * POOL_OPS
                dve.wait_ge(pool_step, ps + 4)

                def rope(pair, which, u, bank, part=None):
                    n = pair * 2 + which
                    if part != 1:
                        dve.wait_ge(unit_used, u + 3)
                        V.tensor_tensor(ropet[:, 1, :], bank[:, :], cosr[:, :], ALU.mult).then_inc(rope_a, 1)
                    for a in {None: range(4), 0: (0, 1), 1: (2, 3)}[part]:
                        b = a ^ 1
                        V.tensor_tensor(ropet[32 * b:32 * b + 32, 0, :], bank[32 * a:32 * a + 32, :],
                                        sinr[32 * a:32 * a + 32, :], ALU.mult).then_inc(rope_a, 1)
                    if part != 0:
                        dve.wait_ge(rope_a, n * ROPE_READS + ROPE_READS)
                        dve.nop().then_inc(proj_read, 1)
                        V.tensor_tensor(qk[:, which, :], ropet[:, 0, :], ropet[:, 1, :], ALU.add)\
                            .then_inc(rope_done, 1)
                        dve.wait_ge(rope_done, n + 1)

                def low_q(pair, e):
                    dve.wait_ge(qk_hi, pair * 6 + 2)
                    for a in range(2):
                        r, o = slice(HD * a, HD * (a + 1)), slice(HD * (1 - a), HD * (2 - a))
                        V.tensor_tensor(qs[o, e, a, :], qk[r, 0, :], qs[r, e, a, :].bitcast(F32), ALU.subtract)\
                            .then_inc(qk_lo, 1)
                    dve.wait_ge(qk_lo, pair * 4 + 2)

                def low_k(pair, e):
                    dve.wait_ge(qk_hi, pair * 6 + 6)
                    for a in range(2):
                        r = slice(HD * a, HD * (a + 1))
                        V.tensor_tensor(kl[r, e, :], qk[r, 1, :], ks[r, e, a, :].bitcast(F32), ALU.subtract)\
                            .then_inc(qk_lo, 1)
                    dve.wait_ge(qk_lo, pair * 4 + 4)

                def v_out(pair, u, bank):
                    dve.wait_ge(unit_used, u + 3)
                    V.tensor_tensor(vraw[:, :], bank[:, :], rstd[:, :], ALU.mult).then_inc(v_evac, 1)
                    dve.wait_ge(v_evac, pair + 1)
                    dve.nop().then_inc(proj_read, 1)

                rope(l * PAIRS, 0, u0, B[0])
                rope(l * PAIRS, 1, u0 + 1, B[1])
                v_out(l * PAIRS, u0 + 2, B[6])
                for t in range(2):
                    dve.wait_ge(unit_used, u0 + (t + 6))
                    V.tensor_tensor(padded[:, t, PAD:PAD + T], B[3 + t][:, :], rstd[:, :], ALU.mult)\
                        .then_inc(pool_evac, 1)
                dve.wait_ge(pool_evac, l * 2 + 2)
                dve.nop().then_inc(proj_read, 2)
                low_q(l * PAIRS, 0)
                low_k(l * PAIRS, 0)
                dve.nop().then_inc(dve_turn, 1)

                E = PAD + T + PAD
                low, high = slice(0, HD), slice(HD, P)
                inner = slice(PAD, PAD + T)
                add, mul, sub = ALU.add, ALU.mult, ALU.subtract
                pool_ops = [
                    (4, win[:, :, 1:E], padded[:, :, 0:E - 1], padded[:, :, 1:E], add),
                    (5, win16[:, PAD - 6:PAD + T + 6], win[:, 1, PAD - 7:PAD + T + 5],
                     win[:, 1, PAD - 5:PAD + T + 7], add),
                    (6, win[high, 1, inner], win[high, 0, PAD - 1:PAD + T - 1],
                     win[high, 0, PAD + 1:PAD + T + 1], add),
                    (7, win[high, 0, inner], win[high, 1, inner], invcount[high, 0, :], mul),
                    (7, win[low, 0, inner], win[low, 0, inner], invcount[low, 0, :], mul),
                    (9, win[:, 1, PAD - 4:PAD + T + 4], win16[:, PAD - 6:PAD + T + 2],
                     win16[:, PAD - 2:PAD + T + 6], add),
                    (10, win16[high, inner], win[high, 1, PAD - 4:PAD + T - 4],
                     win[high, 1, PAD + 4:PAD + T + 4], add),
                    (10, win[low, 1, inner], win[low, 1, inner], invcount[low, 1, :], mul),
                    (12, win[high, 1, inner], win16[high, inner], invcount[high, 1, :], mul),
                    (13, padded[:, :, inner], win[:, :, inner], padded[:, :, inner], sub),
                ]

                def pair_steps(j, e, more, pooled=False):
                    pair = l * PAIRS + j
                    step0 = pair * 8
                    u = u0 + 5 + j * 3
                    slot = (1 + e) % 2

                    for s in range(8):
                        i = s % 4
                        dve.wait_ge(s_done, step0 + (s + 1))
                        dve.wait_ge(tr_done, step0 + (s + 1))
                        dve.nop().then_inc(dve_turn, 1)
                        off = 384 - P * i
                        V.tensor_tensor_reduce(sc[:, s % 4, :], B[(5, 2)[s % 2]][:, :], band[:, off:off + T], 1.0,
                                               -3.0e38, ALU.add, ALU.max, smax[:, s:s + 1]).then_inc(t_done, 1)
                        dve.wait_ge(t_done, step0 + (s + 3))
                        V.tensor_scalar(sneg[:, s:s + 1], smax[:, s:s + 1], -SCALE, None, ALU.mult)\
                            .then_inc(neg_done, 1)
                        if s in (3, 4) and more:
                            rope(pair + 1, 0, u, B[slot], s - 3)
                        if s == 6 and more:
                            low_q(pair + 1, 1 - e)
                        if s == 7 and more:
                            rope(pair + 1, 1, u + 1, B[1 - slot], 0)
                        for n in range(len(pool_ops) * s // 8, len(pool_ops) * (s + 1) // 8) if pooled else ():
                            after, o, in0, in1, op = pool_ops[n]
                            dve.wait_ge(pool_step, ps + after)
                            V.tensor_tensor(o, in0, in1, op).then_inc(pool_step, 1)
                        if s in (4, 6) and not more:
                            t = s // 2 - 2
                            dve.wait_ge(mh_done, l * 8 + (t + 6))
                            V.scalar_tensor_tensor(ml1[:, t, :], B[t][:, :], poolscale_now[:, t:t + 1],
                                                   mh1[:, t, :].bitcast(F32), ALU.mult, ALU.subtract)\
                                .then_inc(ml_done, 1)
                    if more:
                        rope(pair + 1, 1, u + 1, B[1 - slot], 1)
                        low_k(pair + 1, 1 - e)
                    dve.wait_ge(exp_done, step0 + 8)
                    dve.wait_ge(otok_done, pair + 1)
                    V.reciprocal(srec[:, :], sden[:, :]).then_inc(rec_done, 1)
                    dve.wait_ge(rec_done, pair + 1)
                    dve.wait_ge(pv_done, step0 + 10)
                    V.tensor_tensor(otok[:, :, :], B[7][:, :].rearrange("p (c d) -> p c d", c=8),
                                    srec[:, :].rearrange("p (c a) -> p c a", a=1).to_broadcast([P, 8, HD]), ALU.mult)\
                        .then_inc(otok_done, 1)
                    if more:
                        v_out(pair + 1, u + 2, B[slot])

                def output(done, at):
                    h, lo = mh1[:, at, :], ml1[:, at, :]
                    if not isinstance(at, int):
                        h, lo = h.rearrange("p a t -> p (a t)"), lo.rearrange("p a t -> p (a t)")
                    dve.wait_ge(mh_done, done)
                    V.tensor_tensor(lo, B[6][:, :], h.bitcast(F32), ALU.subtract).then_inc(ml_done, 1)

                with dve.Fori(0, 2) as it:
                    for e in range(2):
                        pair_steps(it * 2 + e, e, True)
                        output(l * 8 + it * 2 + (e + 1), bass.ds(it * 2 + (2 + e), 1))
                pair_steps(4, 0, True, True)
                output(l * 8 + 5, 6)
                pair_steps(5, 1, False)
                output(l * 8 + 8, 7)

            with dve.Fori(0, DEPTH) as l:
                V.tensor_copy(gain[:, :, :], gains[:, bass.ds(l, 1), :, :].rearrange("p a n k -> p (a n) k"))\
                    .then_inc(layer_set, 1)
                V.tensor_copy(poolw_now[:, :, :], poolw[:, bass.ds(l, 1), :, :].rearrange("p a n k -> p (a n) k"))\
                    .then_inc(layer_set, 1)
                V.tensor_copy(poolscale_now[:, :], poolscale[:, bass.ds(l, 1), :].rearrange("p a n -> p (a n)"))\
                    .then_inc(layer_set, 1)
                dve.wait_ge(layer_set, (l + 1) * LAYER_COPIES)
                for m in range(KT):
                    low_part(l * 3, m, gain[:, 0, m:m + 1])
                norm(l * 3, l * 3, B[7])
                ffn_unit[0] = l * U_LAYER
                feed_forward(l * 2)
                updates(0.5, down_done(l * 2, l * U_LAYER), l * 3 + 1, lambda m: gain[:, 1, m:m + 1])
                V.memset(padded[:, :, :], 0.0).then_inc(pool_step, 1)
                V.memset(win[:, :, :], 0.0).then_inc(pool_step, 1)
                norm(l * 3 + 1, l * 3 + 1, B[7])
                mixer1(l)
                uo = l * U_LAYER + (U_FFN + U_PROJ)
                updates(1.0, lambda m: (unit_used, uo + (m + 3)), l * 3 + 2, lambda m: gain[:, 2, m:m + 1], 1)
                norm(l * 3 + 2, l * 3 + 2, B[7])
                ffn_unit[0] = l * U_LAYER + (U_FFN + U_PROJ + U_OUT)
                feed_forward(l * 2 + 1)
                updates(0.5, down_done(l * 2 + 1, l * U_LAYER + (U_FFN + U_PROJ + U_OUT)))

            dve.wait_ge(sq_used, 7 * 8 + 4)
            inverse_rms(6, B[0])
            for m in range(KT):
                V.scalar_tensor_tensor(x[:, m, :], x[:, m, :], gains2[:, 0, m:m + 1], rstd[:, :], ALU.mult, ALU.mult)\
                    .then_inc(x_done, 1)
            for m in range(KT):
                dve.wait_ge(x_done, 8 * 7 + m + 1)
                low_part(6, m, gains2[:, 1, m:m + 1])
            norm(7, 6, B[0])
            u0 = U_BLOCK2
            dve.wait_ge(const2_in, 16 * N_CONST2)
            V.tensor_copy(wgh[:, :, :], wg[:, :, :]).then_inc(wg_part, 1)
            dve.wait_ge(wg_part, 1)
            V.tensor_tensor(wgl[:, :, :], wg[:, :, :], wgh[:, :, :].bitcast(F32), ALU.subtract).then_inc(wg_done, 1)
            V.tensor_tensor(wst[:, :, :], wst[:, :, :],
                            causal[:, :].rearrange("p (a n) -> p a n", a=1).to_broadcast([P, 8, P]), ALU.mult)\
                .then_inc(ws_done, 1)

            def bank(n):
                dve.wait_ge(unit_used, u0 + n + 3)
                return B[4 + n % 4]

            def scaled(n, dst, last):
                V.tensor_tensor(dst, bank(n)[:, :], rstd[:, :], ALU.mult).then_inc(last, 1)

            def inverse_rms2(n, b, width):
                dve.wait_ge(ss2_done, n + 1)
                V.tensor_scalar(rstd2[:, :], b[:, :], 1.0 / width, EPS, ALU.mult, ALU.add).then_inc(mean2, 1)
                dve.wait_ge(root2, n + 1)
                V.reciprocal(rstd2[:, :], rstd2[:, :]).then_inc(rstd2_done, 1)
                dve.wait_ge(rstd2_done, n + 1)

            def normalised_v():
                inverse_rms2(0, B[3], 512)
                for t in range(4):
                    dve.wait_ge(sq2_done, t + 1)
                    V.scalar_tensor_tensor(gv[:, t, :], gv[:, t, :], vec2[:, 0, t:t + 1], rstd2[:, :],
                                           ALU.mult, ALU.mult).then_inc(vn_done, 1)

            def gate_sums():
                dve.wait_ge(gate_mm, 1)
                V.tensor_tensor(qall[0:NGATE, 0, :], B[0][0:NGATE, :], rstd[0:NGATE, :], ALU.mult).then_inc(gate_a, 1)

            def gate_columns():
                dve.wait_ge(gate_tr, 1)
                V.tensor_copy(gates[:, :, :], B[0][:, 0:NQ * NGATE].rearrange("p (i n) -> p i n", i=NQ))\
                    .then_inc(gates_done, 1)

            def compressed_keys():
                dve.wait_ge(cmp_mm, 1)
                V.memset(kcall[:, :, NCMP:NCMP + 1], 0.0).then_inc(cmp_done, 1)
                V.tensor_copy(kcall[:, :, 0:NCMP], B[2][:, 0:NKV * NCMP].rearrange("p (a n) -> p a n", a=NKV))\
                    .then_inc(cmp_done, 1)

            def compressed_values():
                dve.wait_ge(cmp_mm, 2)
                V.tensor_copy(vcall[0:NCMP, :, :], B[0][0:NCMP, 0:NKV * HD].rearrange("p (a n) -> p a n", a=NKV))\
                    .then_inc(cmp_done, 1)

            def gated(t):
                dve.wait_ge(gelu_done, 8)
                dve.wait_ge(sv_mm, t + 1)
                if t >= 2:
                    dve.wait_ge(a_done, t - 1)
                V.tensor_tensor(svt(t), B[2 * (t % 2)][:, :].rearrange("p (c n) -> p c n", c=NQ),
                                bsb[:, t:t + 1, :].to_broadcast([P, NQ, P]), ALU.add).then_inc(sv_add, 1)
                dve.wait_ge(sv_add, t + 1)
                V.tensor_tensor(gu[:, t, :], gu[:, t, :], shifted[:, t % 2, :], ALU.mult).then_inc(a_done, 1)

            def normed(n, src, base):
                for t in range(4):
                    V.scalar_tensor_tensor(src[:, t, :], src[:, t, :], vec2[:, n, t:t + 1], rstd2[:, :],
                                           ALU.mult, ALU.mult).then_inc(norm_mul, 1)
                for t in range(4):
                    dve.wait_ge(norm_mul, 4 * (n - 1) + t + 1)
                    dve.wait_ge(mh2_done, 4 * (n - 1) + t + 1)
                    V.tensor_tensor(ml2[:, base + t, :], src[:, t, :], mh2[:, base + t, :].bitcast(F32), ALU.subtract)\
                        .then_inc(ml2_done, 1)

            beside = {
                6: [gate_sums], 7: [normalised_v], 9: [compressed_keys], 10: [compressed_values, gate_columns],
                11: [lambda: gated(0)], 12: [lambda: gated(1)], 13: [lambda: gated(2), lambda: gated(3)],
                15: [lambda: inverse_rms2(1, B[0], 512), lambda: normed(1, gu, 0)],
            }
            halves = [0]
            for n in range(U_PROJ2):
                if 2 <= n < 6:
                    scaled(n, gv[:, n - 2, :], gelu_in)
                    dve.wait_ge(gelu_in, n - 1)
                elif n < 2:
                    which = n
                    b = bank(n)
                    if which:
                        dve.wait_ge(blk_done, 4)
                    for kv in range(NKV):
                        r = slice(HD * kv, HD * kv + HD)
                        V.tensor_tensor(shifted[0:HD, kv, :], b[r, :], rstd[0:HD, :], ALU.mult).then_inc(shift_done, 1)
                        V.tensor_tensor(shifted[HD:P, kv, 0:T - 1], b[r, 1:T], rstd[HD:P, 1:T], ALU.mult)\
                            .then_inc(shift_done, 1)
                    dve.wait_ge(shift_done, 4 * which + 4)
                    for kv in range(NKV):
                        v = shifted[:, kv, :].rearrange("p (n s two) -> p s n two", s=8, two=2)
                        for half in range(2):
                            V.tensor_tensor(blk[:, which, 8 * half:8 * half + 8, NCMP * kv:NCMP * (kv + 1)],
                                            v[:, :, half:half + NCMP, 0],
                                            poscol[:, which, 8 * half:8 * half + 8]
                                            .rearrange("p (s a) -> p s a", a=1).to_broadcast([P, 8, NCMP]), ALU.add)\
                                .then_inc(blk_done, 1)
                elif 10 <= n < 12:
                    b = bank(n)
                    for kv in range(NKV):
                        for half in range(2):
                            V.tensor_tensor(kdup[HD * half:HD * half + HD, n - 10, kv, :],
                                            b[HD * kv:HD * kv + HD, :], rstd[HD * half:HD * half + HD, :], ALU.mult)\
                                .then_inc(half2, 1)
                            halves[0] += 1
                    dve.wait_ge(half2, halves[0])
                elif 12 <= n < 14:
                    scaled(n, vs2[:, n - 12, :], half2)
                    halves[0] += 1
                    dve.wait_ge(half2, halves[0])
                elif n >= 14:
                    scaled(n, qall[:, n - 14, :], half2)
                    halves[0] += 1
                    dve.wait_ge(half2, halves[0])
                else:
                    scaled(n, gu[:, n - 6, :], gelu_in)
                    dve.wait_ge(gelu_in, n - 1)
                dve.nop().then_inc(evac2, 1)
                for work in beside.get(n, ()):
                    work()


            dve.wait_ge(gates_done, 1)
            dve.wait_ge(cmp_done, 3)
            dve.wait_ge(v2_done, 2)
            def wide(v):
                return v.rearrange("p (i a) -> p i a", a=1).to_broadcast([P, NQ, NCMP])

            def compressed_max(g, hh):
                H = g * 4 + hh
                dve.wait_ge(cs_done, H + 1)
                dve.wait_ge(ctr_done, H + 1)
                V.tensor_tensor(scc[:, :, :], B[5][:, 0:NQ * (NCMP + 1)].rearrange("p (i n) -> p i n", i=NQ)[:, :, 0:NCMP],
                                cmpbias[:, :, :], ALU.add).then_inc(ct_step, 1)
                dve.wait_ge(ct_step, H * 2 + 1)
                V.reduce_max(cmax[:, :], scc[:, :, :], mybir.AxisListType.X).then_inc(ct_step, 1)
                dve.wait_ge(ct_step, H * 2 + 2)
                V.tensor_tensor(scc[:, :, :], scc[:, :, :], wide(cmax[:, :]), ALU.subtract).then_inc(ct_done, 1)

            def compressed_normalise(g, hh):
                H = g * 4 + hh
                dve.wait_ge(ce_done, H + 1)
                V.reduce_sum(cden[:, :], scc[:, :, :], mybir.AxisListType.X).then_inc(cn_step, 1)
                dve.wait_ge(cn_step, H * 4 + 1)
                V.reciprocal(cden[:, :], cden[:, :]).then_inc(cn_step, 1)
                dve.wait_ge(cn_step, H * 4 + 2)
                V.tensor_tensor(cden[:, :], cden[:, :], gst[:, :, 0, hh], ALU.mult).then_inc(cn_step, 1)
                dve.wait_ge(cn_step, H * 4 + 3)
                V.tensor_tensor(scc[:, :, :], scc[:, :, :], wide(cden[:, :]), ALU.mult).then_inc(cn_step, 1)
                dve.wait_ge(cn_step, H * 4 + 4)
                V.tensor_tensor(scc[:, :, :], scc[:, :, :], cmpseen[:, :, :], ALU.mult).then_inc(cp_done, 1)

            with dve.Fori(0, NKV) as g:
                dve.wait_ge(hi2_done, g * LOW_PARTS + 1)
                V.tensor_tensor(kcl[:, :], kcall[:, bass.ds(g, 1), :].rearrange("p a t -> p (a t)"),
                                kch[:, :].bitcast(F32), ALU.subtract).then_inc(lo2_done, 1)
                for n in range(2):
                    dve.wait_ge(hi2_done, g * LOW_PARTS + (n + 2))
                    V.tensor_tensor(kl2[:, n, :], kdup[:, n, bass.ds(g, 1), :].rearrange("p a t -> p (a t)"),
                                    kh2[:, n, :].bitcast(F32), ALU.subtract).then_inc(lo2_done, 1)

                def low_queries(hd):
                    a = hd % 2
                    r, o = slice(HD * a, HD * (a + 1)), slice(HD * (1 - a), HD * (2 - a))
                    dve.wait_ge(hi2_done, g * LOW_PARTS + (hd + 4))
                    V.tensor_tensor(qs2[o, hd, :], qall[r, bass.ds(g * 2 + hd // 2, 1), :].rearrange("p a t -> p (a t)"),
                                    qs2[r, hd, :].bitcast(F32), ALU.subtract).then_inc(lo2_done, 1)

                low_queries(0)
                dve.wait_ge(pv2_done, g * 16 + 2)
                V.tensor_copy(gst[:, :, :, :], gates[:, :, :].rearrange("p i (n h) -> p i n h", n=3)
                              [:, :, :, bass.ds(g * 4, 4)]).then_inc(staged, 1)
                V.tensor_copy(vcst[0:NCMP, :], vcall[0:NCMP, bass.ds(g, 1), :].rearrange("p a t -> p (a t)"))\
                    .then_inc(staged, 1)
                for n in range(2):
                    V.tensor_copy(vst[:, n, :, :], vall[:, n, :, bass.ds(g * HD, HD)]).then_inc(staged, 1)
                dve.wait_ge(staged, (g + 1) * STAGED)

                def normalise2(s):
                    i, par, hh = TILES2[s % 4], s % 2, s // 4
                    n = P * (i + 1)
                    G = g * 16 + s
                    dve.wait_ge(exp2_done, G * 2 + 2)
                    V.reciprocal(srec2[:, par, :], sden2[:, par, :]).then_inc(rec2_done, 1)
                    dve.wait_ge(rec2_done, G + 1)
                    V.tensor_tensor(coef2[:, par, :], srec2[:, par, :], gst[:, i, 1:3, hh], ALU.mult)\
                        .then_inc(coef2_done, 1)
                    dve.wait_ge(coef2_done, G + 1)
                    for c in range(2):
                        V.tensor_scalar(sc2[:, s % 4, c, 0:n], sc2[:, s % 4, c, 0:n], coef2[:, par, c:c + 1], None,
                                        ALU.mult).then_inc(p2_done, 1)

                def output2(t2, done):
                    dve.wait_ge(pv2_done, done)
                    V.tensor_scalar(oall[:, bass.ds(g * 2 + t2, 1), :].rearrange("p a t -> p (a t)"), B[7][:, :],
                                    1.0, None, ALU.mult).then_inc(o2_done, 1)

                for s in range(16):
                    i, par = TILES2[s % 4], s % 2
                    n = P * (i + 1)
                    off = 384 - P * i
                    G = g * 16 + s
                    dve.wait_ge(s2_done, G + 1)
                    dve.wait_ge(tr2_done, G + 1)
                    dve.nop().then_inc(turn2, 1)
                    for c in range(2):
                        V.tensor_tensor_reduce(sc2[:, s % 4, c, 0:n], B[1 + 2 * c + par][:, 0:n], tri[:, off:off + n],
                                               1.0, -3.0e38, ALU.add, ALU.max, smax2[:, par, c:c + 1])\
                            .then_inc(t2_done, 1)
                    dve.wait_ge(t2_done, G * 2 + 6)
                    V.tensor_scalar(sneg2[:, par, :], smax2[:, par, :], -SCALE, None, ALU.mult).then_inc(neg2_done, 1)
                    if s == 1:
                        compressed_normalise(g, 0)
                    if 1 <= s <= 3:
                        low_queries(s)
                    if s >= 1:
                        normalise2(s - 1)
                    if s % 4 == 0:
                        compressed_max(g, s // 4)
                    if s % 4 == 1 and s > 4:
                        compressed_normalise(g, s // 4)
                    if s == 8 + LAG2:
                        output2(0, g * 16 + 10)
                normalise2(15)
                output2(1, g * 16 + 18)
            inverse_rms2(2, B[5], 512)
            normed(2, oall, 4)
            uo = U_BLOCK2 + U_PROJ2
            updates(1.0, lambda m: (unit_used, uo + m + 3), 7, lambda m: gains2[:, 2, m:m + 1], 1)
            norm(8, 7, B[7])
            ffn_unit[0] = uo + U_OUT
            feed_forward(4)
            updates(1.0, down_done(4, uo + U_OUT))
            dve.wait_ge(sq_used, 10 * 8 + 4)
            inverse_rms(9, B[0])
            for m in range(KT):
                V.scalar_tensor_tensor(x[:, m, :], x[:, m, :], gains2[:, 3, m:m + 1], rstd[:, :], ALU.mult, ALU.mult)\
                    .then_inc(fin_done, 1)


def lay_out(inputs):
    a = {k: np.asarray(v) for k, v in inputs.items()}

    def cols(w, c):
        return w[:, c:c + P].reshape(8, P, P).transpose(1, 0, 2)

    units = []

    def ffn(g, u, dn):
        for f in range(FT):
            units.append(cols(g, f * P))
            units.append(cols(u, f * P))
        for f in range(FT):
            units.append(dn[f * P:(f + 1) * P].reshape(P, 8, P))

    turned = np.r_[HEAD_ORDER, HD + HEAD_ORDER]

    for l in range(DEPTH):
        ffn(a["ffn1_w_gate"][l], a["ffn1_w_up"][l], a["ffn1_w_down"][l])
        w = a["w_in"][l]
        pooled = [cols(w, 0), cols(w, P)]
        for j in range(PAIRS):
            q, k, v = [cols(w, POOL_W + n * PAIRS * P + j * P) for n in range(3)]
            units += [q[..., turned], k[..., turned], v] + (pooled if j == 0 else [])
        units += [cols(a["w_out"][l], m * P) for m in range(KT)]
        ffn(a["ffn2_w_gate"][l], a["ffn2_w_up"][l], a["ffn2_w_down"][l])
    w = a["w_in_2"][0]
    units += [cols(w, c * P) for c in ORDER2]
    units += [cols(a["w_o_2"][0], m * P) for m in range(KT)]
    ffn(a["w_gate_2"][0], a["w_up_2"][0], a["w_down_2"][0])
    assert len(units) == U_ALL
    stream = np.empty((U_ALL // 2, P, 2, 8 * P), np.float32)
    for u, unit in enumerate(units):
        stream[u // 2, :, u % 2] = unit.reshape(P, 8 * P)

    def tiles(v):
        v = v.reshape(*v.shape[:-1], -1, P)
        return np.moveaxis(v, -1, 0)

    out = {
        "x": a["x"][0].T.reshape(KT, P, T).transpose(1, 0, 2),
        "positions": a["positions"].reshape(1, T),
        "stream": stream,
        "gains": tiles(np.stack([a["ffn1_norm"], a["mix_norm"], a["ffn2_norm"]], 1)),
        "gains2": tiles(np.stack([a["final_norm"], a["norm_mix_w_2"][0], a["norm_ffn_w_2"][0], a["final_norm_w_2"]])),
        "poolw": a["pool_w"].reshape(DEPTH, 2, P, HD).transpose(2, 0, 1, 3),
        "poolscale": tiles(a["pool_scale"]),
        "ws_2": a["gmlp_ws_2"][0].transpose(2, 0, 1),
        "bs_2": a["gmlp_bs_2"][0].reshape(4, 2, P).transpose(1, 0, 2),
        "wg_2": w[:, U_PROJ2 * P:].reshape(8, P, NGATE).transpose(1, 0, 2),
        "gate_b_2": a["gate_b_2"].reshape(NGATE, 1),
        "vec_2": tiles(np.concatenate([a["gmlp_norm_w_2"], a["out_norm_a_w_2"], a["out_norm_b_w_2"]])),
        "pos_2": np.stack([a["cmp_pos_k_2"][0], a["cmp_pos_v_2"][0]]).reshape(2, SLABS, P).transpose(2, 0, 1),
        "w1k_2": a["cmp_k_w1_2"][0].reshape(SLABS, P, CH).transpose(1, 0, 2),
        "w1v_2": a["cmp_v_w1_2"][0].reshape(SLABS, P, CH).transpose(1, 0, 2),
        "w2k_2": a["cmp_k_w2_2"][0].reshape(2, P, HD).transpose(1, 0, 2),
        "w2v_2": a["cmp_v_w2_2"][0].reshape(2, P, HD).transpose(1, 0, 2),
    }
    out.update(shape_constants())
    return {k: np.ascontiguousarray(v) for k, v in out.items()}


def kernel(**inputs):
    import concourse.bacc as bacc
    from concourse.bass_utils import run_bass_kernel_spmd as run

    nc = bacc.Bacc("TRN2", target_bir_lowering=False, num_devices=1)
    arrays = {"in_" + k: v for k, v in lay_out(inputs).items()}
    d = {k[3:]: nc.dram_tensor(k, v.shape, mybir.dt.from_np(v.dtype), kind="ExternalInput").ap()
         for k, v in arrays.items()}
    d["out"] = nc.dram_tensor("out_dram", (P, KT, T), F32, kind="ExternalOutput").ap()
    build(nc, d)
    r = run(nc, [arrays], core_ids=[0])
    y = r.results[0]["out_dram"]
    return np.ascontiguousarray(y.transpose(1, 0, 2).reshape(D, T).T).reshape(1, T, D)
```
